# Optimizing a Trainium2 kernel written in Bass

```python
import math
import jax, jax.numpy as jnp
from jax import lax
import numpy as np

D_MODEL = 1024
BATCH = 1
SEQ = 256
DEPTH = 2

HEAD_DIM = 64
N_HEAD_SLOTS = D_MODEL // HEAD_DIM
MIX_WIDTH = N_HEAD_SLOTS * HEAD_DIM
HEADS_PER_MIXER = N_HEAD_SLOTS // 2
KV_HEADS = 2
GROUP = HEADS_PER_MIXER // KV_HEADS
HQ = HEADS_PER_MIXER * HEAD_DIM
KVW = KV_HEADS * HEAD_DIM
Q_BLOCK = 128
NSA_CMP_LEN = 32
NSA_CMP_STRIDE = 16
NSA_SEL_LEN = 64
NSA_SEL_TOP = 8
NSA_WINDOW = 512
NSA_FORCE = 1e4
SWA_WINDOW = 128
MOBA_BLOCK = 256
MOBA_TOP = 3
MOBA_Q_CHUNK = 32
REL_BUCKETS = 32
REL_MAX_DIST = 128
D_FF = ((8 * D_MODEL // 3 + 255) // 256) * 256
RMS_EPS = 1e-6
NEG = -1e30
AB_WIDTH = HQ + 6 * KVW + 3 * HEADS_PER_MIXER + HQ + 2 * KVW
CD_WIDTH = HQ + 2 * KVW + 3 * HQ
N_EVEN = (DEPTH + 1) // 2
N_ODD = DEPTH // 2


def rms_norm(x, w):
    xf = x.astype(jnp.float32)
    y = xf * lax.rsqrt(jnp.mean(xf * xf, axis=-1, keepdims=True) + RMS_EPS)
    return (y * w.astype(jnp.float32)).astype(x.dtype)

def rel_bucket(dist):
    n = jnp.maximum(dist, 0)
    max_exact = REL_BUCKETS // 2
    nf = jnp.maximum(n, 1).astype(jnp.float32)
    large = max_exact + (jnp.log(nf / max_exact) / math.log(REL_MAX_DIST / max_exact)
                         * (REL_BUCKETS - max_exact)).astype(jnp.int32)
    large = jnp.minimum(large, REL_BUCKETS - 1)
    return jnp.where(n < max_exact, n, large)

def masked_softmax(s, valid):
    s = jnp.where(valid, s.astype(jnp.float32), NEG)
    p = jax.nn.softmax(s, axis=-1)
    return jnp.where(valid, p, 0.0)

def nsa_attention(q, k_cmp, v_cmp, k_sel, v_sel, k_win, v_win, gates, cmp_wk, cmp_wv, cmp_pe, rel_tab):
    B, S, H, dh = q.shape
    G, R = KV_HEADS, GROUP
    dt = q.dtype
    scale = HEAD_DIM ** -0.5
    n_cmp = (S - NSA_CMP_LEN) // NSA_CMP_STRIDE + 1
    cmp_start = jnp.arange(n_cmp) * NSA_CMP_STRIDE
    gidx = cmp_start[:, None] + jnp.arange(NSA_CMP_LEN)[None, :]
    kc = jnp.einsum('bnlgd,lde->bnge', k_cmp[:, gidx] + cmp_pe[:, None, :], cmp_wk)
    vc = jnp.einsum('bnlgd,lde->bnge', v_cmp[:, gidx] + cmp_pe[:, None, :], cmp_wv)
    cmp_end = cmp_start + NSA_CMP_LEN - 1
    n_sel = S // NSA_SEL_LEN
    sel_start = jnp.arange(n_sel) * NSA_SEL_LEN
    overlap = jnp.maximum(jnp.minimum(cmp_end[:, None] + 1, sel_start[None, :] + NSA_SEL_LEN)
                          - jnp.maximum(cmp_start[:, None], sel_start[None, :]), 0)
    overlap_w = overlap.astype(jnp.float32) / NSA_CMP_LEN
    top = min(NSA_SEL_TOP, n_sel)
    ksb = k_sel.reshape(B, n_sel, NSA_SEL_LEN, G, dh).transpose(0, 3, 1, 2, 4)
    vsb = v_sel.reshape(B, n_sel, NSA_SEL_LEN, G, dh).transpose(0, 3, 1, 2, 4)
    kw = jnp.pad(k_win, ((0, 0), (NSA_WINDOW, 0), (0, 0), (0, 0)))
    vw = jnp.pad(v_win, ((0, 0), (NSA_WINDOW, 0), (0, 0), (0, 0)))
    bi = jnp.arange(B)[:, None, None, None]
    gi = jnp.arange(G)[None, :, None, None]
    sb = jnp.arange(n_sel)

    def block(n):
        t0 = n * Q_BLOCK
        tq = t0 + jnp.arange(Q_BLOCK)
        qb = lax.dynamic_slice_in_dim(q, t0, Q_BLOCK, axis=1).reshape(B, Q_BLOCK, G, R, dh)
        gb = lax.dynamic_slice_in_dim(gates, t0, Q_BLOCK, axis=1).reshape(B, Q_BLOCK, G, R, 1, 3)
        dist = tq[:, None] - cmp_end[None, :]
        s = jnp.einsum('bqgrd,bngd->bgrqn', qb, kc) * scale
        s = s + rel_tab[rel_bucket(dist)].transpose(2, 3, 0, 1)
        p_cmp = masked_softmax(s, dist >= 0)
        o_cmp = jnp.einsum('bgrqn,bngd->bqgrd', p_cmp.astype(dt), vc)
        imp = jnp.einsum('bgrqn,ns->bgqs', p_cmp, overlap_w)
        own = tq // NSA_SEL_LEN
        forced = (sb[None, :] == 0) | (sb[None, :] == own[:, None]) | (sb[None, :] == own[:, None] - 1)
        causal_blk = sb[None, :] <= own[:, None]
        imp = jnp.where(causal_blk, imp + jnp.where(forced, NSA_FORCE, 0.0), NEG)
        _, sel = lax.top_k(imp, top)
        ks = ksb[bi, gi, sel].reshape(B, G, Q_BLOCK, top * NSA_SEL_LEN, dh)
        vs = vsb[bi, gi, sel].reshape(B, G, Q_BLOCK, top * NSA_SEL_LEN, dh)
        pos = (sel[..., None] * NSA_SEL_LEN + jnp.arange(NSA_SEL_LEN)).reshape(B, G, Q_BLOCK, top * NSA_SEL_LEN)
        dist = tq[None, None, :, None] - pos
        s = jnp.einsum('bqgrd,bgqkd->bgrqk', qb, ks) * scale
        s = s + rel_tab[rel_bucket(dist), gi].transpose(0, 1, 4, 2, 3)
        p = masked_softmax(s, (dist >= 0)[:, :, None])
        o_sel = jnp.einsum('bgrqk,bgqkd->bqgrd', p.astype(dt), vs)
        kwb = lax.dynamic_slice_in_dim(kw, t0, NSA_WINDOW + Q_BLOCK, axis=1)
        vwb = lax.dynamic_slice_in_dim(vw, t0, NSA_WINDOW + Q_BLOCK, axis=1)
        kpos = t0 - NSA_WINDOW + jnp.arange(NSA_WINDOW + Q_BLOCK)
        dist = tq[:, None] - kpos[None, :]
        valid = (dist >= 0) & (dist < NSA_WINDOW) & (kpos[None, :] >= 0)
        s = jnp.einsum('bqgrd,bkgd->bgrqk', qb, kwb) * scale
        s = s + rel_tab[rel_bucket(dist)].transpose(2, 3, 0, 1)
        p = masked_softmax(s, valid)
        o_win = jnp.einsum('bgrqk,bkgd->bqgrd', p.astype(dt), vwb)
        o = jnp.stack([o_cmp, o_sel, o_win], axis=-1)
        return jnp.sum(o * gb, axis=-1).reshape(B, Q_BLOCK, H * dh)

    out = lax.map(block, jnp.arange(S // Q_BLOCK))
    return out.transpose(1, 0, 2, 3).reshape(B, S, H * dh)

def swa_sink_attention(q, k, v, sinks, rel_tab):
    B, S, H, dh = q.shape
    G, R = KV_HEADS, GROUP
    dt = q.dtype
    scale = HEAD_DIM ** -0.5
    kp = jnp.pad(k, ((0, 0), (SWA_WINDOW, 0), (0, 0), (0, 0)))
    vp = jnp.pad(v, ((0, 0), (SWA_WINDOW, 0), (0, 0), (0, 0)))
    sink = jnp.broadcast_to(sinks.astype(jnp.float32).reshape(G, R)[None, :, :, None, None],
                            (B, G, R, Q_BLOCK, 1))

    def block(n):
        t0 = n * Q_BLOCK
        tq = t0 + jnp.arange(Q_BLOCK)
        qb = lax.dynamic_slice_in_dim(q, t0, Q_BLOCK, axis=1).reshape(B, Q_BLOCK, G, R, dh)
        kb = lax.dynamic_slice_in_dim(kp, t0, SWA_WINDOW + Q_BLOCK, axis=1)
        vb = lax.dynamic_slice_in_dim(vp, t0, SWA_WINDOW + Q_BLOCK, axis=1)
        kpos = t0 - SWA_WINDOW + jnp.arange(SWA_WINDOW + Q_BLOCK)
        dist = tq[:, None] - kpos[None, :]
        valid = (dist >= 0) & (dist < SWA_WINDOW) & (kpos[None, :] >= 0)
        s = jnp.einsum('bqgrd,bkgd->bgrqk', qb, kb) * scale
        s = s + rel_tab[rel_bucket(dist)].transpose(2, 3, 0, 1)
        s = jnp.where(valid, s.astype(jnp.float32), NEG)
        p = jax.nn.softmax(jnp.concatenate([s, sink], axis=-1), axis=-1)[..., :-1]
        o = jnp.einsum('bgrqk,bkgd->bqgrd', p.astype(dt), vb)
        return o.reshape(B, Q_BLOCK, H * dh)

    out = lax.map(block, jnp.arange(S // Q_BLOCK))
    return out.transpose(1, 0, 2, 3).reshape(B, S, H * dh)

def moba_attention(q, k, v, rel_tab_h):
    B, S, H, dh = q.shape
    G, R = KV_HEADS, GROUP
    L = MOBA_BLOCK
    dt = q.dtype
    scale = HEAD_DIM ** -0.5
    nb = max(-(-S // L), 2)
    pad = nb * L - S
    kp = jnp.pad(k, ((0, 0), (0, pad), (0, 0), (0, 0)))
    vp = jnp.pad(v, ((0, 0), (0, pad), (0, 0), (0, 0)))
    head_grp = jnp.arange(H) // R
    kb = kp.reshape(B, nb, L, G, dh)
    k_mean = jnp.mean(kb.astype(jnp.float32), axis=2).astype(dt)[:, :, head_grp]
    kbh = kb[:, :, :, head_grp].transpose(0, 3, 1, 2, 4)
    vbh = vp.reshape(B, nb, L, G, dh)[:, :, :, head_grp].transpose(0, 3, 1, 2, 4)
    top = min(MOBA_TOP, nb - 1)
    bi = jnp.arange(B)[:, None, None, None]
    hi = jnp.arange(H)[None, None, :, None]
    Qc = MOBA_Q_CHUNK

    def chunk(n):
        t0 = n * Qc
        tq = t0 + jnp.arange(Qc)
        qc = lax.dynamic_slice_in_dim(q, t0, Qc, axis=1)
        own = t0 // L
        gs = jnp.einsum('bqhd,bnhd->bqhn', qc, k_mean).astype(jnp.float32)
        gs = jnp.where(jnp.arange(nb) < own, gs, NEG)
        _, sel = lax.top_k(gs, top)
        sel_ok = sel < own
        ks = kbh[bi, hi, sel]
        vs = vbh[bi, hi, sel]
        pos = sel[..., None] * L + jnp.arange(L)
        s_past = jnp.einsum('bqhd,bqhnld->bqhnl', qc, ks) * scale
        s_past = s_past + rel_tab_h[rel_bucket(tq[None, :, None, None, None] - pos), hi[..., None]]
        k_own = lax.dynamic_slice_in_dim(kp, own * L, L, axis=1)[:, :, head_grp]
        v_own = lax.dynamic_slice_in_dim(vp, own * L, L, axis=1)[:, :, head_grp]
        dist_own = tq[:, None] - (own * L + jnp.arange(L))[None, :]
        s_own = jnp.einsum('bqhd,blhd->bqhl', qc, k_own) * scale
        s_own = s_own + rel_tab_h[rel_bucket(dist_own)].transpose(0, 2, 1)
        s = jnp.concatenate([s_past.reshape(B, Qc, H, top * L), s_own], axis=-1)
        valid = jnp.concatenate([
            jnp.broadcast_to(sel_ok[..., None], (B, Qc, H, top, L)).reshape(B, Qc, H, top * L),
            jnp.broadcast_to((dist_own >= 0)[:, None, :], (B, Qc, H, L))], axis=-1)
        p = masked_softmax(s, valid).astype(dt)
        o = (jnp.einsum('bqhk,bqhkd->bqhd', p[..., :top * L], vs.reshape(B, Qc, H, top * L, dh))
             + jnp.einsum('bqhl,blhd->bqhd', p[..., top * L:], v_own))
        return o.reshape(B, Qc, H * dh)

    out = lax.map(chunk, jnp.arange(S // Qc))
    return out.transpose(1, 0, 2, 3).reshape(B, S, H * dh)

def stick_breaking_attention(q, k, v):
    B, S, H, dh = q.shape
    dt = q.dtype
    scale = HEAD_DIM ** -0.5
    kpos = jnp.arange(S)

    def block(n):
        t0 = n * Q_BLOCK
        tq = t0 + jnp.arange(Q_BLOCK)
        qb = lax.dynamic_slice_in_dim(q, t0, Q_BLOCK, axis=1)
        z = jnp.einsum('bqhd,bkhd->bhqk', qb, k).astype(jnp.float32) * scale
        strict = kpos[None, :] < tq[:, None]
        log_1m = jnp.where(strict, jax.nn.log_sigmoid(-z), 0.0)
        after = lax.cumsum(log_1m, axis=3, reverse=True) - log_1m
        w = jnp.where(strict, jnp.exp(jax.nn.log_sigmoid(z) + after), 0.0)
        o = jnp.einsum('bhqk,bkhd->bqhd', w.astype(dt), v)
        return o.reshape(B, Q_BLOCK, H * dh)

    out = lax.map(block, jnp.arange(S // Q_BLOCK))
    return out.transpose(1, 0, 2, 3).reshape(B, S, H * dh)

def mixer_ab(h, w_in, w_out, cmp_wk, cmp_wv, cmp_pe, sinks, rel_table):
    B, S, _ = h.shape
    H, G, dh = HEADS_PER_MIXER, KV_HEADS, HEAD_DIM
    proj = h @ w_in
    sizes = [HQ, KVW, KVW, KVW, KVW, KVW, KVW, 3 * H, HQ, KVW, KVW]
    qa, kca, vca, ksa, vsa, kwa, vwa, ga, qb, kb, vb = jnp.split(proj, np.cumsum(sizes)[:-1].tolist(), axis=-1)
    kv = lambda t: t.reshape(B, S, G, dh)
    gates = jax.nn.sigmoid(ga.astype(jnp.float32)).astype(h.dtype).reshape(B, S, H, 3)
    tab_a = rel_table[:, :H].reshape(REL_BUCKETS, G, GROUP)
    tab_b = rel_table[:, H:2 * H].reshape(REL_BUCKETS, G, GROUP)
    o_a = nsa_attention(qa.reshape(B, S, H, dh), kv(kca), kv(vca), kv(ksa), kv(vsa), kv(kwa), kv(vwa),
                        gates, cmp_wk, cmp_wv, cmp_pe, tab_a)
    o_b = swa_sink_attention(qb.reshape(B, S, H, dh), kv(kb), kv(vb), sinks, tab_b)
    return jnp.concatenate([o_a, o_b], axis=-1) @ w_out

def mixer_cd(h, w_in, w_out, rel_table):
    B, S, _ = h.shape
    H, G, dh = HEADS_PER_MIXER, KV_HEADS, HEAD_DIM
    proj = h @ w_in
    sizes = [HQ, KVW, KVW, HQ, HQ, HQ]
    qc, kc, vc, qd, kd, vd = jnp.split(proj, np.cumsum(sizes)[:-1].tolist(), axis=-1)
    o_c = moba_attention(qc.reshape(B, S, H, dh), kc.reshape(B, S, G, dh), vc.reshape(B, S, G, dh),
                         rel_table[:, :H])
    o_d = stick_breaking_attention(qd.reshape(B, S, H, dh), kd.reshape(B, S, H, dh), vd.reshape(B, S, H, dh))
    return jnp.concatenate([o_c, o_d], axis=-1) @ w_out

def swiglu(h, w_in, w_out):
    gate, up = jnp.split(h @ w_in, 2, axis=-1)
    return (jax.nn.silu(gate) * up) @ w_out

def first_inputs(seed: int = 0) -> dict:
    key = jax.random.key(seed)
    ks = jax.random.split(key, 16)
    f32 = jnp.float32

    def nrm(k, shape, s):
        return jax.random.normal(k, shape, f32) * s

    return {
        "x": nrm(ks[0], (BATCH, SEQ, D_MODEL), 1.0),
        "c": nrm(ks[1], (BATCH, D_MODEL), 1.0),
        "rel_table": nrm(ks[2], (REL_BUCKETS, N_HEAD_SLOTS), 0.5),
        "mod_w": nrm(ks[3], (DEPTH, 2, D_MODEL, 3 * D_MODEL), 0.5 * D_MODEL ** -0.5),
        "mod_b": nrm(ks[4], (DEPTH, 2, 3 * D_MODEL), 0.02),
        "norm_w": 1.0 + nrm(ks[5], (DEPTH, 2, 2, D_MODEL), 0.02),
        "w_in_ab": nrm(ks[6], (N_EVEN, D_MODEL, AB_WIDTH), D_MODEL ** -0.5),
        "w_out_ab": nrm(ks[7], (N_EVEN, MIX_WIDTH, D_MODEL), MIX_WIDTH ** -0.5),
        "nsa_cmp_wk": nrm(ks[8], (N_EVEN, NSA_CMP_LEN, HEAD_DIM, HEAD_DIM), (NSA_CMP_LEN * HEAD_DIM) ** -0.5),
        "nsa_cmp_wv": nrm(ks[9], (N_EVEN, NSA_CMP_LEN, HEAD_DIM, HEAD_DIM), (NSA_CMP_LEN * HEAD_DIM) ** -0.5),
        "nsa_cmp_pe": nrm(ks[10], (N_EVEN, NSA_CMP_LEN, HEAD_DIM), 0.1),
        "swa_sinks": nrm(ks[11], (N_EVEN, HEADS_PER_MIXER), 0.5),
        "w_in_cd": nrm(ks[12], (N_ODD, D_MODEL, CD_WIDTH), D_MODEL ** -0.5),
        "w_out_cd": nrm(ks[13], (N_ODD, MIX_WIDTH, D_MODEL), MIX_WIDTH ** -0.5),
        "ffn_w_in": nrm(ks[14], (DEPTH, D_MODEL, 2 * D_FF), D_MODEL ** -0.5),
        "ffn_w_out": nrm(ks[15], (DEPTH, D_FF, D_MODEL), D_FF ** -0.5),
    }

def first_block(x, c, rel_table, mod_w, mod_b, norm_w, w_in_ab, w_out_ab, nsa_cmp_wk, nsa_cmp_wv,
              nsa_cmp_pe, swa_sinks, w_in_cd, w_out_cd, ffn_w_in, ffn_w_out):
    for layer in range(DEPTH):
        shift, scale, gate = jnp.split((c @ mod_w[layer, 0] + mod_b[layer, 0])[:, None, :], 3, axis=-1)
        h = rms_norm(x, norm_w[layer, 0, 0]) * (1.0 + scale) + shift
        i = layer // 2
        if layer % 2 == 0:
            y = mixer_ab(h, w_in_ab[i], w_out_ab[i], nsa_cmp_wk[i], nsa_cmp_wv[i], nsa_cmp_pe[i],
                         swa_sinks[i], rel_table)
        else:
            y = mixer_cd(h, w_in_cd[i], w_out_cd[i], rel_table)
        x = x + gate * rms_norm(y, norm_w[layer, 0, 1])
        shift, scale, gate = jnp.split((c @ mod_w[layer, 1] + mod_b[layer, 1])[:, None, :], 3, axis=-1)
        h = rms_norm(x, norm_w[layer, 1, 0]) * (1.0 + scale) + shift
        y = swiglu(h, ffn_w_in[layer], ffn_w_out[layer])
        x = x + gate * rms_norm(y, norm_w[layer, 1, 1])
    return x


ATTN_HEADS = 8
ATTN_WIDTH = ATTN_HEADS * HEAD_DIM
GLA_HEADS = 4
GLA_DK = 64
GLA_DV = 128
GLA_K_WIDTH = GLA_HEADS * GLA_DK
GLA_V_WIDTH = GLA_HEADS * GLA_DV
GLA_GATE_RANK = 16
GLA_TAU = 16.0
GLA_CHUNK = 64
MIX_WIDTH_2 = ATTN_WIDTH + GLA_V_WIDTH
IN_WIDTH = 3 * ATTN_WIDTH + 2 * GLA_K_WIDTH + 2 * GLA_V_WIDTH + GLA_GATE_RANK
D_FF_2 = -(-8 * D_MODEL // (3 * 256)) * 256
ROPE_THETA = 500000.0
ROPE_DIM = HEAD_DIM // 4
DILATED_PATTERNS = ((128, 1), (512, 4), (2048, 16))
N_PATTERNS = len(DILATED_PATTERNS)
N_KEYS = DILATED_PATTERNS[0][0] // DILATED_PATTERNS[0][1] + 1


F32 = jnp.float32

def rmsnorm(x, g):
    xf = x.astype(F32)
    y = xf * lax.rsqrt(jnp.mean(xf * xf, axis=-1, keepdims=True) + RMS_EPS)
    return (y * g.astype(F32)).astype(x.dtype)

def rope_partial(x, pos):
    half = ROPE_DIM // 2
    inv = ROPE_THETA ** (-(jnp.arange(half, dtype=F32) * 2.0) / ROPE_DIM)
    ang = pos.astype(F32)[:, None] * inv[None, :]
    cos = jnp.cos(ang)[None, :, None, :]
    sin = jnp.sin(ang)[None, :, None, :]
    xr = x[..., :ROPE_DIM].astype(F32)
    x1, x2 = xr[..., :half], xr[..., half:]
    rot = jnp.concatenate([x1 * cos - x2 * sin, x2 * cos + x1 * sin], axis=-1).astype(x.dtype)
    return jnp.concatenate([rot, x[..., ROPE_DIM:]], axis=-1)

def dilated_attention(q, k, v):
    B, S, H, hd = q.shape
    nblk = S // Q_BLOCK
    dists = jnp.concatenate([d * jnp.arange(w // d + 1) for (w, d) in DILATED_PATTERNS])
    q_blocks = q.reshape(B, nblk, Q_BLOCK, H, hd).transpose(1, 0, 2, 3, 4)
    starts = jnp.arange(nblk) * Q_BLOCK
    scale = hd ** -0.5

    def block(args):
        q_blk, start = args
        pos = start + jnp.arange(Q_BLOCK)
        idx = pos[:, None] - dists[None, :]
        valid = idx >= 0
        idx_c = jnp.maximum(idx, 0)
        kg = jnp.take(k, idx_c, axis=1).astype(F32)
        vg = jnp.take(v, idx_c, axis=1).astype(F32)
        s = jnp.einsum('bqhd,bqnhd->bhqn', q_blk.astype(F32), kg) * scale
        s = jnp.where(valid[None, None], s, -jnp.inf)
        s = s.reshape(B, H, Q_BLOCK, N_PATTERNS, N_KEYS)
        lse = jax.nn.logsumexp(s, axis=-1, keepdims=True)
        p = jnp.exp(s - lse)
        o_pat = jnp.einsum('bhqpn,bqpnhd->bhqpd', p,
                           vg.reshape(B, Q_BLOCK, N_PATTERNS, N_KEYS, H, hd))
        w = jax.nn.softmax(lse, axis=-2)
        o = jnp.sum(w * o_pat, axis=-2)
        return o.transpose(0, 2, 1, 3).astype(q.dtype)

    out = lax.map(block, (q_blocks, starts))
    return out.transpose(1, 0, 2, 3, 4).reshape(B, S, H, hd)

def gla_chunked(q, k, v, g):
    B, S, H, dk = q.shape
    dv = v.shape[-1]
    C = GLA_CHUNK
    nc = S // C

    def chunks(t):
        return t.astype(F32).reshape(B, nc, C, H, t.shape[-1]).transpose(1, 0, 3, 2, 4)

    causal = jnp.tril(jnp.ones((C, C), dtype=bool))

    def step(state, inp):
        qc, kc, vc, gc = inp
        b = jnp.cumsum(gc, axis=-2)
        o_inter = jnp.einsum('bhtk,bhkv->bhtv', qc * jnp.exp(b), state)
        diff = b[:, :, :, None, :] - b[:, :, None, :, :]
        decay = jnp.exp(jnp.where(causal[None, None, :, :, None], diff, -jnp.inf))
        attn = jnp.einsum('bhtk,bhsk,bhtsk->bhts', qc, kc, decay)
        o_intra = jnp.einsum('bhts,bhsv->bhtv', attn, vc)
        b_last = b[:, :, -1:, :]
        state = jnp.exp(b_last[:, :, 0, :])[..., None] * state + \
            jnp.einsum('bhsk,bhsv->bhkv', kc * jnp.exp(b_last - b), vc)
        return state, o_intra + o_inter

    s0 = jnp.zeros((B, H, dk, dv), F32)
    _, o = lax.scan(step, s0, (chunks(q) * (dk ** -0.5), chunks(k), chunks(v), chunks(g)))
    return o.transpose(1, 0, 3, 2, 4).reshape(B, S, H, dv).astype(v.dtype)

def hybrid_mixer(h, w_in, gla_w_gate_up, gla_b_gate, gla_out_norm, attn_out_norm, w_out):
    B, S, _ = h.shape
    proj = h @ w_in
    cuts = [ATTN_WIDTH, 2 * ATTN_WIDTH, 3 * ATTN_WIDTH,
            3 * ATTN_WIDTH + GLA_K_WIDTH, 3 * ATTN_WIDTH + 2 * GLA_K_WIDTH,
            3 * ATTN_WIDTH + 2 * GLA_K_WIDTH + GLA_V_WIDTH,
            3 * ATTN_WIDTH + 2 * GLA_K_WIDTH + 2 * GLA_V_WIDTH]
    aq, ak, av, gq, gk, gv, gr, g_low = jnp.split(proj, cuts, axis=-1)

    pos = jnp.arange(S)
    aq = rope_partial(aq.reshape(B, S, ATTN_HEADS, HEAD_DIM), pos)
    ak = rope_partial(ak.reshape(B, S, ATTN_HEADS, HEAD_DIM), pos)
    av = av.reshape(B, S, ATTN_HEADS, HEAD_DIM)
    a_out = dilated_attention(aq, ak, av).reshape(B, S, ATTN_WIDTH)
    a_out = rmsnorm(a_out, attn_out_norm)

    z = g_low @ gla_w_gate_up + gla_b_gate
    log_alpha = jax.nn.log_sigmoid(z.astype(F32)) / GLA_TAU
    o = gla_chunked(gq.reshape(B, S, GLA_HEADS, GLA_DK),
                    gk.reshape(B, S, GLA_HEADS, GLA_DK),
                    gv.reshape(B, S, GLA_HEADS, GLA_DV),
                    log_alpha.reshape(B, S, GLA_HEADS, GLA_DK))
    o = rmsnorm(o, gla_out_norm.reshape(GLA_HEADS, GLA_DV)).reshape(B, S, GLA_V_WIDTH)
    g_out = o * jax.nn.silu(gr)

    mixed = jnp.concatenate([a_out, g_out], axis=-1)
    return mixed @ w_out

def swiglu_2(h, w_gate, w_up, w_down):
    return (jax.nn.silu(h @ w_gate) * (h @ w_up)) @ w_down

def second_inputs(seed: int = 0) -> dict:
    key = jax.random.key(seed)
    ks = jax.random.split(key, 16)
    L, D = DEPTH, D_MODEL

    def nrm(k, shape, fan_in):
        return jax.random.normal(k, shape, F32) * (fan_in ** -0.5)

    def gain(k, shape):
        return 1.0 + 0.05 * jax.random.normal(k, shape, F32)

    return {
        "x": jax.random.normal(ks[0], (BATCH, SEQ, D), F32),
        "mix_pre_norm": gain(ks[1], (L, D)),
        "mix_post_norm": gain(ks[2], (L, D)),
        "ffn_pre_norm": gain(ks[3], (L, D)),
        "ffn_post_norm": gain(ks[4], (L, D)),
        "w_in": nrm(ks[5], (L, D, IN_WIDTH), D),
        "gla_w_gate_up": nrm(ks[6], (L, GLA_GATE_RANK, GLA_K_WIDTH), GLA_GATE_RANK),
        "gla_b_gate": 0.1 * jax.random.normal(ks[7], (L, GLA_K_WIDTH), F32),
        "gla_out_norm": gain(ks[8], (L, GLA_V_WIDTH)),
        "attn_out_norm": gain(ks[9], (L, ATTN_WIDTH)),
        "w_out": nrm(ks[10], (L, MIX_WIDTH_2, D), MIX_WIDTH_2),
        "w_gate": nrm(ks[11], (L, D, D_FF_2), D),
        "w_up": nrm(ks[12], (L, D, D_FF_2), D),
        "w_down": nrm(ks[13], (L, D_FF_2, D), D_FF_2),
    }

def second_block(x, mix_pre_norm, mix_post_norm, ffn_pre_norm, ffn_post_norm, w_in,
              gla_w_gate_up, gla_b_gate, gla_out_norm, attn_out_norm, w_out,
              w_gate, w_up, w_down):
    h = x
    for l in range(DEPTH):
        m = hybrid_mixer(rmsnorm(h, mix_pre_norm[l]), w_in[l], gla_w_gate_up[l], gla_b_gate[l],
                         gla_out_norm[l], attn_out_norm[l], w_out[l])
        h = h + rmsnorm(m, mix_post_norm[l])
        f = swiglu_2(rmsnorm(h, ffn_pre_norm[l]), w_gate[l], w_up[l], w_down[l])
        h = h + rmsnorm(f, ffn_post_norm[l])
    return h


def setup_inputs(seed=0):
    out = dict(first_inputs(seed))
    for name, value in second_inputs(seed + 1).items():
        if name != "x":
            out[name + "_2"] = value
    return out


def reference(
    x, c, rel_table, mod_w, mod_b, norm_w, w_in_ab, w_out_ab, nsa_cmp_wk, nsa_cmp_wv,
    nsa_cmp_pe, swa_sinks, w_in_cd, w_out_cd, ffn_w_in, ffn_w_out, mix_pre_norm_2,
    mix_post_norm_2, ffn_pre_norm_2, ffn_post_norm_2, w_in_2, gla_w_gate_up_2, gla_b_gate_2,
    gla_out_norm_2, attn_out_norm_2, w_out_2, w_gate_2, w_up_2, w_down_2,
):
    x = first_block(
        x, c, rel_table, mod_w, mod_b, norm_w, w_in_ab, w_out_ab, nsa_cmp_wk, nsa_cmp_wv,
        nsa_cmp_pe, swa_sinks, w_in_cd, w_out_cd, ffn_w_in, ffn_w_out,
    )
    return second_block(
        x, mix_pre_norm_2, mix_post_norm_2, ffn_pre_norm_2, ffn_post_norm_2, w_in_2,
        gla_w_gate_up_2, gla_b_gate_2, gla_out_norm_2, attn_out_norm_2, w_out_2, w_gate_2,
        w_up_2, w_down_2,
    )


_drawn_inputs = setup_inputs


def setup_inputs(seed=0):
    import zlib

    import numpy as np

    out = dict(_drawn_inputs(seed))
    spreads = {}
    factors = {'swa_sinks': 3.789}
    for name, (base, spread) in spreads.items():
        noise = np.random.default_rng([zlib.crc32(name.encode()), seed]).standard_normal(out[name].shape)
        drawn = base * np.exp(spread * noise) if base else spread * noise
        out[name] = __import__('jax').numpy.asarray(drawn.astype(out[name].dtype))
    for name, factor in factors.items():
        out[name] = (out[name] * factor).astype(out[name].dtype)
    return out
```

```python
import math
from contextlib import ExitStack

import numpy as np
import concourse.bass as bass
from concourse import mybir

F = mybir.dt.float32
R = mybir.dt.float32r
U32 = mybir.dt.uint32
ACT = mybir.ActivationFunctionType
ALU = mybir.AluOpType
AX = mybir.AxisListType

S = 256
D = 1024
KC = 8
DFF = 2816
FC = 22
NEG = -1e30
TW = 2048
RAW = 4
SPL = 4
AHEAD = 3
BIG = 3.0e38

V_C = 0
V_MODB = 8
V_NORM = V_MODB + 96
V_NORM2 = V_NORM + 64
V_ONORM = V_NORM2 + 64
V_GB = V_ONORM + 16
V_PE = V_GB + 4
V_EPS = V_PE + 32
V_ROW = V_EPS + 1
NV = V_ROW + 1

C_ID = 0
C_TRI = 128
C_ONE = 256
C_ROT = 384
C_STRICT = 512
C_DIL = 896
C_COS = 1152
C_SIN = 1408
C_HSEL = 1664
C_REP = 1672
C_REV = 1800
NCONST = 1928

HQ, KVW = 512, 128


def split_heads(base):
    return [np.concatenate([base + 64 * c + np.arange(64), base + 64 * (4 + c) + np.arange(64)])
            for c in range(4)]


def chunks(base, n):
    return [base + 128 * c + np.arange(128) for c in range(n)]


AB = np.cumsum([0, 512, 128, 128, 128, 128, 128, 128, 24, 512, 128, 128]).tolist()
AB_T = (chunks(AB[1], 1) + chunks(AB[2], 1) + chunks(AB[3], 1) + chunks(AB[5], 1)
        + split_heads(AB[0]) + chunks(AB[9], 1) + split_heads(AB[8]))
AB_M = [np.concatenate([AB[4] + np.arange(128), AB[6] + np.arange(128)]),
        np.concatenate([AB[10] + np.arange(128), AB[7] + np.arange(24)])]
CD = np.cumsum([0, 512, 128, 128, 512, 512, 512]).tolist()
CD_T = chunks(CD[1], 1) + split_heads(CD[0]) + chunks(CD[3], 4) + chunks(CD[4], 4)
CD_M = [CD[2] + np.arange(128), CD[5] + np.arange(256), CD[5] + 256 + np.arange(256)]
HY = np.cumsum([0, 512, 512, 512, 256, 256, 512, 512, 16]).tolist()
HY_T = ([HY[7] + np.arange(16)] + chunks(HY[3], 2) + chunks(HY[4], 2) + chunks(HY[0], 4) + chunks(HY[1], 4))
HY_M = [HY[s] + 256 * i + np.arange(256) for s in (2, 5, 6) for i in range(2)]


def plan():
    out = []

    def t_tiles(name, cols):
        for i in range(0, len(cols), 2):
            out.append((name, "T", cols[i:i + 2], True))

    def m_tiles(name, cols):
        for c in cols:
            out.append((name, "M", c, True))

    def mods(layer, sub):
        for i in range(12):
            out.append((("mod", layer, sub), "T", chunks(256 * i, 2), False))

    def ffn(gate, up, down, off):
        for j in range(FC):
            out.append(((gate, up), "GU", (j, off), True))
        for m in range(KC):
            for half in range(2):
                out.append((down, "DN", (m, half), True))

    for layer in range(2):
        mods(layer, 0)
        if layer == 0:
            t_tiles(("ab",), AB_T)
            m_tiles(("ab",), AB_M)
            for name in ("wk", "wv"):
                for half in range(2):
                    out.append(((name,), "CMP", half, False))
            t_tiles(("ab_out",), chunks(0, 8))
        else:
            t_tiles(("cd",), CD_T)
            m_tiles(("cd",), CD_M)
            t_tiles(("cd_out",), chunks(0, 8))
        mods(layer, 1)
        ffn(("ffn_in", layer), ("ffn_in", layer), ("ffn_out", layer), DFF)
    for layer in range(2):
        t_tiles(("hy", layer), HY_T)
        m_tiles(("hy", layer), HY_M)
        t_tiles(("hy_out", layer), chunks(0, 8))
        ffn(("gate", layer), ("up", layer), ("down", layer), 0)
    return out


def width(tile):
    _, what, arg, _ = tile
    if what == "T":
        return KC * sum(len(c) for c in arg)
    if what == "M":
        return KC * len(arg)
    if what == "DN":
        return 11 * 128
    return TW


class Queue:

    def __init__(self, sem):
        self.sem = sem
        self.count = 0
        self.ops = []
        self.seen = {}

    def wait(self, *toks):
        for t in toks:
            if t is None:
                continue
            if isinstance(t, list):
                self.wait(*t)
                continue
            sem, val = t
            if self.seen.get(sem.name, 0) < val:
                self.seen[sem.name] = val
                self.ops.append(lambda e, sem=sem, val=val: e.wait_ge(sem, val))

    def run(self, f, *toks):
        self.wait(*toks)
        self.ops.append(f)

    def do(self, f, *toks):
        self.wait(*toks)
        self.count += 1
        self.ops.append(lambda e: f(e).then_inc(self.sem, 1))
        return (self.sem, self.count)

    def dma(self, sem, f, *toks):
        self.wait(*toks)
        self.ops.append(lambda e: f(e).then_inc(sem, 16))

    def emit(self, e):
        for f in self.ops:
            f(e)


def build(nc, wall, xin, vecs, consts, onehot, sinks, table, gup, out, scratch):
    TILES = plan()
    ctx = ExitStack()
    with ctx:
        names = [0]

        def sb(shape, dt=F, where=ctx):
            names[0] += 1
            return where.enter_context(nc.sbuf_tensor(f"t{names[0]}", shape, dt))

        def sem(name):
            return ctx.enter_context(nc.semaphore(name))

        banks = [ctx.enter_context(nc.psum_tensor(f"bank{i}", [128, 512], F)) for i in range(8)]
        free = [None] * 8

        pe, act, dve, pool, sp = (Queue(sem(f"s_{n}")) for n in ("pe", "act", "dve", "pool", "sp"))

        raw = [sb([128, TW]) for _ in range(RAW)]
        wh = [sb([128, TW], R) for _ in range(SPL)]
        wl = [sb([128, TW], R) for _ in range(SPL)]
        s_raw = [sem(f"s_raw{i}") for i in range(RAW)]
        X = sb([128, KC, S])
        HH = sb([128, KC, S], R)
        HL = sb([128, KC, S], R)
        Y = sb([128, KC, S])
        RS = sb([128, S])
        LN = sb([128, S])
        SQ = [sb([128, S]) for _ in range(2)]
        TM = [sb([128, S]) for _ in range(3)]
        VEC = sb([128, NV])
        CON = sb([128, NCONST])
        BIAS = sb([128, 16, S])
        A4 = sb([128, 8])
        MOD = sb([128, 24])
        G4 = sb([128, 8])
        MB = sb([128, 8])
        HM = sb([128, 128])

        s_in = sem("s_in")
        s_x = sem("s_x")
        s_tab = sem("s_tab")
        s_u = sem("s_u")
        s_b = sem("s_b")
        s_sk = sem("s_sk")
        s_gu = sem("s_gu")
        s_out = sem("s_out")

        ident = CON[:, C_ID:C_ID + 128]
        tri = CON[:, C_TRI:C_TRI + 128]
        ones = CON[:, C_ONE:C_ONE + 128]
        rot = CON[:, C_ROT:C_ROT + 128]
        strict = CON[:, C_STRICT:C_STRICT + 384]
        dil = CON[:, C_DIL:C_DIL + 256]
        cosT = CON[:, C_COS:C_COS + 256]
        sinT = CON[:, C_SIN:C_SIN + 256]
        rep16 = CON[0:16, C_REP:C_REP + 128]
        hsel = CON[:, C_HSEL:C_HSEL + 8]
        eps = VEC[:, V_EPS:V_EPS + 1]

        raw_free = {}
        spl_free = {}
        state = {"dma": 0, "split": 0, "use": 0}
        split_tok = {}
        split_no = {}
        k = 0
        for i, t in enumerate(TILES):
            if t[3]:
                split_no[i] = k
                k += 1

        def raw_ready(i):
            return (s_raw[i % RAW], 16 * (i // RAW + 1))

        def pump():
            while state["dma"] < len(TILES):
                i = state["dma"]
                if i >= RAW and i - RAW not in raw_free:
                    return
                n = width(TILES[i])
                toks = raw_free[i - RAW] if i >= RAW else None
                sp.dma(s_raw[i % RAW], lambda e, i=i, n=n: e.dma_start(raw[i % RAW][:, 0:n], wall[i, :, 0:n]), toks)
                state["dma"] += 1

        def splits(upto):
            while state["split"] <= min(upto, len(TILES) - 1):
                i = state["split"]
                state["split"] += 1
                if i not in split_no:
                    continue
                n = width(TILES[i])
                sl = split_no[i] % SPL
                r, h, l = raw[i % RAW], wh[sl], wl[sl]
                fr = spl_free.get(split_no[i] - SPL)
                th = act.do(lambda e, r=r, h=h, n=n: e.activation(h[:, 0:n], r[:, 0:n], ACT.Copy),
                            raw_ready(i), fr)
                tl = dve.do(lambda e, r=r, h=h, l=l, n=n: e.tensor_tensor(
                    l[:, 0:n], r[:, 0:n], h[:, 0:n].bitcast(F), ALU.subtract), raw_ready(i), th, fr)
                split_tok[i] = [th, tl]
                raw_free[i] = [tl]
                pump()

        def next_tile(kind):
            i = state["use"]
            state["use"] += 1
            assert TILES[i][1] == kind, (i, TILES[i], kind)
            j = i
            while j < len(TILES) and j < i + AHEAD and (j not in split_no or j in split_tok or True):
                if j in split_no and split_no[j] - SPL >= 0 and split_no[j] - SPL not in spl_free:
                    break
                if j > i and state["dma"] <= j:
                    break
                splits(j)
                j += 1
            return i

        def done_tile(i, tok):
            if i in split_no:
                spl_free[split_no[i]] = tok
            else:
                raw_free[i] = [tok]
            pump()

        def wt(i):
            sl = split_no[i] % SPL
            return wh[sl], wl[sl]

        def mm3(out, lh, ll, rh, rl, first, last, sig=False):
            pe.run(lambda e: e.matmul(out, lh, rh, start=first, stop=False, skip_group_check=True))
            pe.run(lambda e: e.matmul(out, lh, rl, start=False, stop=False, skip_group_check=True))
            f = lambda e: e.matmul(out, ll, rh, start=False, stop=last, skip_group_check=True)
            if last or sig:
                return pe.do(f)
            pe.run(f)

        def mm(out, l, r, start=True, stop=True, toks=(), sig=True):
            f = lambda e: e.matmul(out, l, r, start=start, stop=stop, skip_group_check=True)
            pe.wait(*toks)
            return pe.do(f) if sig else pe.run(f)

        pump()

        act.dma(s_in, lambda e: e.dma_start(VEC[:, :], vecs))
        act.dma(s_in, lambda e: e.dma_start(CON[:, :], consts))
        act.dma(s_x, lambda e: e.dma_start(X[:, :, :], xin))
        small = (s_in, 32)
        x_in = (s_x, 16)

        with ExitStack() as ph:
            TB = sb([33, 16], where=ph)
            OH = sb([33, 1024], where=ph)
            UT = sb([8, 2, 512], where=ph)
            t0 = dve.do(lambda e: e.memset(TB[:, :], NEG))
            act.dma(s_tab, lambda e: e.dma_start(TB[0:32, :], table), t0)
            act.dma(s_tab, lambda e: e.dma_start(OH[:, :], onehot))
            for j in range(2):
                mm(banks[j][0:8, 0:512], TB[:, 8 * j:8 * j + 8], OH[:, 512 * j:512 * j + 512],
                   toks=[(s_tab, 32), t0])
            tp = (pe.sem, pe.count)
            tu = [dve.do(lambda e, j=j: e.tensor_copy(UT[:, j, :], banks[j][0:8, 0:512]), tp) for j in range(2)]
            for j in range(2):
                act.dma(s_u, lambda e, j=j: e.dma_start(scratch[8 * j:8 * j + 8, :], UT[:, j, :]), tu[j])
            BR = sb([128, 16, S], where=ph)
            toep = bass.AP(tensor=scratch.tensor, offset=0, ap=[[1, 128], [512, 16], [1, 256]])
            act.dma(s_b, lambda e: e.dma_start(BR[:, :, :], toep), (s_u, 32))
            rev = CON[:, C_REV:C_REV + 128]
            bias_ready = []
            for j in range(8):
                b = j % 4
                pe.wait(tu, free[b], small, (s_b, 16))
                t = pe.do(lambda e, j=j, b=b: e.matmul(banks[b][:, :], rev, BR[:, 2 * j:2 * j + 2, :], start=True,
                                                       stop=True))
                t = dve.do(lambda e, j=j, b=b: e.tensor_copy(
                    BIAS[:, 2 * j:2 * j + 2, :].rearrange("p a b -> p (a b)"), banks[b][:, :]), t)
                free[b] = [t]
            bias_ready = [t]

        mod_tok = [None]

        def modulation(layer, sub):
            b = 7
            pe.wait(free[b], small)
            for t in range(12):
                i = next_tile("T")
                w = raw[i % RAW][:, :].rearrange("p (c k m) -> p c k m", c=2, k=KC)
                pe.wait(raw_ready(i))
                for c in range(2):
                    col = 2 * t + c
                    for kc in range(KC):
                        f = lambda e, col=col, w=w, c=c, kc=kc: e.matmul(
                            banks[b][:, col:col + 1], w[:, c, kc, :], VEC[:, V_C + kc:V_C + kc + 1],
                            start=(kc == 0), stop=(kc == KC - 1), skip_group_check=True)
                        if c == 1 and kc == KC - 1:
                            tok = pe.do(f)
                        else:
                            pe.run(f)
                done_tile(i, tok)
            o = V_MODB + 24 * (2 * layer + sub)
            n = V_NORM + 16 * (2 * layer + sub)
            t1 = dve.do(lambda e: e.tensor_tensor(MOD[:, :], banks[b][:, 0:24], VEC[:, o:o + 24], ALU.add),
                        tok, small, mod_tok[0])
            t2 = dve.do(lambda e: e.scalar_tensor_tensor(
                out=A4[:, :], in0=MOD[:, 8:16], scalar=1.0, in1=VEC[:, n:n + 8], op0=ALU.add, op1=ALU.mult), t1)
            t3 = dve.do(lambda e: e.tensor_tensor(G4[:, :], MOD[:, 16:24], VEC[:, n + 8:n + 16], ALU.mult), t1)
            free[b] = t1
            return [t2, t3]

        sq_free = [None, None]
        sqn = [0]

        def stat_start(src, tok):
            j = sqn[0] % 2
            sqn[0] += 1
            t = act.do(lambda e: e.activation(SQ[j][:, :], src, ACT.Square), tok, sq_free[j])
            return j, t

        def stat_add(c, jt):
            j, t = jt
            if c == 0:
                pe.wait(free[6])
            tok = mm(banks[6][:, 0:S], ones, SQ[j][:, :], start=(c == 0), stop=(c == KC - 1), toks=[t, small])
            sq_free[j] = tok
            return tok

        rs_free = [None]

        def rstd(tok):
            t = act.do(lambda e: e.activation(LN[:, :], banks[6][:, 0:S], ACT.Ln, scale=1.0 / D, bias=eps),
                       tok, small)
            free[6] = t
            return act.do(lambda e: e.activation(RS[:, :], LN[:, :], ACT.Exp, scale=-0.5), t, rs_free[0])

        tm_free = [None] * 3
        h_free = [None]

        def make_h(stat, a_of, shift_of, mtok):
            r = rstd(stat)
            toks = []
            for c in range(KC):
                j = c % 3
                t = dve.do(lambda e, c=c, j=j: e.scalar_tensor_tensor(
                    out=TM[j][:, :], in0=X[:, c, :], scalar=a_of(c), in1=RS[:, :], op0=ALU.mult, op1=ALU.mult),
                    r, mtok, tm_free[j])
                if shift_of is None:
                    th = act.do(lambda e, c=c, j=j: e.activation(HH[:, c, :], TM[j][:, :], ACT.Copy), t, h_free[0])
                    tl = dve.do(lambda e, c=c, j=j: e.tensor_tensor(
                        HL[:, c, :], TM[j][:, :], HH[:, c, :].bitcast(F), ALU.subtract), th)
                else:
                    th = act.do(lambda e, c=c, j=j: e.activation(
                        HH[:, c, :], TM[j][:, :], ACT.Identity, bias=shift_of(c)), t, h_free[0])
                    tl = dve.do(lambda e, c=c, j=j: e.scalar_tensor_tensor(
                        out=HL[:, c, :], in0=TM[j][:, :], scalar=shift_of(c), in1=HH[:, c, :].bitcast(F),
                        op0=ALU.add, op1=ALU.subtract), th)
                tm_free[j] = tl
                toks.append([th, tl])
            rs_free[0] = t
            return toks

        def x_stats(toks):
            for c in range(KC):
                st = stat_add(c, stat_start(X[:, c, :], toks[c]))
            return st

        def residual(stat, g_of, mtok, ytoks):
            r = rstd(stat)
            toks = []
            for c in range(KC):
                j = c % 3
                t = dve.do(lambda e, c=c, j=j: e.scalar_tensor_tensor(
                    out=TM[j][:, :], in0=Y[:, c, :], scalar=g_of(c), in1=RS[:, :], op0=ALU.mult, op1=ALU.mult),
                    r, mtok, tm_free[j], ytoks[c])
                t2 = dve.do(lambda e, c=c, j=j: e.tensor_tensor(
                    X[:, c, :], X[:, c, :], TM[j][:, :], ALU.add), t)
                tm_free[j] = t2
                toks.append(t2)
            rs_free[0] = t
            return toks

        def take_turns(handle, toks):
            t = toks[-1][-1]
            for x in toks:
                t = handle(*x[:-1], [t, toks[-1][-1]])
            return [t]

        def proj_T(cols, htoks, handle, ring):
            n = 0
            for t in range(0, len(cols), 2):
                i = next_tile("T")
                h, l = wt(i)
                b = ring[(t // 2) % len(ring)]
                off = 0
                toks = []
                for c in cols[t:t + 2]:
                    m = len(c)
                    o = banks[b][0:m, 256 * (n % 2):256 * (n % 2) + 256]
                    pe.wait(free[b], split_tok[i])
                    for kc in range(KC):
                        if n == 0:
                            pe.wait(htoks[kc])
                        q = slice(off + kc * m, off + kc * m + m)
                        tok = mm3(o, h[:, q], l[:, q], HH[:, kc, :], HL[:, kc, :], kc == 0, kc == KC - 1)
                    toks.append((n, o, tok))
                    off += KC * m
                    n += 1
                done_tile(i, tok)
                free[b] = take_turns(handle, toks)
            h_free[0] = tok

        def proj_M(cols, handle, ring):
            for n, c in enumerate(cols):
                i = next_tile("M")
                h, l = wt(i)
                m = len(c)
                b = ring[n % len(ring)]
                pe.wait(free[b], split_tok[i])
                toks = []
                for qt in range(2):
                    o = banks[b][:, 256 * qt:256 * qt + m]
                    for kc in range(KC):
                        q = slice(kc * m, kc * m + m)
                        s = slice(128 * qt, 128 * qt + 128)
                        tok = mm3(o, HH[:, kc, s], HL[:, kc, s], h[:, q], l[:, q], kc == 0, kc == KC - 1)
                    toks.append((n, qt, o, tok))
                done_tile(i, tok)
                free[b] = take_turns(handle, toks)
            h_free[0] = tok

        def out_proj():
            ytoks, pend = [], None
            for t in range(4):
                i = next_tile("T")
                h, l = wt(i)
                b = t % 4
                fr, outs = [], []
                for c in range(2):
                    m = 2 * t + c
                    o = banks[b][:, 256 * c:256 * c + 256]
                    pe.wait(free[b], split_tok[i])
                    for kc in range(KC):
                        if m == 0:
                            pe.wait(ot_tok[kc])
                        q = slice((c * KC + kc) * 128, (c * KC + kc) * 128 + 128)
                        tok = mm3(o, h[:, q], l[:, q], HH[:, kc, :], HL[:, kc, :], kc == 0, kc == KC - 1)
                    outs.append((m, o))
                done_tile(i, tok)
                if pend is not None:
                    for m, jt in pend:
                        stat_add(m, jt)
                pend = []
                for m, o in outs:
                    ty = dve.do(lambda e, m=m, o=o: e.tensor_copy(Y[:, m, :], o), tok)
                    ytoks.append(ty)
                    pend.append((m, stat_start(Y[:, m, :], ty)))
                    fr.append(ty)
                free[b] = fr
            for m, jt in pend:
                st = stat_add(m, jt)
            h_free[0] = tok
            return ytoks, st

        def ffn(htoks):
            with ExitStack() as ph:
                AH = sb([128, FC, S], R, ph)
                AL = sb([128, FC, S], R, ph)
                SG = [Y[:, 4 + k, :] for k in range(2)]
                PV = [Y[:, 6 + k, :] for k in range(2)]
                sg_free, pv_free = [None] * 2, [None] * 2
                atoks = []
                for j in range(FC):
                    i = next_tile("GU")
                    h, l = wt(i)
                    b = j % 3
                    pe.wait(free[b], split_tok[i])
                    for c in range(2):
                        o = banks[b][:, 256 * c:256 * c + 256]
                        for kc in range(KC):
                            if j == 0 and c == 0:
                                pe.wait(htoks[kc])
                            q = slice((c * KC + kc) * 128, (c * KC + kc) * 128 + 128)
                            tok = mm3(o, h[:, q], l[:, q], HH[:, kc, :], HL[:, kc, :], kc == 0, kc == KC - 1)
                    done_tile(i, tok)
                    s, v, bb = SG[j % 2], PV[j % 2], banks[b]
                    t1 = act.do(lambda e, s=s, bb=bb: e.activation(s, bb[:, 0:256], ACT.Silu),
                                tok, sg_free[j % 2])
                    t2 = dve.do(lambda e, s=s, v=v, bb=bb: e.tensor_tensor(
                        v, s, bb[:, 256:512], ALU.mult), t1, pv_free[j % 2])
                    th = act.do(lambda e, v=v, j=j: e.activation(AH[:, j, :], v, ACT.Copy), t2)
                    tl = dve.do(lambda e, v=v, j=j: e.tensor_tensor(
                        AL[:, j, :], v, AH[:, j, :].bitcast(F), ALU.subtract), th)
                    sg_free[j % 2], pv_free[j % 2] = t2, tl
                    free[b] = [t2]
                    atoks.append([th, tl])
                h_free[0] = tok
                ytoks, pend = [], None
                for m in range(KC):
                    b = 3 + m % 3
                    o = banks[b][:, 0:256]
                    pe.wait(free[b])
                    for half in range(2):
                        i = next_tile("DN")
                        h, l = wt(i)
                        pe.wait(split_tok[i])
                        for kk in range(11):
                            kc = 11 * half + kk
                            if m == 0:
                                pe.wait(atoks[kc])
                            q = slice(kk * 128, kk * 128 + 128)
                            last = kk == 10 and half == 1
                            tok = mm3(o, h[:, q], l[:, q], AH[:, kc, :], AL[:, kc, :], kc == 0, last,
                                      sig=kk == 10)
                        done_tile(i, tok)
                    ty = dve.do(lambda e, m=m, o=o: e.tensor_copy(Y[:, m, :], o), tok)
                    ytoks.append(ty)
                    jt = stat_start(Y[:, m, :], ty)
                    free[b] = [ty]
                    if pend is not None:
                        stat_add(m - 1, pend)
                    pend = jt
                return ytoks, stat_add(KC - 1, pend)

        ot_tok = [None] * KC

        def transposed(o_sb, o_toks, scale_of, ring=(0, 1)):
            for c in range(KC):
                b = ring[c % len(ring)]
                pe.wait(free[b])
                for qt in range(2):
                    tok = pe.do(lambda e, qt=qt, b=b, c=c: e.transpose(
                        banks[b][:, 128 * qt:128 * qt + 128], o_sb[:, qt, 128 * c:128 * c + 128], ident),
                        o_toks[qt][c // 4], small)
                src = banks[b][:, 0:S]
                if scale_of is None:
                    th = act.do(lambda e, c=c, src=src: e.activation(HH[:, c, :], src, ACT.Copy), tok, h_free[0])
                    tl = dve.do(lambda e, c=c, src=src: e.tensor_tensor(
                        HL[:, c, :], src, HH[:, c, :].bitcast(F), ALU.subtract), th)
                else:
                    w = scale_of(c)
                    th = act.do(lambda e, c=c, src=src, w=w: e.activation(
                        HH[:, c, :], src, ACT.Copy, scale=w), tok, h_free[0])
                    tl = dve.do(lambda e, c=c, src=src, w=w: e.scalar_tensor_tensor(
                        out=HL[:, c, :], in0=src, scalar=w, in1=HH[:, c, :].bitcast(F),
                        op0=ALU.mult, op1=ALU.subtract), th)
                free[b] = [th, tl]
                ot_tok[c] = [th, tl]

        def softmax_heads(insts, P):
            n = len(insts)
            fr_s, fr_p, fr_n, fr_t = P["fr_s"], P["fr_p"], P["fr_n"], P["fr_t"]

            def score(i):
                a = insts[i]
                g = P["n"] + i
                K = 128 * (a["qt"] + 1)
                b = 4 + g % 2
                ps = banks[b][:, 0:K]
                pe.wait(fr_s[g % 2], free[b], a["toks"])
                t = pe.do(lambda e: e.matmul(ps, a["q"][:, 128 * a["qt"]:128 * a["qt"] + 128], a["k"][:, 0:K],
                                             start=True, stop=True, skip_group_check=True))
                s, p = P["s"][g % 3], P["p"][g % 3]
                nm = P["nm"][:, g % 8:g % 8 + 1]
                t = dve.do(lambda e: e.tensor_tensor_reduce(
                    out=s[:, 0:K], in0=ps, in1=a["bias"], scale=-1.0, scalar=a["start"], op0=ALU.add, op1=ALU.min,
                    accum_out=nm), t, fr_n[g % 3], bias_ready, a.get("nmwait"))
                fr_s[g % 2] = t
                if a.get("keep") is not None:
                    t2 = dve.do(lambda e: e.tensor_copy(a["keep"], nm), t)
                    a["kept"].append(t2)
                    tx = [t, t2]
                else:
                    tx = t
                t = act.do(lambda e: e.activation(p[:, 0:K], s[:, 0:K], ACT.Exp, scale=-1.0, bias=nm,
                                                  accum_out=a["sum"]), t, fr_p[g % 3])
                fr_n[g % 3] = t
                a["exp"] = t
                a["sums"].append(t)

            def turn(i):
                a = insts[i]
                g = P["n"] + i
                K = 128 * (a["qt"] + 1)
                p, pT = P["p"][g % 3], P["pT"][g % 3]
                b = 6 + g % 2
                pe.wait(fr_t[g % 2], free[b], a["exp"])
                for kt in range(a["qt"] + 1):
                    o = banks[b][:, 128 * kt:128 * kt + 128]
                    t = pe.do(lambda e, kt=kt, o=o: e.transpose(o, p[:, 128 * kt:128 * kt + 128], ident))
                fr_p[g % 3] = t
                src = banks[b][:, 0:K]
                if g % 2:
                    t = act.do(lambda e: e.activation(pT[:, 0:K], src, ACT.Copy), t, P["fr_pt"][g % 3])
                else:
                    t = dve.do(lambda e: e.tensor_copy(pT[:, 0:K], src), t, P["fr_pt"][g % 3])
                fr_t[g % 2] = t
                a["turned"] = t

            def value(i):
                a = insts[i]
                g = P["n"] + i
                pT = P["pT"][g % 3]
                pe.wait(a["turned"], free[a["ob"]], a["vtoks"])
                for kt in range(a["qt"] + 1):
                    t = pe.do(lambda e, kt=kt: e.matmul(
                        a["out"], pT[:, 128 * kt:128 * kt + 128], a["v"][kt], start=(kt == 0),
                        stop=(kt == a["qt"]), skip_group_check=True))
                P["fr_pt"][g % 3] = t
                if a.get("after"):
                    a["after"](t)

            for i in range(n + 2):
                if i < n:
                    score(i)
                if 1 <= i <= n:
                    turn(i - 1)
                if i >= 2:
                    value(i - 2)
            P["n"] += n

        def att_pool(ph):
            P = {"s": [sb([128, S], F, ph) for _ in range(3)], "p": [sb([128, S], F, ph) for _ in range(3)],
                 "pT": [sb([128, S], F, ph) for _ in range(3)], "nm": sb([128, 8], F, ph),
                 "fr_s": [None] * 2, "fr_p": [None] * 3, "fr_n": [None] * 3, "fr_t": [None] * 2,
                 "fr_pt": [None] * 3, "n": 0}
            return P

        def heads_list(P, qt, Q, K, V, bias, ob, sums, sumtoks, qtoks, vtoks, after, grouped=True, sink=None):
            out = []
            for h in range(8):
                if grouped:
                    g = h // 4
                    q, kk = Q[64 * g:64 * g + 64, h % 4, :], K[64 * g:64 * g + 64, :]
                    v = [V[:, kt, 64 * g:64 * g + 64] for kt in range(2)]
                else:
                    r = 64 * (h % 2)
                    q, kk = Q[r:r + 64, h // 2, :], K[r:r + 64, h // 2, :]
                    v = [V[:, kt, 64 * h:64 * h + 64] for kt in range(2)]
                a = dict(q=q, k=kk, v=v, qt=qt, bias=bias(h)[:, 0:256] if qt else bias(h)[:, 128:256],
                         start=BIG, ob=ob, out=banks[ob][:, 64 * h:64 * h + 64], sum=sums[:, h:h + 1],
                         sums=sumtoks, toks=qtoks, vtoks=vtoks)
                if sink is not None:
                    a["start"] = sink["neg"][:, h:h + 1]
                    a["keep"] = sink["nm"][:, h:h + 1]
                    a["kept"] = sink["toks"]
                if h == 7:
                    a["after"] = after
                out.append(a)
            return out

        def bc(ap, n):
            return ap.unsqueeze(2).to_broadcast([ap.shape[0], ap.shape[1], n])

        def mixer_ab(htoks):
            with ExitStack() as ph:
                KVT = sb([128, 4, S], F, ph)
                QA = sb([128, 4, S], F, ph)
                KB = sb([128, S], F, ph)
                QB = sb([128, 4, S], F, ph)
                VM = sb([128, 2, 408], F, ph)
                CA = sb([128, 2, 2, 272], F, ph)
                KCT = sb([128, 16], F, ph)
                VBD = sb([128, 512], F, ph)
                BC = sb([128, 2, 8, 16], F, ph)
                SC = sb([128, 8, 16], F, ph)
                PC = sb([128, 8, 16], F, ph)
                PCT = sb([128, 128], F, ph)
                O = Y[:, :, :].rearrange("p c s -> p (c s)").rearrange("p (q d) -> p q d", q=2)
                OT = sb([128, 512], F, ph)
                OT2 = sb([128, 512], F, ph)
                GT = sb([128, 2, 24], F, ph)
                NS = sb([128, 8], F, ph)
                SM = sb([128, 64], F, ph)
                P = att_pool(ph)
                act.dma(s_sk, lambda e: e.dma_start(SM[:, 0:8], sinks.partition_broadcast(128)))
                kvt, qa, qb = [], [], []

                def take(n, o, tok):
                    if n < 4:
                        t = dve.do(lambda e: e.tensor_copy(KVT[:, n, :], o), tok)
                        kvt.append(t)
                    elif n < 8:
                        t = act.do(lambda e: e.activation(QA[:, n - 4, :], o, ACT.Copy, scale=0.125), tok)
                        qa.append(t)
                    elif n == 8:
                        t = dve.do(lambda e: e.tensor_copy(KB[:, :], o), tok)
                        qb.append(t)
                    else:
                        t = act.do(lambda e: e.activation(QB[:, n - 9, :], o, ACT.Copy, scale=0.125), tok)
                        qb.append(t)
                    return t

                proj_T(AB_T, htoks, take, (0, 1, 2, 3))
                vm = []

                def take_m(n, qt, o, tok):
                    m = 256 if n == 0 else 152
                    t = dve.do(lambda e: e.tensor_copy(VM[:, qt, 256 * n:256 * n + m], o), tok)
                    vm.append(t)
                    return t

                proj_M(AB_M, take_m, (0, 1))

                tz = dve.do(lambda e: e.memset(CA[:, :, :, 256:272], 0.0))
                cat = []
                for kv in range(2):
                    for v in range(2):
                        cat.append(dve.do(lambda e, kv=kv, v=v: e.tensor_tensor(
                            CA[:, kv, v, 0:256].rearrange("p (n l) -> p n l", l=16),
                            KVT[:, kv, :].rearrange("p (n l) -> p n l", l=16),
                            VEC[:, V_PE + 16 * v:V_PE + 16 * v + 16].unsqueeze(1).to_broadcast([128, 16, 16]),
                            ALU.add), kvt, small))
                pe.wait(free[2], free[3], cat, tz)
                for kv in range(2):
                    for half in range(2):
                        i = next_tile("CMP")
                        w = raw[i % RAW][:, :].rearrange("p (l m) -> p l m", l=16)
                        pe.wait(raw_ready(i))
                        for l in range(16):
                            c0 = 16 * half + l
                            src = CA[:, kv, half, c0:c0 + 241:16]
                            first, last = (half == 0 and l == 0), (half == 1 and l == 15)
                            if kv == 0:
                                f = lambda e, w=w, l=l, src=src, a=first, z=last: e.matmul(
                                    banks[2][:, 0:16], w[:, l, :], src, start=a, stop=z, skip_group_check=True)
                            else:
                                f = lambda e, w=w, l=l, src=src, a=first, z=last: e.matmul(
                                    banks[3][0:16, 0:128], src, w[:, l, :], start=a, stop=z, skip_group_check=True)
                            tok = pe.do(f) if l == 15 else pe.run(f)
                        done_tile(i, tok)
                    if kv == 0:
                        tk = dve.do(lambda e: e.tensor_copy(KCT[:, :], banks[2][:, 0:16]), tok)
                tv = dve.do(lambda e: e.tensor_copy(PCT[0:16, :], banks[3][0:16, 0:128]), tok)
                tok = mm(banks[3][:, 0:128], rep16, PCT[0:16, :], toks=[tv, small])
                tv = dve.do(lambda e: e.tensor_tensor(
                    VBD[:, :].rearrange("p (g r e) -> p g r e", g=2, r=4),
                    banks[3][:, 0:128].rearrange("p (g e) -> p g e", g=2).unsqueeze(2).to_broadcast([128, 2, 4, 64]),
                    hsel.rearrange("p (g r) -> p g r", g=2).unsqueeze(3).to_broadcast([128, 2, 4, 64]),
                    ALU.mult), tok, small)
                free[2], free[3] = [tk], [tv]

                tg = []
                for qt in range(2):
                    t = act.do(lambda e, qt=qt: e.activation(GT[:, qt, :], VM[:, qt, 384:408], ACT.Exp, scale=-1.0), vm)
                    t = dve.do(lambda e, qt=qt: e.tensor_scalar(GT[:, qt, :], GT[:, qt, :], 1.0, None, ALU.add), t)
                    tg.append(dve.do(lambda e, qt=qt: e.reciprocal(GT[:, qt, :], GT[:, qt, :]), t))
                t = dve.do(lambda e: e.memset(BC[:, :, :, :], NEG))
                t1 = dve.do(lambda e: e.tensor_copy(BC[:, 0, :, 0:7], BIAS[:, 0:8, 159:256:16]), t, bias_ready)
                t2 = dve.do(lambda e: e.tensor_copy(BC[:, 1, :, 0:15], BIAS[:, 0:8, 31:256:16]), t)
                tb = [t1, t2]
                tns = dve.do(lambda e: e.tensor_scalar(NS[:, :], SM[:, 0:8], -1.0, None, ALU.mult), (s_sk, 16))

                o_toks = [[None, None], [None, None]]
                prev = {"pc": tv}
                for qt in range(2):
                    mx, sm, rc = SM[:, 8:16], SM[:, 16:24], SM[:, 24:32]
                    pe.wait(free[2], free[3], qa, tk)
                    for h in range(8):
                        g = h // 4
                        tok = pe.do(lambda e, h=h, g=g, qt=qt: e.matmul(
                            banks[2 + g][:, 16 * h:16 * h + 16],
                            QA[64 * g:64 * g + 64, h % 4, 128 * qt:128 * qt + 128], KCT[64 * g:64 * g + 64, :],
                            start=True, stop=True, skip_group_check=True))
                    for g in range(2):
                        t = dve.do(lambda e, qt=qt, g=g: e.tensor_tensor(
                            SC[:, 4 * g:4 * g + 4, :],
                            banks[2 + g][:, 64 * g:64 * g + 64].rearrange("p (h n) -> p h n", h=4),
                            BC[:, qt, 4 * g:4 * g + 4, :], ALU.add), tok, tb, prev["pc"])
                        free[2 + g] = [t]
                    t = dve.do(lambda e: e.tensor_reduce(mx, SC[:, :, :], AX.X, ALU.max), t)
                    t = dve.do(lambda e: e.tensor_tensor(SC[:, :, :], SC[:, :, :], bc(mx, 16), ALU.subtract), t)
                    t = act.do(lambda e: e.activation(PC[:, :, :], SC[:, :, :], ACT.Exp), t, prev["pc"])
                    te = t
                    t = dve.do(lambda e: e.tensor_reduce(sm, PC[:, :, :], AX.X, ALU.add), t)
                    t = dve.do(lambda e: e.reciprocal(rc, sm), t)
                    t = dve.do(lambda e, qt=qt: e.tensor_tensor(rc, rc, GT[:, qt, 0:24:3], ALU.mult), t, tg)
                    if qt == 0:
                        t = dve.do(lambda e: e.tensor_scalar(rc, rc, VEC[:, V_ROW:V_ROW + 1], None, ALU.mult), t)
                    trc = t
                    pe.wait(free[0])
                    tok = pe.do(lambda e: e.transpose(banks[0][:, 0:128], PC[:, :, :].rearrange("p h n -> p (h n)"),
                                                      ident), te)
                    t = dve.do(lambda e: e.tensor_copy(PCT[:, :], banks[0][:, 0:128]), tok, prev["pc"])
                    free[0] = [t]
                    pe.wait(free[1])
                    tok = mm(banks[1][:, 0:512], PCT[:, :], VBD[:, :], toks=[t, tv])
                    prev["pc"] = [tok, trc]
                    acc = O[:, qt, 0:512].rearrange("p (h e) -> p h e", h=8)
                    t = dve.do(lambda e, acc=acc: e.tensor_tensor(
                        acc, banks[1][:, 0:512].rearrange("p (h e) -> p h e", h=8), bc(rc, 64), ALU.mult),
                        tok, trc)
                    free[1] = [t]
                    last = [t]
                    lst = []
                    for w, (kc, vo, bank) in enumerate(((2, 0, 0), (3, 128, 1))):
                        sums = SM[:, 32 + 8 * w:40 + 8 * w]
                        stoks = []

                        def after(tok, w=w, bank=bank, sums=sums, stoks=stoks, qt=qt, acc=acc):
                            t = dve.do(lambda e: e.reciprocal(sums, sums), stoks)
                            t = dve.do(lambda e: e.tensor_tensor(sums, sums, GT[:, qt, 1 + w:24:3], ALU.mult), t, tg)
                            tmp = OT if w == 0 else OT2
                            t = dve.do(lambda e: e.tensor_tensor(
                                tmp[:, :].rearrange("p (h e) -> p h e", h=8),
                                banks[bank][:, :].rearrange("p (h e) -> p h e", h=8), bc(sums, 64), ALU.mult), t, tok)
                            free[bank] = [t]
                            t = dve.do(lambda e: e.tensor_tensor(
                                acc, acc, tmp[:, :].rearrange("p (h e) -> p h e", h=8), ALU.add), t, last[0])
                            last[0] = t
                            if w == 1:
                                o_toks[qt][0] = t

                        lst += heads_list(P, qt, QA, KVT[:, kc, :], VM[:, :, vo:vo + 128], lambda h: BIAS[:, h, :],
                                          bank, sums, stoks, qa + kvt, vm, after)
                    sums, es, nms = SM[:, 48:56], SM[:, 56:64], MB[:, 0:8]
                    stoks, keeps = [], []

                    def after_b(tok, sums=sums, es=es, nms=nms, stoks=stoks, keeps=keeps, qt=qt):
                        t = dve.do(lambda e: e.tensor_tensor(es, nms, NS[:, :], ALU.subtract), keeps, tns)
                        t = act.do(lambda e: e.activation(es, es, ACT.Exp), t)
                        t = dve.do(lambda e: e.tensor_tensor(sums, sums, es, ALU.add), t, stoks)
                        t = dve.do(lambda e: e.reciprocal(sums, sums), t)
                        t = dve.do(lambda e: e.tensor_tensor(
                            O[:, qt, 512:1024].rearrange("p (h e) -> p h e", h=8),
                            banks[3][:, :].rearrange("p (h e) -> p h e", h=8), bc(sums, 64), ALU.mult), t, tok)
                        free[3] = [t]
                        o_toks[qt][1] = t

                    lst += heads_list(P, qt, QB, KB[:, :], VM[:, :, 256:384], lambda h: BIAS[:, 8 + h, :], 3,
                                      sums, stoks, qb, vm, after_b, sink={"neg": NS, "nm": nms, "toks": keeps})
                    for a in lst[16:24]:
                        a["nmwait"] = tns
                    softmax_heads(lst, P)
                release(P)
                transposed(O, o_toks, None)
                return out_proj()

        def release(P):
            free[4] = free[5] = [t for t in P["fr_s"] if t]
            free[6] = free[7] = [t for t in P["fr_t"] if t]

        def plain_after(O, qt, half, bank, sums, stoks, o_toks, done=None):
            def after(tok):
                t = dve.do(lambda e: e.reciprocal(sums, sums), stoks)
                t = dve.do(lambda e: e.tensor_tensor(
                    O[:, qt, 512 * half:512 * half + 512].rearrange("p (h e) -> p h e", h=8),
                    banks[bank][:, :].rearrange("p (h e) -> p h e", h=8), bc(sums, 64), ALU.mult), t, tok)
                free[bank] = [t]
                o_toks[qt][half] = t
                if done:
                    done(t)
            return after

        def mixer_cd(htoks):
            with ExitStack() as ph:
                KCm = sb([128, S], F, ph)
                QC = sb([128, 4, S], F, ph)
                QD = sb([128, 4, S], F, ph)
                KD = sb([128, 4, S], F, ph)
                VC = sb([128, 2, 128], F, ph)
                VD = sb([128, 2, 512], F, ph)
                O = Y[:, :, :].rearrange("p c s -> p (c s)").rearrange("p (q d) -> p q d", q=2)
                SM = sb([128, 16], F, ph)
                Z = [sb([128, 384], F, ph) for _ in range(2)]
                AZ = [sb([128, 384], F, ph) for _ in range(2)]
                SPm = [sb([128, 384], F, ph) for _ in range(2)]
                WT = [sb([128, 384], F, ph) for _ in range(2)]
                P = att_pool(ph)
                kq, dq = [], []

                def take(n, o, tok):
                    if n == 0:
                        t = dve.do(lambda e: e.tensor_copy(KCm[:, :], o), tok)
                        kq.append(t)
                    elif n < 5:
                        t = act.do(lambda e: e.activation(QC[:, n - 1, :], o, ACT.Copy, scale=0.125), tok)
                        kq.append(t)
                    elif n < 9:
                        t = act.do(lambda e: e.activation(QD[:, n - 5, :], o, ACT.Copy, scale=0.125), tok)
                        dq.append(t)
                    else:
                        t = dve.do(lambda e: e.tensor_copy(KD[:, n - 9, :], o), tok)
                        dq.append(t)
                    return t

                proj_T(CD_T, htoks, take, (0, 1, 2, 3))
                vt, dt_ = [], []

                def take_m(n, qt, o, tok):
                    if n == 0:
                        t = dve.do(lambda e: e.tensor_copy(VC[:, qt, :], o), tok)
                        vt.append(t)
                    else:
                        t = dve.do(lambda e: e.tensor_copy(VD[:, qt, 256 * (n - 1):256 * n], o), tok)
                        dt_.append(t)
                    return t

                proj_M(CD_M, take_m, (0, 1, 2))
                o_toks = [[None, None], [None, None]]
                lst = []
                for qt in range(2):
                    stoks = []
                    sums = SM[:, 8 * qt:8 * qt + 8]
                    lst += heads_list(P, qt, QC, KCm[:, :], VC[:, :, :], lambda h: BIAS[:, h, :], qt, sums, stoks,
                                      kq, vt, plain_after(O, qt, 0, qt, sums, stoks, o_toks))
                softmax_heads(lst, P)
                release(P)

                zf = [None] * 2
                wf = [None] * 2
                spf = [None] * 2
                pe.wait(free[0], free[1])

                def first(h):
                    j = h % 2
                    r = 64 * (h % 2)
                    q, kk = QD[r:r + 64, h // 2, :], KD[r:r + 64, h // 2, :]
                    b = 4 + j
                    pe.wait(free[b], dq)
                    pe.run(lambda e: e.matmul(banks[b][:, 0:256], kk[:, 0:128], q, start=True, stop=True,
                                              skip_group_check=True))
                    t = pe.do(lambda e: e.matmul(banks[b][:, 256:384], kk[:, 128:256], q[:, 128:256], start=True,
                                                 stop=True, skip_group_check=True))
                    tz = dve.do(lambda e: e.tensor_tensor(Z[j][:, :], banks[b][:, 0:384], strict, ALU.add), t, zf[j])
                    free[b] = [tz]
                    t = dve.do(lambda e: e.scalar_tensor_tensor(
                        out=AZ[j][:, :], in0=Z[j][:, :], scalar=-1.0, in1=Z[j][:, :], op0=ALU.mult, op1=ALU.min),
                        tz, spf[j])
                    t = act.do(lambda e: e.activation(AZ[j][:, :], AZ[j][:, :], ACT.Exp), t)
                    t = act.do(lambda e: e.activation(AZ[j][:, :], AZ[j][:, :], ACT.Ln, bias=1.0), t)
                    return dve.do(lambda e: e.scalar_tensor_tensor(
                        out=SPm[j][:, :], in0=Z[j][:, :], scalar=0.0, in1=AZ[j][:, :], op0=ALU.max, op1=ALU.add), t)

                def second(h, tsp):
                    j = h % 2
                    b = 6 + j
                    pe.wait(free[b], tsp)
                    pe.run(lambda e: e.matmul(banks[b][:, 0:256], tri, SPm[j][:, 0:256], start=True, stop=False,
                                              skip_group_check=True))
                    pe.run(lambda e: e.matmul(banks[b][:, 128:256], ones, SPm[j][:, 256:384], start=False, stop=True,
                                              skip_group_check=True))
                    t = pe.do(lambda e: e.matmul(banks[b][:, 256:384], tri, SPm[j][:, 256:384], start=False, stop=True,
                                                 skip_group_check=True))
                    spf[j] = t
                    t = dve.do(lambda e: e.tensor_tensor(Z[j][:, :], Z[j][:, :], banks[b][:, 0:384], ALU.subtract), t)
                    free[b] = [t]
                    t = act.do(lambda e: e.activation(WT[j][:, :], Z[j][:, :], ACT.Exp), t, wf[j])
                    zf[j] = t
                    return t

                def third(h, tw):
                    j = h % 2
                    v = [VD[:, kt, 64 * h:64 * h + 64] for kt in range(2)]
                    pe.wait(tw, dt_, free[2], free[3])
                    pe.run(lambda e: e.matmul(banks[2][:, 64 * h:64 * h + 64], WT[j][:, 0:128], v[0], start=True,
                                              stop=True, skip_group_check=True))
                    pe.run(lambda e: e.matmul(banks[3][:, 64 * h:64 * h + 64], WT[j][:, 128:256], v[0], start=True,
                                              stop=False, skip_group_check=True))
                    t = pe.do(lambda e: e.matmul(banks[3][:, 64 * h:64 * h + 64], WT[j][:, 256:384], v[1],
                                                 start=False, stop=True, skip_group_check=True))
                    wf[j] = t
                    return t

                a, b_ = {}, {}
                for i in range(10):
                    if i < 8:
                        a[i] = first(i)
                    if 1 <= i <= 8:
                        b_[i - 1] = second(i - 1, a[i - 1])
                    if i >= 2:
                        tok = third(i - 2, b_[i - 2])
                for qt in range(2):
                    t = dve.do(lambda e, qt=qt: e.tensor_copy(O[:, qt, 512:1024], banks[2 + qt][:, :]), tok)
                    free[2 + qt] = [t]
                    o_toks[qt][1] = t
                transposed(O, o_toks, None)
                return out_proj()

        def hybrid(layer, htoks):
            with ExitStack() as ph:
                GL = sb([16, S], F, ph)
                GW = sb([16, 256], F, ph)
                GQ = sb([128, 2, S], F, ph)
                GK = sb([128, 2, S], F, ph)
                Q = sb([128, 4, S], F, ph)
                K = sb([128, 4, S], F, ph)
                QP = [sb([128, S], F, ph) for _ in range(2)]
                R1 = [sb([128, S], F, ph) for _ in range(2)]
                V = sb([128, 2, 512], F, ph)
                GV = sb([128, 2, 512], F, ph)
                GR = sb([128, 2, 512], F, ph)
                O = Y[:, :, :].rearrange("p c s -> p (c s)").rearrange("p (q d) -> p q d", q=2)
                SM = sb([128, 40], F, ph)
                P = att_pool(ph)
                s_g = s_gu
                act.dma(s_g, lambda e: e.dma_start(GW[:, :], gup[layer]))
                gw_ready = (s_g, 16 * (layer + 1))
                kq, gq, gl = [], [], []
                qpf = [None] * 2
                r1f = [None] * 2

                def take(n, o, tok):
                    if n == 0:
                        t = dve.do(lambda e: e.tensor_copy(GL[:, :], o), tok)
                        gl.append(t)
                        return t
                    if n < 3:
                        t = act.do(lambda e: e.activation(GQ[:, n - 1, :], o, ACT.Copy, scale=0.125), tok)
                        gq.append(t)
                        return t
                    if n < 5:
                        t = dve.do(lambda e: e.tensor_copy(GK[:, n - 3, :], o), tok)
                        gq.append(t)
                        return t
                    j = n % 2
                    dst = Q[:, n - 5, :] if n < 9 else K[:, n - 9, :]
                    sc = 0.125 if n < 9 else 1.0
                    t = act.do(lambda e: e.activation(QP[j][:, :], o, ACT.Copy, scale=sc), tok, qpf[j])
                    free_o = t
                    b = 4 + j
                    t2 = mm(banks[b][:, 0:256], rot, QP[j][:, :], toks=[t, free[b], small])
                    t3 = dve.do(lambda e: e.tensor_tensor(R1[j][:, :], banks[b][:, 0:256], sinT, ALU.mult), t2, r1f[j])
                    free[b] = [t3]
                    t4 = dve.do(lambda e: e.tensor_tensor(dst, QP[j][:, :], cosT, ALU.mult), t)
                    t5 = dve.do(lambda e: e.tensor_tensor(dst, dst, R1[j][:, :], ALU.add), t3, t4)
                    qpf[j] = [t4, t2]
                    r1f[j] = t5
                    kq.append(t5)
                    return free_o

                proj_T(HY_T, htoks, take, (0, 1, 2, 3))
                vt, gv, gr = [], [], []

                def take_m(n, qt, o, tok):
                    dst = (V, GV, GR)[n // 2][:, qt, 256 * (n % 2):256 * (n % 2) + 256]
                    lst = (vt, gv, gr)[n // 2]
                    if n < 4:
                        t = dve.do(lambda e: e.tensor_copy(dst, o), tok)
                    else:
                        t = act.do(lambda e: e.activation(dst, o, ACT.Copy), tok)
                    lst.append(t)
                    return t

                proj_M(HY_M, take_m, (0, 1, 2, 3))
                o_toks = [[None, None], [None, None]]
                lst = []
                sq = R1
                nw = V_ONORM + 8 * layer
                for qt in range(2):
                    stoks = []
                    sums = SM[:, 8 * qt:8 * qt + 8]

                    def norm(t, qt=qt):
                        ss = SM[:, 16 + qt:17 + qt]
                        t1 = act.do(lambda e: e.activation(SQ512[:, :], O[:, qt, 0:512], ACT.Square, accum_out=ss), t,
                                    sq512_free[0])
                        t2 = act.do(lambda e: e.activation(ss, ss, ACT.Ln, scale=1.0 / 512, bias=eps), t1)
                        t3 = act.do(lambda e: e.activation(ss, ss, ACT.Exp, scale=-0.5), t2)
                        sq512_free[0] = t1
                        o_toks[qt][0] = dve.do(lambda e: e.tensor_scalar(
                            O[:, qt, 0:512], O[:, qt, 0:512], ss, None, ALU.mult), t3)

                    lst += heads_list(P, qt, Q, K, V, lambda h: dil, qt, sums, stoks, kq, vt,
                                      plain_after(O, qt, 0, qt, sums, stoks, o_toks, norm), grouped=False)
                SQ512 = sb([128, 512], F, ph)
                sq512_free = [None]
                softmax_heads(lst, P)
                release(P)

                with ExitStack() as p2:
                    ONE, B, T1, T2, E1, E2 = (BIAS[:, k, :] for k in range(6))
                    X1, X2, QD_, KD_ = ([BIAS[:, 6 + 2 * k + n, :] for n in range(2)] for k in range(4))
                    AT = [sb([128, 384], F, p2) for _ in range(2)]
                    SG = sb([128, 512], F, p2)
                    one_t = dve.do(lambda e: e.memset(ONE[:, :], 1.0), sq512_free[0])
                    atz = [dve.do(lambda e, j=j: e.memset(AT[j][:, :], 0.0)) for j in range(2)]
                    atf = [atz[0], atz[1]]
                    ready = []
                    chain = one_t
                    for p in range(2):
                        z = mm(banks[4][:, 0:256], GW[:, 128 * p:128 * p + 128], GL[:, :],
                               toks=[gl, gw_ready, free[4]])
                        gb = VEC[:, V_GB + 2 * layer + p:V_GB + 2 * layer + p + 1]
                        t = dve.do(lambda e, gb=gb: e.tensor_scalar(B[:, :], banks[4][:, 0:256], gb, None, ALU.add),
                                   z, chain)
                        free[4] = [t]
                        t = dve.do(lambda e: e.scalar_tensor_tensor(
                            out=T1[:, :], in0=B[:, :], scalar=-1.0, in1=B[:, :], op0=ALU.mult, op1=ALU.min), t)
                        t = act.do(lambda e: e.activation(T1[:, :], T1[:, :], ACT.Exp), t)
                        t = act.do(lambda e: e.activation(T1[:, :], T1[:, :], ACT.Ln, bias=1.0), t)
                        t = dve.do(lambda e: e.scalar_tensor_tensor(
                            out=T1[:, :], in0=B[:, :], scalar=0.0, in1=T1[:, :], op0=ALU.min, op1=ALU.subtract), t)
                        tb = dve.do(lambda e: e.tensor_tensor_scan(
                            B[:, :], ONE[:, :], T1[:, :], 0.0, ALU.mult, ALU.add), t)
                        t = dve.do(lambda e: e.tensor_scalar(
                            T1[:, :], B[:, :], B[:, 127:128], None, ALU.subtract), tb)
                        t = dve.do(lambda e: e.scalar_tensor_tensor(
                            out=T1[:, :], in0=T1[:, :], scalar=-1.0, in1=T1[:, :], op0=ALU.mult, op1=ALU.min), t)
                        t = act.do(lambda e: e.activation(E1[:, :], T1[:, :], ACT.Exp, scale=1.0 / 16), t)
                        t1 = dve.do(lambda e, p=p: e.tensor_tensor(
                            X1[p][:, 0:128], E1[:, 0:128], GK[:, p, 0:128], ALU.mult), t, gq)
                        t2 = dve.do(lambda e, p=p: e.tensor_tensor(
                            X1[p][:, 128:256], E1[:, 128:256], GQ[:, p, 128:256], ALU.mult), t)
                        v4 = lambda a: a.rearrange("p (c t) -> p c t", c=2)
                        t = dve.do(lambda e: e.tensor_tensor(
                            v4(T2[:, :]), v4(B[:, :]), B[:, 63:192:128].unsqueeze(2).to_broadcast([128, 2, 128]),
                            ALU.subtract), tb)
                        t = dve.do(lambda e: e.scalar_tensor_tensor(
                            out=T2[:, :], in0=T2[:, :], scalar=-1.0, in1=T2[:, :], op0=ALU.mult, op1=ALU.min), t)
                        t = act.do(lambda e: e.activation(E2[:, :], T2[:, :], ACT.Exp, scale=1.0 / 16), t)
                        t3 = dve.do(lambda e, p=p: e.tensor_tensor(
                            v4(X2[p][:, :])[:, :, 0:64], v4(E2[:, :])[:, :, 0:64], v4(GK[:, p, :])[:, :, 0:64],
                            ALU.mult), t)
                        t4 = dve.do(lambda e, p=p: e.tensor_tensor(
                            v4(X2[p][:, :])[:, :, 64:128], v4(E2[:, :])[:, :, 64:128], v4(GQ[:, p, :])[:, :, 64:128],
                            ALU.mult), t)
                        t = dve.do(lambda e: e.tensor_tensor(
                            T1[:, :].rearrange("p (c t) -> p c t", c=4), B[:, :].rearrange("p (c t) -> p c t", c=4),
                            B[:, 31:256:64].unsqueeze(2).to_broadcast([128, 4, 64]), ALU.subtract), t1, t2)
                        t = dve.do(lambda e: e.tensor_scalar(T1[:, :], T1[:, :], 1280.0, -1280.0, ALU.min, ALU.max), t)
                        ta = act.do(lambda e: e.activation(E1[:, :], T1[:, :], ACT.Exp, scale=1.0 / 16), t)
                        tc = act.do(lambda e: e.activation(E2[:, :], T1[:, :], ACT.Exp, scale=-1.0 / 16), t3, t4)
                        t5 = dve.do(lambda e, p=p: e.tensor_tensor(QD_[p][:, :], E1[:, :], GQ[:, p, :], ALU.mult), ta)
                        t6 = dve.do(lambda e, p=p: e.tensor_tensor(KD_[p][:, :], E2[:, :], GK[:, p, :], ALU.mult), tc)
                        chain = [t5, t6]
                        ready.append([t1, t2, t3, t4, t5, t6])
                    causal = hmask
                    for h in range(4):
                        p, r, j = h // 2, 64 * (h % 2), h % 2
                        b = 4 + j
                        x1, x2, qd, kd = (a[p][r:r + 64, :] for a in (X1, X2, QD_, KD_))
                        pe.wait(free[b], ready[p])

                        def m(o, l, rr, b=b):
                            return pe.do(lambda e: e.matmul(o, l, rr, start=True, stop=True, skip_group_check=True))
                        m(banks[b][:, 128:256], x1[:, 0:128], x1[:, 128:256])
                        for hh in range(2):
                            c0 = 0 if hh == 0 else 256
                            t0 = 128 * hh
                            m(banks[b][0:64, c0:c0 + 64], kd[:, t0:t0 + 64], qd[:, t0:t0 + 64])
                            m(banks[b][0:64, c0 + 64:c0 + 128], x2[:, t0:t0 + 64], x2[:, t0 + 64:t0 + 128])
                            tok = m(banks[b][64:128, c0:c0 + 128], kd[:, t0 + 64:t0 + 128], qd[:, t0:t0 + 128])
                        A = AT[j]
                        ta = act.do(lambda e, A=A, b=b: e.activation(A[:, 128:256], banks[b][:, 128:256], ACT.Copy),
                                    tok, atf[j])
                        tc = [dve.do(lambda e, A=A, b=b, c0=c0: e.copy_predicated(
                            A[:, c0:c0 + 128], causal, banks[b][:, c0:c0 + 128]), tok, ta, atf[j], mask_ready)
                            for c0 in (0, 256)]
                        free[b] = [ta] + tc
                        pe.wait(ta, tc, gv)
                        if h == 0:
                            pe.wait(free[6], free[7])
                        v = [GV[:, kt, 128 * h:128 * h + 128] for kt in range(2)]
                        oc = slice(128 * h, 128 * h + 128)
                        mm(banks[6][:, oc], A[:, 0:128], v[0], sig=False)
                        mm(banks[7][:, oc], A[:, 128:256], v[0], stop=False, sig=False)
                        tok = mm(banks[7][:, oc], A[:, 256:384], v[1], start=False)
                        atf[j] = tok
                    gfree = None
                    for qt in range(2):
                        bb = banks[6 + qt]
                        ss = SM[:, 20 + 4 * qt:24 + 4 * qt]
                        g = O[:, qt, 512:1024]
                        t = dve.do(lambda e, bb=bb, g=g: e.tensor_copy(g, bb[:, :]), tok)
                        free[6 + qt] = [t]
                        t1 = act.do(lambda e, g=g: e.activation(SQ512[:, :], g, ACT.Square), t, sq512_free[0], gfree)
                        t2 = dve.do(lambda e, ss=ss: e.tensor_reduce(
                            ss, SQ512[:, :].rearrange("p (h e) -> p h e", h=4), AX.X, ALU.add), t1)
                        sq512_free[0] = t2
                        t3 = act.do(lambda e, ss=ss: e.activation(ss, ss, ACT.Ln, scale=1.0 / 128, bias=eps), t2)
                        t3 = act.do(lambda e, ss=ss: e.activation(ss, ss, ACT.Exp, scale=-0.5), t3)
                        t4 = act.do(lambda e, qt=qt: e.activation(SG[:, :], GR[:, qt, :], ACT.Exp, scale=-1.0), gr, gfree)
                        t4 = dve.do(lambda e: e.tensor_scalar(SG[:, :], SG[:, :], 1.0, None, ALU.add), t4)
                        t4 = dve.do(lambda e: e.reciprocal(SG[:, :], SG[:, :]), t4)
                        t4 = dve.do(lambda e, qt=qt: e.tensor_tensor(SG[:, :], SG[:, :], GR[:, qt, :], ALU.mult), t4)
                        t5 = dve.do(lambda e, g=g: e.tensor_tensor(SG[:, :], SG[:, :], g, ALU.mult), t4)
                        t6 = dve.do(lambda e, g=g, ss=ss: e.tensor_tensor(
                            g.rearrange("p (h e) -> p h e", h=4), SG[:, :].rearrange("p (h e) -> p h e", h=4),
                            bc(ss, 128), ALU.mult), t5, t3)
                        gfree = t6
                        o_toks[qt][1] = t6
                    transposed(O, o_toks, lambda c: VEC[:, nw + c:nw + c + 1])
                    return out_proj()

        t = pool.do(lambda e: e.memset(HM[:, :], 1.0))
        mask_ready = pool.do(lambda e: e.affine_select(
            out=HM[:, :], in_=HM[:, :], compare_op=ALU.is_ge, fill=0.0, base=0, pattern=[[1, 128]],
            channel_multiplier=-1), t)
        hmask = HM[:, :].bitcast(U32)

        xt = [x_in] * KC
        for layer in range(2):
            for sub in range(2):
                mt = modulation(layer, sub)
                h = make_h(x_stats(xt), lambda c: A4[:, c:c + 1], lambda c: MOD[:, c:c + 1], mt)
                if sub == 0:
                    y, st = (mixer_ab if layer == 0 else mixer_cd)(h)
                else:
                    y, st = ffn(h)
                xt = residual(st, lambda c: G4[:, c:c + 1], mt, y)
                mod_tok[0] = xt[-1]
        for layer in range(2):
            for sub in range(2):
                o = V_NORM2 + 32 * layer + 16 * sub
                h = make_h(x_stats(xt), lambda c, o=o: VEC[:, o + c:o + c + 1], None, small)
                y, st = hybrid(layer, h) if sub == 0 else ffn(h)
                xt = residual(st, lambda c, o=o: VEC[:, o + 8 + c:o + 9 + c], small, y)
        sp.dma(s_out, lambda e: e.dma_start(out, X[:, :, :]), xt[-1])
        sp.wait((s_out, 16))
        assert state["use"] == len(TILES)

        block = ctx.enter_context(nc.Block())
        block.sync(sp.emit)
        block.gpsimd(pool.emit)
        block.scalar(act.emit)
        block.vector(dve.emit)
        block.tensor(pe.emit)


def shape_constants():
    c = np.zeros((128, NCONST), np.float32)
    i = np.arange(128)
    c[:, C_ID:C_ID + 128] = i[:, None] == i[None, :]
    c[:, C_TRI:C_TRI + 128] = i[:, None] >= i[None, :]
    c[:, C_ONE:C_ONE + 128] = 1.0
    d = i % 64
    for p in range(128):
        if d[p] < 8:
            c[p + 8, C_ROT + p] = 1.0
        elif d[p] < 16:
            c[p - 8, C_ROT + p] = 1.0
    q = np.arange(256)
    st = np.concatenate([np.where(i[:, None] < q[None, :], 0.0, NEG),
                         np.where(128 + i[:, None] < q[None, 128:], 0.0, NEG)], axis=1)
    c[:, C_STRICT:C_STRICT + 384] = st
    dist = 128 + i[:, None] - q[None, :]
    m = ((dist >= 0) & (dist <= 128)).astype(np.int64) + ((dist >= 0) & (dist % 4 == 0)) + \
        ((dist >= 0) & (dist % 16 == 0))
    c[:, C_DIL:C_DIL + 256] = np.where(m > 0, np.log(np.maximum(m, 1)), NEG)
    inv = (np.float32(500000.0) ** (-(np.arange(8, dtype=np.float32) * np.float32(2.0)) / np.float32(16))).astype(
        np.float32)
    ang = (q.astype(np.float32)[None, :] * inv[:, None]).astype(np.float32).astype(np.float64)
    for p in range(128):
        if d[p] < 16:
            c[p, C_COS:C_COS + 256] = np.cos(ang[d[p] % 8])
            c[p, C_SIN:C_SIN + 256] = np.sin(ang[d[p] % 8]) * (-1.0 if d[p] < 8 else 1.0)
        else:
            c[p, C_COS:C_COS + 256] = 1.0
    c[:, C_HSEL:C_HSEL + 8] = (i[:, None] // 16) == np.arange(8)[None, :]
    c[:, C_REV:C_REV + 128] = (i[:, None] + i[None, :]) == 127
    c[0:16, C_REP:C_REP + 128] = i[:16, None] == (i[None, :] % 16)
    u = np.zeros((33, 1024), np.float32)
    for j in range(2):
        for t in range(512):
            dd = 255 - t
            lim = 256 if j == 0 else 128
            if dd < 0 or dd >= lim:
                u[32, 512 * j + t] = 1.0
            else:
                b = dd if dd < 16 else min(31, 16 + int(math.log(dd / 16) / math.log(8) * 16 + 1e-9))
                u[b, 512 * j + t] = 1.0
    return c, u


def pack_weights(a):
    tiles = plan()
    wall = np.zeros((len(tiles), 128, TW), np.float32)

    def src(name):
        n = name[0]
        if n == "mod":
            return a["mod_w"][name[1], name[2]]
        if n in ("ab", "ab_out", "cd", "cd_out"):
            return a[{"ab": "w_in_ab", "ab_out": "w_out_ab", "cd": "w_in_cd", "cd_out": "w_out_cd"}[n]][0]
        if n in ("wk", "wv"):
            return a["nsa_cmp_" + n][0]
        return a[{"hy": "w_in_2", "hy_out": "w_out_2", "gate": "w_gate_2", "up": "w_up_2", "down": "w_down_2",
                  "ffn_in": "ffn_w_in", "ffn_out": "ffn_w_out"}[n]][name[1]]

    for i, (name, what, arg, _) in enumerate(tiles):
        if what == "T":
            w = src(name).reshape(KC, 128, -1)
            off = 0
            for c in arg:
                m = len(c)
                wall[i, :, off:off + KC * m] = w[:, :, c].transpose(1, 0, 2).reshape(128, KC * m)
                off += KC * m
        elif what == "M":
            w = src(name).reshape(KC, 128, -1)
            wall[i, :, :KC * len(arg)] = w[:, :, arg].transpose(1, 0, 2).reshape(128, -1)
        elif what == "GU":
            j, off = arg
            for c in range(2):
                w = src(name[c]).reshape(KC, 128, -1)
                o = 128 * j + (off if c else 0)
                wall[i, :, 1024 * c:1024 * c + 1024] = w[:, :, o:o + 128].transpose(1, 0, 2).reshape(128, 1024)
        elif what == "DN":
            m, half = arg
            w = src(name).reshape(FC, 128, D)[11 * half:11 * half + 11, :, 128 * m:128 * m + 128]
            wall[i, :, :11 * 128] = w.transpose(1, 0, 2).reshape(128, -1)
        else:
            w = src(name)[16 * arg:16 * arg + 16].transpose(1, 0, 2)
            t = wall[i].reshape(128, 16, 128)
            t[0:64, :, 0:64] = w
            t[64:128, :, 64:128] = w
    return wall


def pack_vectors(a):
    v = np.zeros((128, NV), np.float32)
    col = lambda x: x.reshape(-1, 128).T
    v[:, V_C:V_C + 8] = col(a["c"])
    for l in range(2):
        for s in range(2):
            o = V_MODB + 24 * (2 * l + s)
            v[:, o:o + 24] = col(a["mod_b"][l, s])
            o = V_NORM + 16 * (2 * l + s)
            v[:, o:o + 16] = col(a["norm_w"][l, s])
            o = V_NORM2 + 32 * l + 16 * s
            pre, post = (("mix_pre_norm_2", "mix_post_norm_2"), ("ffn_pre_norm_2", "ffn_post_norm_2"))[s]
            v[:, o:o + 8] = col(a[pre][l])
            v[:, o + 8:o + 16] = col(a[post][l])
        o = V_ONORM + 8 * l
        v[:, o:o + 4] = col(a["attn_out_norm_2"][l])
        v[:, o + 4:o + 8] = col(a["gla_out_norm_2"][l])
        v[:, V_GB + 2 * l:V_GB + 2 * l + 2] = col(a["gla_b_gate_2"][l])
    pe = a["nsa_cmp_pe"][0].T
    v[0:64, V_PE:V_PE + 32] = pe
    v[64:128, V_PE:V_PE + 32] = pe
    v[:, V_EPS] = 1e-6
    v[31:, V_ROW] = 1.0
    return v


def kernel(**inputs):
    import numpy as _np
    import concourse.bacc as _bacc
    from concourse import mybir as _mybir
    from concourse.bass_utils import run_bass_kernel_spmd as _run

    a = {k: _np.asarray(v) for k, v in inputs.items()}
    con, onehot = shape_constants()
    arrays = {
        "wall": pack_weights(a),
        "xin": _np.ascontiguousarray(a["x"][0].T.reshape(KC, 128, S).transpose(1, 0, 2)),
        "vecs": pack_vectors(a),
        "consts": con,
        "onehot": onehot,
        "sinks": _np.ascontiguousarray(a["swa_sinks"][0]),
        "table": _np.ascontiguousarray(a["rel_table"]),
        "gup": _np.ascontiguousarray(a["gla_w_gate_up_2"]),
    }
    nc = _bacc.Bacc("TRN2", target_bir_lowering=False, num_devices=1)
    f = _mybir.dt.float32
    args = [nc.dram_tensor(n, v.shape, f, kind="ExternalInput").ap() for n, v in arrays.items()]
    out = nc.dram_tensor("out_0", (128, KC, S), f, kind="ExternalOutput").ap()
    scratch = nc.dram_tensor("scratch", (16, 512), f).ap()
    build(nc, *args, out, scratch)
    r = _run(nc, [arrays], core_ids=[0])
    got = r.results[0]["out_0"]
    return _np.ascontiguousarray(got.transpose(1, 0, 2).reshape(D, S).T)[None]
```

```python
import math
from contextlib import ExitStack

import numpy as np
import concourse.bass as bass
from concourse import mybir

F = mybir.dt.float32
R = mybir.dt.float32r
U32 = mybir.dt.uint32
ACT = mybir.ActivationFunctionType
ALU = mybir.AluOpType
AX = mybir.AxisListType

S = 256
D = 1024
KC = 8
DFF = 2816
FC = 22
NEG = -1e30
TW = 2048
RAW = 4
SPL = 3
MRING = 2
AHEAD = 3
BIG = 3.0e38

V_C = 0
V_MODB = 8
V_NORM = V_MODB + 96
V_NORM2 = V_NORM + 64
V_ONORM = V_NORM2 + 64
V_GB = V_ONORM + 16
V_PE = V_GB + 4
V_EPS = V_PE + 32
V_ROW = V_EPS + 1
NV = V_ROW + 1

C_ID = 0
C_TRI = 128
C_ONE = 256
C_ROT = 384
C_STRICT = 512
C_DIL = 896
C_COS = 1152
C_SIN = 1408
C_HSEL = 1664
C_REP = 1672
C_REV = 1800
NCONST = 1928

HQ, KVW = 512, 128


def split_heads(base):
    return [np.concatenate([base + 64 * c + np.arange(64), base + 64 * (4 + c) + np.arange(64)])
            for c in range(4)]


def chunks(base, n):
    return [base + 128 * c + np.arange(128) for c in range(n)]


AB = np.cumsum([0, 512, 128, 128, 128, 128, 128, 128, 24, 512, 128, 128]).tolist()
AB_T = (chunks(AB[1], 1) + chunks(AB[2], 1) + chunks(AB[3], 1) + chunks(AB[5], 1)
        + split_heads(AB[0]) + chunks(AB[9], 1) + split_heads(AB[8]))
AB_M = [np.concatenate([AB[4] + np.arange(128), AB[6] + np.arange(128)]),
        np.concatenate([AB[10] + np.arange(128), AB[7] + np.arange(24)])]
CD = np.cumsum([0, 512, 128, 128, 512, 512, 512]).tolist()
CD_T = chunks(CD[1], 1) + split_heads(CD[0]) + chunks(CD[3], 4) + chunks(CD[4], 4)
CD_M = [CD[2] + np.arange(128), CD[5] + np.arange(256), CD[5] + 256 + np.arange(256)]
HY = np.cumsum([0, 512, 512, 512, 256, 256, 512, 512, 16]).tolist()
HY_T = chunks(HY[3], 2) + chunks(HY[4], 2) + chunks(HY[0], 4) + chunks(HY[1], 4) + [HY[7] + np.arange(16)]
HY_M = [HY[s] + 256 * i + np.arange(256) for s in (2, 5, 6) for i in range(2)]


def plan():
    out = []

    def t_tiles(name, cols):
        for i in range(0, len(cols), 2):
            out.append((name, "T", cols[i:i + 2], True))

    def m_tiles(name, cols):
        for c in cols:
            out.append((name, "M", c, True))

    def mods(layer, sub, a, b):
        return [(("mod", layer, sub), "T", chunks(256 * i, 2), False) for i in range(a, b)]

    def ffn(gate, up, down, off):
        for j in range(FC):
            out.append(((gate, up), "GU", (j, off), True))
        for m in range(KC):
            for half in range(2):
                out.append((down, "DN", (m, half), True))

    out += mods(0, 0, 0, 8)
    for layer in range(2):
        if layer == 0:
            t_tiles(("ab",), AB_T)
            m_tiles(("ab",), AB_M)
            for name in ("wk", "wv"):
                for half in range(2):
                    out.append(((name,), "CMP", half, False))
            t_tiles(("ab_out",), chunks(0, 8))
        else:
            t_tiles(("cd",), CD_T)
            m_tiles(("cd",), CD_M)
            t_tiles(("cd_out",), chunks(0, 8))
        ffn(("ffn_in", layer), ("ffn_in", layer), ("ffn_out", layer), DFF)
    for layer in range(2):
        t_tiles(("hy", layer), HY_T)
        m_tiles(("hy", layer), HY_M)
        t_tiles(("hy_out", layer), chunks(0, 8))
        ffn(("gate", layer), ("up", layer), ("down", layer), 0)
    side = mods(0, 0, 8, 12) + mods(0, 1, 0, 12) + mods(1, 0, 0, 12) + mods(1, 1, 0, 12)
    return out, side


def width(tile):
    _, what, arg, _ = tile
    if what == "T":
        return KC * sum(len(c) for c in arg)
    if what == "M":
        return KC * len(arg)
    if what == "DN":
        return 11 * 128
    return TW


class Queue:

    def __init__(self, sem):
        self.sem = sem
        self.count = 0
        self.ops = []
        self.seen = {}

    def wait(self, *toks):
        for t in toks:
            if t is None:
                continue
            if isinstance(t, list):
                self.wait(*t)
                continue
            sem, val = t
            if self.seen.get(sem.name, 0) < val:
                self.seen[sem.name] = val
                self.ops.append(lambda e, sem=sem, val=val: e.wait_ge(sem, val))

    def run(self, f, *toks):
        self.wait(*toks)
        self.ops.append(f)

    def do(self, f, *toks):
        self.wait(*toks)
        self.count += 1
        self.ops.append(lambda e: f(e).then_inc(self.sem, 1))
        return (self.sem, self.count)

    def dma(self, sem, f, *toks):
        self.wait(*toks)
        self.ops.append(lambda e: f(e).then_inc(sem, 16))

    def emit(self, e):
        for f in self.ops:
            f(e)


def build(nc, wall, xin, vecs, consts, onehot, sinks, table, gup, out, scratch):
    TILES, SIDE = plan()
    ctx = ExitStack()
    with ctx:
        names = [0]

        def sb(shape, dt=F, where=ctx):
            names[0] += 1
            return where.enter_context(nc.sbuf_tensor(f"t{names[0]}", shape, dt))

        def sem(name):
            return ctx.enter_context(nc.semaphore(name))

        banks = [ctx.enter_context(nc.psum_tensor(f"bank{i}", [128, 512], F)) for i in range(8)]
        free = [None] * 8

        pe, act, dve, pool, sp = (Queue(sem(f"s_{n}")) for n in ("pe", "act", "dve", "pool", "sp"))

        raw = [sb([128, TW]) for _ in range(RAW)]
        wh = [sb([128, TW], R) for _ in range(SPL)]
        wl = [sb([128, TW], R) for _ in range(SPL)]
        s_raw = [sem(f"s_raw{i}") for i in range(RAW)]
        X = sb([128, KC, S])
        HH = sb([128, KC, S], R)
        HL = sb([128, KC, S], R)
        Y = sb([128, KC, S])
        RS = sb([128, S])
        LN = sb([128, S])
        SQ = [sb([128, S]) for _ in range(2)]
        VEC = sb([128, NV])
        CON = sb([128, NCONST])
        BIAS = sb([128, 16, S])
        A4 = sb([128, 8])
        MOD = sb([128, 24])
        SIDER = [sb([128, TW]) for _ in range(MRING)]
        ACC = [[sb([128, 256]) for _ in range(2)] for _ in range(2)]
        s_side = [sem(f"s_side{i}") for i in range(MRING)]
        G4 = sb([128, 8])
        MB = sb([128, 8])
        HM = sb([128, 128])

        s_in = sem("s_in")
        s_x = sem("s_x")
        s_tab = sem("s_tab")
        s_u = sem("s_u")
        s_b = sem("s_b")
        s_sk = sem("s_sk")
        s_gu = sem("s_gu")
        s_out = sem("s_out")

        ident = CON[:, C_ID:C_ID + 128]
        tri = CON[:, C_TRI:C_TRI + 128]
        ones = CON[:, C_ONE:C_ONE + 128]
        rot = CON[:, C_ROT:C_ROT + 128]
        strict = CON[:, C_STRICT:C_STRICT + 384]
        dil = CON[:, C_DIL:C_DIL + 256]
        cosT = CON[:, C_COS:C_COS + 256]
        sinT = CON[:, C_SIN:C_SIN + 256]
        rep16 = CON[0:16, C_REP:C_REP + 128]
        hsel = CON[:, C_HSEL:C_HSEL + 8]
        eps = VEC[:, V_EPS:V_EPS + 1]

        raw_free = {}
        spl_free = {}
        state = {"dma": 0, "split": 0, "use": 0}
        split_tok = {}
        split_no = {}
        k = 0
        for i, t in enumerate(TILES):
            if t[3]:
                split_no[i] = k
                k += 1

        def raw_ready(i):
            return (s_raw[i % RAW], 16 * (i // RAW + 1))

        def pump():
            while state["dma"] < len(TILES):
                i = state["dma"]
                if i >= RAW and i - RAW not in raw_free:
                    return
                n = width(TILES[i])
                toks = raw_free[i - RAW] if i >= RAW else None
                sp.dma(s_raw[i % RAW], lambda e, i=i, n=n: e.dma_start(raw[i % RAW][:, 0:n], wall[i, :, 0:n]), toks)
                state["dma"] += 1

        def splits(upto):
            while state["split"] <= min(upto, len(TILES) - 1):
                i = state["split"]
                state["split"] += 1
                if i not in split_no:
                    continue
                n = width(TILES[i])
                sl = split_no[i] % SPL
                r, h, l = raw[i % RAW], wh[sl], wl[sl]
                fr = spl_free.get(split_no[i] - SPL)
                th = act.do(lambda e, r=r, h=h, n=n: e.activation(h[:, 0:n], r[:, 0:n], ACT.Copy),
                            raw_ready(i), fr)
                tl = dve.do(lambda e, r=r, h=h, l=l, n=n: e.tensor_tensor(
                    l[:, 0:n], r[:, 0:n], h[:, 0:n].bitcast(F), ALU.subtract), raw_ready(i), th, fr)
                split_tok[i] = [th, tl]
                raw_free[i] = [tl]
                pump()

        def next_tile(kind):
            i = state["use"]
            state["use"] += 1
            assert TILES[i][1] == kind, (i, TILES[i], kind)
            j = i
            while j < len(TILES) and j < i + AHEAD and (j not in split_no or j in split_tok or True):
                if j in split_no and split_no[j] - SPL >= 0 and split_no[j] - SPL not in spl_free:
                    break
                if j > i and state["dma"] <= j:
                    break
                splits(j)
                j += 1
            return i

        def done_tile(i, tok):
            if i in split_no:
                spl_free[split_no[i]] = tok
            else:
                raw_free[i] = tok
            pump()

        def wt(i):
            sl = split_no[i] % SPL
            return wh[sl], wl[sl]

        def mm3(out, lh, ll, rh, rl, first, last, sig=False):
            pe.run(lambda e: e.matmul(out, lh, rh, start=first, stop=False, skip_group_check=True))
            pe.run(lambda e: e.matmul(out, lh, rl, start=False, stop=False, skip_group_check=True))
            f = lambda e: e.matmul(out, ll, rh, start=False, stop=last, skip_group_check=True)
            if last or sig:
                return pe.do(f)
            pe.run(f)

        def mm(out, l, r, start=True, stop=True, toks=(), sig=True):
            f = lambda e: e.matmul(out, l, r, start=start, stop=stop, skip_group_check=True)
            pe.wait(*toks)
            return pe.do(f) if sig else pe.run(f)

        pump()

        act.dma(s_in, lambda e: e.dma_start(VEC[:, :], vecs))
        act.dma(s_in, lambda e: e.dma_start(CON[:, :], consts))
        act.dma(s_x, lambda e: e.dma_start(X[:, :, :], xin))
        small = (s_in, 32)
        x_in = (s_x, 16)

        with ExitStack() as ph:
            TB = sb([33, 16], where=ph)
            OH = sb([33, 1024], where=ph)
            UT = sb([8, 2, 512], where=ph)
            t0 = dve.do(lambda e: e.memset(TB[:, :], NEG))
            act.dma(s_tab, lambda e: e.dma_start(TB[0:32, :], table), t0)
            act.dma(s_tab, lambda e: e.dma_start(OH[:, :], onehot))
            for j in range(2):
                mm(banks[j][0:8, 0:512], TB[:, 8 * j:8 * j + 8], OH[:, 512 * j:512 * j + 512],
                   toks=[(s_tab, 32), t0])
            tp = (pe.sem, pe.count)
            tu = [dve.do(lambda e, j=j: e.tensor_copy(UT[:, j, :], banks[j][0:8, 0:512]), tp) for j in range(2)]
            for j in range(2):
                act.dma(s_u, lambda e, j=j: e.dma_start(scratch[8 * j:8 * j + 8, :], UT[:, j, :]), tu[j])
            BR = sb([128, 16, S], where=ph)
            toep = bass.AP(tensor=scratch.tensor, offset=0, ap=[[1, 128], [512, 16], [1, 256]])
            act.dma(s_b, lambda e: e.dma_start(BR[:, :, :], toep), (s_u, 32))
            rev = CON[:, C_REV:C_REV + 128]
            bias_ready = []
            for j in range(8):
                b = j % 4
                pe.wait(tu, free[b], small, (s_b, 16))
                t = pe.do(lambda e, j=j, b=b: e.matmul(banks[b][:, :], rev, BR[:, 2 * j:2 * j + 2, :], start=True,
                                                       stop=True))
                t = dve.do(lambda e, j=j, b=b: e.tensor_copy(
                    BIAS[:, 2 * j:2 * j + 2, :].rearrange("p a b -> p (a b)"), banks[b][:, :]), t)
                free[b] = [t]
            bias_ready = [t]

        acc_free = [None, None]
        accn = [0]
        mod_done = {}
        pending = []
        side = {"dma": 0, "use": 0}
        side_free = {}

        def side_pump():
            while side["dma"] < len(SIDE):
                i = side["dma"]
                if i >= MRING and i - MRING not in side_free:
                    return
                toks = side_free[i - MRING] if i >= MRING else None
                sp.dma(s_side[i % MRING], lambda e, i=i: e.dma_start(SIDER[i % MRING][:, :], wall[len(TILES) + i]),
                       toks)
                side["dma"] += 1

        def mod_tile(buf, ready, block):
            w = buf[:, :].rearrange("p (c k m) -> p c k m", c=2, k=KC)
            j = accn[0] % 2
            accn[0] += 1
            t = [None, None]
            for kc in range(KC):
                a = ACC[j][kc % 2]
                av = a[:, :].rearrange("p (c m) -> p c m", c=2)
                cc = VEC[:, V_C + kc:V_C + kc + 1]
                if kc < 2:
                    t[kc] = dve.do(lambda e, av=av, kc=kc, cc=cc: e.tensor_scalar(
                        av, w[:, :, kc, :], cc, None, ALU.mult), ready, small, acc_free[j])
                else:
                    t[kc % 2] = dve.do(lambda e, av=av, kc=kc, cc=cc: e.scalar_tensor_tensor(
                        out=av, in0=w[:, :, kc, :], scalar=cc, in1=av, op0=ALU.mult, op1=ALU.add), t[kc % 2])
            col = 24 * (block // 12 % 2) + 2 * (block % 12)

            def over_partitions():
                pe.wait(free[7], t[0], t[1], small)
                for c in range(2):
                    pe.run(lambda e, c=c: e.matmul(
                        banks[7][:, col + c:col + c + 1], ACC[j][0][:, 128 * c:128 * c + 128], ones[:, 0:1],
                        start=True, stop=False, skip_group_check=True))
                    tok = pe.do(lambda e, c=c: e.matmul(
                        banks[7][:, col + c:col + c + 1], ACC[j][1][:, 128 * c:128 * c + 128], ones[:, 0:1],
                        start=False, stop=True, skip_group_check=True))
                acc_free[j] = tok
                mod_done[block] = mod_done["last"] = tok

            pending.append(over_partitions)
            if len(pending) > 1:
                pending.pop(0)()
            return [t[0], t[1]]

        def background(n=1):
            for _ in range(n):
                i = side["use"]
                if i >= len(SIDE):
                    return
                side["use"] += 1
                side_pump()
                side_free[i] = mod_tile(SIDER[i % MRING], (s_side[i % MRING], 16 * (i // MRING + 1)), 8 + i)
                side_pump()

        def need(block):
            while 8 + side["use"] <= block:
                background()
            while pending:
                pending.pop(0)()
            return mod_done["last"]

        def modulation(st):
            tok = need(12 * st + 7)
            o = V_MODB + 24 * st
            n = V_NORM + 16 * st
            b = 24 * (st % 2)
            t1 = dve.do(lambda e: e.tensor_tensor(MOD[:, 0:16], banks[7][:, b:b + 16], VEC[:, o:o + 16], ALU.add),
                        tok, small, mod_tok[0])
            free[7] = [t1]
            return [dve.do(lambda e: e.scalar_tensor_tensor(
                out=A4[:, :], in0=MOD[:, 8:16], scalar=1.0, in1=VEC[:, n:n + 8], op0=ALU.add, op1=ALU.mult), t1)]

        def gating(st):
            tok = need(12 * st + 11)
            o = V_MODB + 24 * st + 16
            n = V_NORM + 16 * st + 8
            b = 24 * (st % 2) + 16
            t1 = dve.do(lambda e: e.tensor_tensor(MOD[:, 16:24], banks[7][:, b:b + 8], VEC[:, o:o + 8], ALU.add), tok)
            free[7] = [t1]
            return [dve.do(lambda e: e.tensor_tensor(G4[:, :], MOD[:, 16:24], VEC[:, n:n + 8], ALU.mult), t1)]

        mod_tok = [None]

        sq_free = [None, None]
        sqn = [0]

        def stat_start(src, tok):
            j = sqn[0] % 2
            sqn[0] += 1
            t = act.do(lambda e: e.activation(SQ[j][:, :], src, ACT.Square), tok, sq_free[j])
            return j, t

        def stat_add(c, jt):
            j, t = jt
            if c == 0:
                pe.wait(free[6])
            tok = mm(banks[6][:, 0:S], ones, SQ[j][:, :], start=(c == 0), stop=(c == KC - 1), toks=[t, small])
            sq_free[j] = tok
            return tok

        rs_free = [None]

        def rstd(tok):
            t = act.do(lambda e: e.activation(LN[:, :], banks[6][:, 0:S], ACT.Ln, scale=1.0 / D, bias=eps),
                       tok, small)
            free[6] = t
            return act.do(lambda e: e.activation(RS[:, :], LN[:, :], ACT.Exp, scale=-0.5), t, rs_free[0])

        h_free = [None]

        def make_h(stat, a_of, shift_of, mtok):
            r = rstd(stat)
            toks = []
            for c in range(KC):
                t = dve.do(lambda e, c=c: e.scalar_tensor_tensor(
                    out=Y[:, c, :], in0=X[:, c, :], scalar=a_of(c), in1=RS[:, :], op0=ALU.mult, op1=ALU.mult),
                    r, mtok)
                if shift_of is None:
                    th = act.do(lambda e, c=c: e.activation(HH[:, c, :], Y[:, c, :], ACT.Copy), t, h_free[0])
                    f = lambda e, c=c: e.tensor_tensor(HL[:, c, :], Y[:, c, :], HH[:, c, :].bitcast(F), ALU.subtract)
                else:
                    th = act.do(lambda e, c=c: e.activation(
                        HH[:, c, :], Y[:, c, :], ACT.Identity, bias=shift_of(c)), t, h_free[0])
                    f = lambda e, c=c: e.scalar_tensor_tensor(
                        out=HL[:, c, :], in0=Y[:, c, :], scalar=shift_of(c), in1=HH[:, c, :].bitcast(F),
                        op0=ALU.add, op1=ALU.subtract)
                toks.append([th])
                if c:
                    toks[c - 1].append(dve.do(fl, toks[c - 1]))
                fl = f
            toks[-1].append(dve.do(fl, th))
            rs_free[0] = t
            return toks

        def x_stats(toks):
            for c in range(KC):
                st = stat_add(c, stat_start(X[:, c, :], toks[c]))
            return st

        def residual(stat, g_of, mtok, ytoks):
            r = rstd(stat)
            toks = []
            for c in range(KC + 1):
                if c < KC:
                    t = dve.do(lambda e, c=c: e.scalar_tensor_tensor(
                        out=Y[:, c, :], in0=Y[:, c, :], scalar=g_of(c), in1=RS[:, :], op0=ALU.mult, op1=ALU.mult),
                        r, mtok, ytoks[c])
                    rs_free[0] = t
                if c:
                    toks.append(dve.do(lambda e, c=c - 1: e.tensor_tensor(
                        X[:, c, :], X[:, c, :], Y[:, c, :], ALU.add), tp))
                tp = t
            return toks

        def blocks2(parts, h, l, htoks):
            order = [(p, kc) for p in range(len(parts)) for kc in range(KC)]
            if htoks is not None:
                order = [(p, kc) for kc in range(KC) for p in range(len(parts))]
            for p, kc in order:
                m, off, o = parts[p]
                if htoks is not None:
                    pe.wait(htoks[kc])
                q = slice(off + kc * m, off + kc * m + m)
                first = kc == 0 and (htoks is None or p == 0)
                tok = mm3(o, h[:, q], l[:, q], HH[:, kc, :], HL[:, kc, :], first, kc == KC - 1)
            return tok

        def take_turns(handle, toks):
            t = toks[-1][-1]
            for x in toks:
                t = handle(*x[:-1], [t, toks[-1][-1]])
            return [t]

        def proj_T(cols, htoks, handle, ring):
            n = 0
            for t in range(0, len(cols), 2):
                i = next_tile("T")
                h, l = wt(i)
                b = ring[(t // 2) % len(ring)]
                off = 0
                toks = []
                pe.wait(free[b], split_tok[i])
                parts = []
                for c in cols[t:t + 2]:
                    parts.append((n, len(c), off, banks[b][0:len(c), 256 * (n % 2):256 * (n % 2) + 256]))
                    off += KC * len(c)
                    n += 1
                tok = blocks2([(m, off, o) for _, m, off, o in parts], h, l, htoks if t == 0 else None)
                toks = [(nn, o, tok) for nn, _, _, o in parts]
                done_tile(i, tok)
                free[b] = take_turns(handle, toks)
                background()
            h_free[0] = tok

        def proj_M(cols, handle, ring):
            for n, c in enumerate(cols):
                i = next_tile("M")
                h, l = wt(i)
                m = len(c)
                b = ring[n % len(ring)]
                pe.wait(free[b], split_tok[i])
                toks = []
                for qt in range(2):
                    o = banks[b][:, 256 * qt:256 * qt + m]
                    for kc in range(KC):
                        q = slice(kc * m, kc * m + m)
                        s = slice(128 * qt, 128 * qt + 128)
                        tok = mm3(o, HH[:, kc, s], HL[:, kc, s], h[:, q], l[:, q], kc == 0, kc == KC - 1)
                    toks.append((n, qt, o, tok))
                done_tile(i, tok)
                free[b] = take_turns(handle, toks)
                background()
            h_free[0] = tok

        def out_proj():
            ytoks, pend = [], None
            for t in range(4):
                i = next_tile("T")
                h, l = wt(i)
                b = t % 4
                fr = []
                pe.wait(free[b], split_tok[i])
                outs = [(2 * t + c, banks[b][:, 256 * c:256 * c + 256]) for c in range(2)]
                tok = blocks2([(128, 1024 * c, outs[c][1]) for c in range(2)], h, l, ot_tok if t == 0 else None)
                done_tile(i, tok)
                if pend is not None:
                    for m, jt in pend:
                        stat_add(m, jt)
                pend = []
                for m, o in outs:
                    ty = dve.do(lambda e, m=m, o=o: e.tensor_copy(Y[:, m, :], o), tok)
                    ytoks.append(ty)
                    pend.append((m, stat_start(Y[:, m, :], ty)))
                    fr.append(ty)
                free[b] = fr
            for m, jt in pend:
                st = stat_add(m, jt)
            h_free[0] = tok
            return ytoks, st

        def ffn(htoks):
            with ExitStack() as ph:
                AH = sb([128, FC, S], R, ph)
                AL = sb([128, FC, S], R, ph)
                SG = [Y[:, 4 + k, :] for k in range(2)]
                PV = [Y[:, 6 + k, :] for k in range(2)]
                sg_free, pv_free = [None] * 2, [None] * 2
                atoks = []
                for j in range(FC):
                    i = next_tile("GU")
                    h, l = wt(i)
                    b = j % 3
                    pe.wait(free[b], split_tok[i])
                    tok = blocks2([(128, 1024 * c, banks[b][:, 256 * c:256 * c + 256]) for c in range(2)], h, l,
                                  htoks if j == 0 else None)
                    done_tile(i, tok)
                    if j % 3 == 1:
                        background()
                    s, v, bb = SG[j % 2], PV[j % 2], banks[b]
                    t1 = act.do(lambda e, s=s, bb=bb: e.activation(s, bb[:, 0:256], ACT.Silu),
                                tok, sg_free[j % 2])
                    t2 = dve.do(lambda e, s=s, v=v, bb=bb: e.tensor_tensor(
                        v, s, bb[:, 256:512], ALU.mult), t1, pv_free[j % 2])
                    th = act.do(lambda e, v=v, j=j: e.activation(AH[:, j, :], v, ACT.Copy), t2)
                    tl = dve.do(lambda e, v=v, j=j: e.tensor_tensor(
                        AL[:, j, :], v, AH[:, j, :].bitcast(F), ALU.subtract), th)
                    sg_free[j % 2], pv_free[j % 2] = t2, tl
                    free[b] = [t2]
                    atoks.append([th, tl])
                h_free[0] = tok
                ytoks, pend = [], None
                for m in range(KC):
                    b = 3 + m % 3
                    o = banks[b][:, 0:256]
                    pe.wait(free[b])
                    for half in range(2):
                        i = next_tile("DN")
                        h, l = wt(i)
                        pe.wait(split_tok[i])
                        for kk in range(11):
                            kc = 11 * half + kk
                            if m == 0:
                                pe.wait(atoks[kc])
                            q = slice(kk * 128, kk * 128 + 128)
                            last = kk == 10 and half == 1
                            tok = mm3(o, h[:, q], l[:, q], AH[:, kc, :], AL[:, kc, :], kc == 0, last,
                                      sig=kk == 10)
                        done_tile(i, tok)
                    ty = dve.do(lambda e, m=m, o=o: e.tensor_copy(Y[:, m, :], o), tok)
                    ytoks.append(ty)
                    jt = stat_start(Y[:, m, :], ty)
                    free[b] = [ty]
                    if m % 2:
                        background()
                    if pend is not None:
                        stat_add(m - 1, pend)
                    pend = jt
                return ytoks, stat_add(KC - 1, pend)

        ot_tok = [None] * KC

        def transposed(o_sb, o_toks, scale_of, ring=(0, 1)):
            for c in range(KC):
                b = ring[c % len(ring)]
                pe.wait(free[b])
                for qt in range(2):
                    tok = pe.do(lambda e, qt=qt, b=b, c=c: e.transpose(
                        banks[b][:, 128 * qt:128 * qt + 128], o_sb[:, qt, 128 * c:128 * c + 128], ident),
                        o_toks[qt][c // 4], small)
                src = banks[b][:, 0:S]
                if scale_of is None:
                    th = act.do(lambda e, c=c, src=src: e.activation(HH[:, c, :], src, ACT.Copy), tok, h_free[0])
                    tl = dve.do(lambda e, c=c, src=src: e.tensor_tensor(
                        HL[:, c, :], src, HH[:, c, :].bitcast(F), ALU.subtract), th)
                else:
                    w = scale_of(c)
                    th = act.do(lambda e, c=c, src=src, w=w: e.activation(
                        HH[:, c, :], src, ACT.Copy, scale=w), tok, h_free[0])
                    tl = dve.do(lambda e, c=c, src=src, w=w: e.scalar_tensor_tensor(
                        out=HL[:, c, :], in0=src, scalar=w, in1=HH[:, c, :].bitcast(F),
                        op0=ALU.mult, op1=ALU.subtract), th)
                free[b] = [th, tl]
                ot_tok[c] = [th, tl]

        def softmax_heads(insts, P):
            n = len(insts)
            fr_s, fr_p, fr_n, fr_t = P["fr_s"], P["fr_p"], P["fr_n"], P["fr_t"]

            def score(i):
                a = insts[i]
                g = P["n"] + i
                K = 128 * (a["qt"] + 1)
                b = 4 + g % 2
                ps = banks[b][:, 0:K]
                pe.wait(fr_s[g % 2], free[b], a["toks"])
                t = pe.do(lambda e: e.matmul(ps, a["q"][:, 128 * a["qt"]:128 * a["qt"] + 128], a["k"][:, 0:K],
                                             start=True, stop=True, skip_group_check=True))
                s, p = P["s"][g % 3], P["p"][g % 4]
                nm = P["nm"][:, g % 8:g % 8 + 1]
                t = dve.do(lambda e: e.tensor_tensor_reduce(
                    out=s[:, 0:K], in0=ps, in1=a["bias"], scale=-1.0, scalar=a["start"], op0=ALU.add, op1=ALU.min,
                    accum_out=nm), t, fr_n[g % 3], bias_ready, a.get("nmwait"))
                fr_s[g % 2] = t
                if a.get("keep") is not None:
                    t2 = dve.do(lambda e: e.tensor_copy(a["keep"], nm), t)
                    a["kept"].append(t2)
                    tx = [t, t2]
                else:
                    tx = t
                t = act.do(lambda e: e.activation(p[:, 0:K], s[:, 0:K], ACT.Exp, scale=-1.0, bias=nm,
                                                  accum_out=a["sum"]), t, fr_p[g % 4])
                fr_n[g % 3] = t
                a["exp"] = t
                a["sums"].append(t)

            def turn(i):
                a = insts[i]
                g = P["n"] + i
                K = 128 * (a["qt"] + 1)
                p, pT = P["p"][g % 4], P["pT"][g % 3]
                b = (6, 2)[g % 2]
                pe.wait(fr_t[g % 2], free[b], a["exp"])
                for kt in range(a["qt"] + 1):
                    o = banks[b][:, 128 * kt:128 * kt + 128]
                    t = pe.do(lambda e, kt=kt, o=o: e.transpose(o, p[:, 128 * kt:128 * kt + 128], ident))
                fr_p[g % 4] = t
                src = banks[b][:, 0:K]
                if g % 2:
                    t = act.do(lambda e: e.activation(pT[:, 0:K], src, ACT.Copy), t, P["fr_pt"][g % 3])
                else:
                    t = dve.do(lambda e: e.tensor_copy(pT[:, 0:K], src), t, P["fr_pt"][g % 3])
                fr_t[g % 2] = t
                a["turned"] = t

            def value(i):
                a = insts[i]
                g = P["n"] + i
                pT = P["pT"][g % 3]
                pe.wait(a["turned"], free[a["ob"]], a["vtoks"])
                for kt in range(a["qt"] + 1):
                    t = pe.do(lambda e, kt=kt: e.matmul(
                        a["out"], pT[:, 128 * kt:128 * kt + 128], a["v"][kt], start=(kt == 0),
                        stop=(kt == a["qt"]), skip_group_check=True))
                P["fr_pt"][g % 3] = t
                if a.get("after"):
                    a["after"](t)

            for i in range(n + 4):
                if i < n:
                    score(i)
                if 2 <= i < n + 2:
                    turn(i - 2)
                if i >= 4:
                    value(i - 4)
            P["n"] += n

        def att_pool(ph):
            P = {"s": [sb([128, S], F, ph) for _ in range(3)], "p": [sb([128, S], F, ph) for _ in range(4)],
                 "pT": [sb([128, S], F, ph) for _ in range(3)], "nm": sb([128, 8], F, ph),
                 "fr_s": [None] * 2, "fr_p": [None] * 4, "fr_n": [None] * 3, "fr_t": [None] * 2,
                 "fr_pt": [None] * 3, "n": 0}
            return P

        def heads_list(P, qt, Q, K, V, bias, ob, sums, sumtoks, qtoks, vtoks, after, grouped=True, sink=None):
            out = []
            for h in range(8):
                if grouped:
                    g = h // 4
                    q, kk = Q[64 * g:64 * g + 64, h % 4, :], K[64 * g:64 * g + 64, :]
                    v = [V[:, kt, 64 * g:64 * g + 64] for kt in range(2)]
                else:
                    r = 64 * (h % 2)
                    q, kk = Q[r:r + 64, h // 2, :], K[r:r + 64, h // 2, :]
                    v = [V[:, kt, 64 * h:64 * h + 64] for kt in range(2)]
                a = dict(q=q, k=kk, v=v, qt=qt, bias=bias(h)[:, 0:256] if qt else bias(h)[:, 128:256],
                         start=BIG, ob=ob, out=banks[ob][:, 64 * h:64 * h + 64], sum=sums[:, h:h + 1],
                         sums=sumtoks, toks=qtoks, vtoks=vtoks)
                if sink is not None:
                    a["start"] = sink["neg"][:, h:h + 1]
                    a["keep"] = sink["nm"][:, h:h + 1]
                    a["kept"] = sink["toks"]
                if h == 7:
                    a["after"] = after
                out.append(a)
            return out

        def bc(ap, n):
            return ap.unsqueeze(2).to_broadcast([ap.shape[0], ap.shape[1], n])

        def mixer_ab(htoks):
            with ExitStack() as ph:
                KVT = sb([128, 4, S], F, ph)
                QA = sb([128, 4, S], F, ph)
                KB = sb([128, S], F, ph)
                QB = sb([128, 4, S], F, ph)
                VM = sb([128, 2, 408], F, ph)
                CA = sb([128, 2, 2, 272], F, ph)
                KCT = sb([128, 16], F, ph)
                VBD = sb([128, 512], F, ph)
                BC = sb([128, 2, 8, 16], F, ph)
                SC = sb([128, 8, 16], F, ph)
                PC = sb([128, 8, 16], F, ph)
                PCT = sb([128, 128], F, ph)
                O = Y[:, :, :].rearrange("p c s -> p (c s)").rearrange("p (q d) -> p q d", q=2)
                OT = sb([128, 512], F, ph)
                OT2 = sb([128, 512], F, ph)
                GT = sb([128, 2, 24], F, ph)
                NS = sb([128, 8], F, ph)
                SM = sb([128, 64], F, ph)
                P = att_pool(ph)
                act.dma(s_sk, lambda e: e.dma_start(SM[:, 0:8], sinks.partition_broadcast(128)))
                kvt, qa, qb = [], [], []

                def take(n, o, tok):
                    if n < 4:
                        t = dve.do(lambda e: e.tensor_copy(KVT[:, n, :], o), tok)
                        kvt.append(t)
                    elif n < 8:
                        t = act.do(lambda e: e.activation(QA[:, n - 4, :], o, ACT.Copy, scale=0.125), tok)
                        qa.append(t)
                    elif n == 8:
                        t = dve.do(lambda e: e.tensor_copy(KB[:, :], o), tok)
                        qb.append(t)
                    else:
                        t = act.do(lambda e: e.activation(QB[:, n - 9, :], o, ACT.Copy, scale=0.125), tok)
                        qb.append(t)
                    return t

                proj_T(AB_T, htoks, take, (0, 1, 2, 3))
                vm = []

                def take_m(n, qt, o, tok):
                    m = 256 if n == 0 else 152
                    t = dve.do(lambda e: e.tensor_copy(VM[:, qt, 256 * n:256 * n + m], o), tok)
                    vm.append(t)
                    return t

                proj_M(AB_M, take_m, (0, 1))

                tz = dve.do(lambda e: e.memset(CA[:, :, :, 256:272], 0.0))
                cat = []
                for kv in range(2):
                    for v in range(2):
                        cat.append(dve.do(lambda e, kv=kv, v=v: e.tensor_tensor(
                            CA[:, kv, v, 0:256].rearrange("p (n l) -> p n l", l=16),
                            KVT[:, kv, :].rearrange("p (n l) -> p n l", l=16),
                            VEC[:, V_PE + 16 * v:V_PE + 16 * v + 16].unsqueeze(1).to_broadcast([128, 16, 16]),
                            ALU.add), kvt, small))
                pe.wait(free[2], free[3], cat, tz)
                for kv in range(2):
                    for half in range(2):
                        i = next_tile("CMP")
                        w = raw[i % RAW][:, :].rearrange("p (l m) -> p l m", l=16)
                        pe.wait(raw_ready(i))
                        for l in range(16):
                            c0 = 16 * half + l
                            src = CA[:, kv, half, c0:c0 + 241:16]
                            first, last = (half == 0 and l == 0), (half == 1 and l == 15)
                            if kv == 0:
                                f = lambda e, w=w, l=l, src=src, a=first, z=last: e.matmul(
                                    banks[2][:, 0:16], w[:, l, :], src, start=a, stop=z, skip_group_check=True)
                            else:
                                f = lambda e, w=w, l=l, src=src, a=first, z=last: e.matmul(
                                    banks[3][0:16, 0:128], src, w[:, l, :], start=a, stop=z, skip_group_check=True)
                            tok = pe.do(f) if l == 15 else pe.run(f)
                        done_tile(i, tok)
                    if kv == 0:
                        tk = dve.do(lambda e: e.tensor_copy(KCT[:, :], banks[2][:, 0:16]), tok)
                tv = dve.do(lambda e: e.tensor_copy(PCT[0:16, :], banks[3][0:16, 0:128]), tok)
                tok = mm(banks[3][:, 0:128], rep16, PCT[0:16, :], toks=[tv, small])
                tv = dve.do(lambda e: e.tensor_tensor(
                    VBD[:, :].rearrange("p (g r e) -> p g r e", g=2, r=4),
                    banks[3][:, 0:128].rearrange("p (g e) -> p g e", g=2).unsqueeze(2).to_broadcast([128, 2, 4, 64]),
                    hsel.rearrange("p (g r) -> p g r", g=2).unsqueeze(3).to_broadcast([128, 2, 4, 64]),
                    ALU.mult), tok, small)
                free[2], free[3] = [tk], [tv]

                tg = []
                for qt in range(2):
                    t = act.do(lambda e, qt=qt: e.activation(GT[:, qt, :], VM[:, qt, 384:408], ACT.Exp, scale=-1.0), vm)
                    t = dve.do(lambda e, qt=qt: e.tensor_scalar(GT[:, qt, :], GT[:, qt, :], 1.0, None, ALU.add), t)
                    tg.append(dve.do(lambda e, qt=qt: e.reciprocal(GT[:, qt, :], GT[:, qt, :]), t))
                t = dve.do(lambda e: e.memset(BC[:, :, :, :], NEG))
                t1 = dve.do(lambda e: e.tensor_copy(BC[:, 0, :, 0:7], BIAS[:, 0:8, 159:256:16]), t, bias_ready)
                t2 = dve.do(lambda e: e.tensor_copy(BC[:, 1, :, 0:15], BIAS[:, 0:8, 31:256:16]), t)
                tb = [t1, t2]
                tns = dve.do(lambda e: e.tensor_scalar(NS[:, :], SM[:, 0:8], -1.0, None, ALU.mult), (s_sk, 16))

                o_toks = [[None, None], [None, None]]
                prev = {"pc": tv}
                for qt in range(2):
                    mx, sm, rc = SM[:, 8:16], SM[:, 16:24], SM[:, 24:32]
                    pe.wait(free[0], free[3], qa, tk)
                    for h in range(8):
                        g = h // 4
                        tok = pe.do(lambda e, h=h, g=g, qt=qt: e.matmul(
                            banks[3 * g][:, 16 * h:16 * h + 16],
                            QA[64 * g:64 * g + 64, h % 4, 128 * qt:128 * qt + 128], KCT[64 * g:64 * g + 64, :],
                            start=True, stop=True, skip_group_check=True))
                    for g in range(2):
                        t = dve.do(lambda e, qt=qt, g=g: e.tensor_tensor(
                            SC[:, 4 * g:4 * g + 4, :],
                            banks[3 * g][:, 64 * g:64 * g + 64].rearrange("p (h n) -> p h n", h=4),
                            BC[:, qt, 4 * g:4 * g + 4, :], ALU.add), tok, tb, prev["pc"])
                        free[3 * g] = [t]
                    t = dve.do(lambda e: e.tensor_reduce(mx, SC[:, :, :], AX.X, ALU.max), t)
                    t = dve.do(lambda e: e.tensor_tensor(SC[:, :, :], SC[:, :, :], bc(mx, 16), ALU.subtract), t)
                    t = act.do(lambda e: e.activation(PC[:, :, :], SC[:, :, :], ACT.Exp), t, prev["pc"])
                    te = t
                    t = dve.do(lambda e: e.tensor_reduce(sm, PC[:, :, :], AX.X, ALU.add), t)
                    t = dve.do(lambda e: e.reciprocal(rc, sm), t)
                    t = dve.do(lambda e, qt=qt: e.tensor_tensor(rc, rc, GT[:, qt, 0:24:3], ALU.mult), t, tg)
                    if qt == 0:
                        t = dve.do(lambda e: e.tensor_scalar(rc, rc, VEC[:, V_ROW:V_ROW + 1], None, ALU.mult), t)
                    trc = t
                    pe.wait(free[0])
                    tok = pe.do(lambda e: e.transpose(banks[0][:, 0:128], PC[:, :, :].rearrange("p h n -> p (h n)"),
                                                      ident), te)
                    t = dve.do(lambda e: e.tensor_copy(PCT[:, :], banks[0][:, 0:128]), tok, prev["pc"])
                    free[0] = [t]
                    pe.wait(free[1])
                    tok = mm(banks[1][:, 0:512], PCT[:, :], VBD[:, :], toks=[t, tv])
                    prev["pc"] = [tok, trc]
                    acc = O[:, qt, 0:512].rearrange("p (h e) -> p h e", h=8)
                    t = dve.do(lambda e, acc=acc: e.tensor_tensor(
                        acc, banks[1][:, 0:512].rearrange("p (h e) -> p h e", h=8), bc(rc, 64), ALU.mult),
                        tok, trc)
                    free[1] = [t]
                    last = [t]
                    lst = []
                    for w, (kc, vo, bank) in enumerate(((2, 0, 0), (3, 128, 1))):
                        sums = SM[:, 32 + 8 * w:40 + 8 * w]
                        stoks = []

                        def after(tok, w=w, bank=bank, sums=sums, stoks=stoks, qt=qt, acc=acc):
                            t = dve.do(lambda e: e.reciprocal(sums, sums), stoks)
                            t = dve.do(lambda e: e.tensor_tensor(sums, sums, GT[:, qt, 1 + w:24:3], ALU.mult), t, tg)
                            tmp = OT if w == 0 else OT2
                            t = dve.do(lambda e: e.tensor_tensor(
                                tmp[:, :].rearrange("p (h e) -> p h e", h=8),
                                banks[bank][:, :].rearrange("p (h e) -> p h e", h=8), bc(sums, 64), ALU.mult), t, tok)
                            free[bank] = [t]
                            t = dve.do(lambda e: e.tensor_tensor(
                                acc, acc, tmp[:, :].rearrange("p (h e) -> p h e", h=8), ALU.add), t, last[0])
                            last[0] = t
                            if w == 1:
                                o_toks[qt][0] = t

                        lst += heads_list(P, qt, QA, KVT[:, kc, :], VM[:, :, vo:vo + 128], lambda h: BIAS[:, h, :],
                                          bank, sums, stoks, qa + kvt, vm, after)
                    sums, es, nms = SM[:, 48:56], SM[:, 56:64], MB[:, 0:8]
                    stoks, keeps = [], []

                    def after_b(tok, sums=sums, es=es, nms=nms, stoks=stoks, keeps=keeps, qt=qt):
                        t = dve.do(lambda e: e.tensor_tensor(es, nms, NS[:, :], ALU.subtract), keeps, tns)
                        t = act.do(lambda e: e.activation(es, es, ACT.Exp), t)
                        t = dve.do(lambda e: e.tensor_tensor(sums, sums, es, ALU.add), t, stoks)
                        t = dve.do(lambda e: e.reciprocal(sums, sums), t)
                        t = dve.do(lambda e: e.tensor_tensor(
                            O[:, qt, 512:1024].rearrange("p (h e) -> p h e", h=8),
                            banks[3][:, :].rearrange("p (h e) -> p h e", h=8), bc(sums, 64), ALU.mult), t, tok)
                        free[3] = [t]
                        o_toks[qt][1] = t

                    lst += heads_list(P, qt, QB, KB[:, :], VM[:, :, 256:384], lambda h: BIAS[:, 8 + h, :], 3,
                                      sums, stoks, qb, vm, after_b, sink={"neg": NS, "nm": nms, "toks": keeps})
                    for a in lst[16:24]:
                        a["nmwait"] = tns
                    softmax_heads(lst, P)
                release(P)
                transposed(O, o_toks, None)
                return out_proj()

        def release(P):
            free[4] = free[5] = [t for t in P["fr_s"] if t]
            free[6] = free[2] = [t for t in P["fr_t"] if t]

        def plain_after(O, qt, half, bank, sums, stoks, o_toks, done=None):
            def after(tok):
                t = dve.do(lambda e: e.reciprocal(sums, sums), stoks)
                t = dve.do(lambda e: e.tensor_tensor(
                    O[:, qt, 512 * half:512 * half + 512].rearrange("p (h e) -> p h e", h=8),
                    banks[bank][:, :].rearrange("p (h e) -> p h e", h=8), bc(sums, 64), ALU.mult), t, tok)
                free[bank] = [t]
                o_toks[qt][half] = t
                if done:
                    done(t)
            return after

        def mixer_cd(htoks):
            with ExitStack() as ph:
                KCm = sb([128, S], F, ph)
                QC = sb([128, 4, S], F, ph)
                QD = sb([128, 4, S], F, ph)
                KD = sb([128, 4, S], F, ph)
                VC = sb([128, 2, 128], F, ph)
                VD = sb([128, 2, 512], F, ph)
                O = Y[:, :, :].rearrange("p c s -> p (c s)").rearrange("p (q d) -> p q d", q=2)
                SM = sb([128, 16], F, ph)
                Z = [sb([128, 384], F, ph) for _ in range(2)]
                AZ = [sb([128, 384], F, ph) for _ in range(2)]
                SPm = [sb([128, 384], F, ph) for _ in range(2)]
                WT = [sb([128, 384], F, ph) for _ in range(2)]
                P = att_pool(ph)
                kq, dq = [], []

                def take(n, o, tok):
                    if n == 0:
                        t = dve.do(lambda e: e.tensor_copy(KCm[:, :], o), tok)
                        kq.append(t)
                    elif n < 5:
                        t = act.do(lambda e: e.activation(QC[:, n - 1, :], o, ACT.Copy, scale=0.125), tok)
                        kq.append(t)
                    elif n < 9:
                        t = act.do(lambda e: e.activation(QD[:, n - 5, :], o, ACT.Copy, scale=0.125), tok)
                        dq.append(t)
                    else:
                        t = dve.do(lambda e: e.tensor_copy(KD[:, n - 9, :], o), tok)
                        dq.append(t)
                    return t

                proj_T(CD_T, htoks, take, (0, 1, 2, 3))
                vt, dt_ = [], []

                def take_m(n, qt, o, tok):
                    if n == 0:
                        t = dve.do(lambda e: e.tensor_copy(VC[:, qt, :], o), tok)
                        vt.append(t)
                    else:
                        t = dve.do(lambda e: e.tensor_copy(VD[:, qt, 256 * (n - 1):256 * n], o), tok)
                        dt_.append(t)
                    return t

                proj_M(CD_M, take_m, (0, 1, 2))
                o_toks = [[None, None], [None, None]]
                lst = []
                for qt in range(2):
                    stoks = []
                    sums = SM[:, 8 * qt:8 * qt + 8]
                    lst += heads_list(P, qt, QC, KCm[:, :], VC[:, :, :], lambda h: BIAS[:, h, :], qt, sums, stoks,
                                      kq, vt, plain_after(O, qt, 0, qt, sums, stoks, o_toks))
                softmax_heads(lst, P)
                release(P)

                zf = [None] * 2
                wf = [None] * 2
                spf = [None] * 2
                pe.wait(free[0], free[1])

                def first(h):
                    j = h % 2
                    r = 64 * (h % 2)
                    q, kk = QD[r:r + 64, h // 2, :], KD[r:r + 64, h // 2, :]
                    b = 4 + j
                    pe.wait(free[b], dq)
                    pe.run(lambda e: e.matmul(banks[b][:, 0:256], kk[:, 0:128], q, start=True, stop=True,
                                              skip_group_check=True))
                    t = pe.do(lambda e: e.matmul(banks[b][:, 256:384], kk[:, 128:256], q[:, 128:256], start=True,
                                                 stop=True, skip_group_check=True))
                    tz = dve.do(lambda e: e.tensor_tensor(Z[j][:, :], banks[b][:, 0:384], strict, ALU.add), t, zf[j])
                    free[b] = [tz]
                    t = dve.do(lambda e: e.scalar_tensor_tensor(
                        out=AZ[j][:, :], in0=Z[j][:, :], scalar=-1.0, in1=Z[j][:, :], op0=ALU.mult, op1=ALU.min),
                        tz, spf[j])
                    t = act.do(lambda e: e.activation(AZ[j][:, :], AZ[j][:, :], ACT.Exp), t)
                    t = act.do(lambda e: e.activation(AZ[j][:, :], AZ[j][:, :], ACT.Ln, bias=1.0), t)
                    return dve.do(lambda e: e.scalar_tensor_tensor(
                        out=SPm[j][:, :], in0=Z[j][:, :], scalar=0.0, in1=AZ[j][:, :], op0=ALU.max, op1=ALU.add), t)

                def second(h, tsp):
                    j = h % 2
                    b = (6, 2)[j]
                    pe.wait(free[b], tsp)
                    pe.run(lambda e: e.matmul(banks[b][:, 0:256], tri, SPm[j][:, 0:256], start=True, stop=False,
                                              skip_group_check=True))
                    pe.run(lambda e: e.matmul(banks[b][:, 128:256], ones, SPm[j][:, 256:384], start=False, stop=True,
                                              skip_group_check=True))
                    t = pe.do(lambda e: e.matmul(banks[b][:, 256:384], tri, SPm[j][:, 256:384], start=False, stop=True,
                                                 skip_group_check=True))
                    spf[j] = t
                    t = dve.do(lambda e: e.tensor_tensor(Z[j][:, :], Z[j][:, :], banks[b][:, 0:384], ALU.subtract), t)
                    free[b] = [t]
                    t = act.do(lambda e: e.activation(WT[j][:, :], Z[j][:, :], ACT.Exp), t, wf[j])
                    zf[j] = t
                    return t

                def third(h, tw):
                    j = h % 2
                    v = [VD[:, kt, 64 * h:64 * h + 64] for kt in range(2)]
                    pe.wait(tw, dt_, free[1], free[3])
                    pe.run(lambda e: e.matmul(banks[1][:, 64 * h:64 * h + 64], WT[j][:, 0:128], v[0], start=True,
                                              stop=True, skip_group_check=True))
                    pe.run(lambda e: e.matmul(banks[3][:, 64 * h:64 * h + 64], WT[j][:, 128:256], v[0], start=True,
                                              stop=False, skip_group_check=True))
                    t = pe.do(lambda e: e.matmul(banks[3][:, 64 * h:64 * h + 64], WT[j][:, 256:384], v[1],
                                                 start=False, stop=True, skip_group_check=True))
                    wf[j] = t
                    return t

                a, b_ = {}, {}
                for i in range(10):
                    if i < 8:
                        a[i] = first(i)
                    if 1 <= i <= 8:
                        b_[i - 1] = second(i - 1, a[i - 1])
                    if i >= 2:
                        tok = third(i - 2, b_[i - 2])
                for qt in range(2):
                    t = dve.do(lambda e, qt=qt: e.tensor_copy(O[:, qt, 512:1024], banks[1 + 2 * qt][:, :]), tok)
                    free[1 + 2 * qt] = [t]
                    o_toks[qt][1] = t
                transposed(O, o_toks, None)
                return out_proj()

        def hybrid(layer, htoks):
            with ExitStack() as ph:
                GL = sb([16, S], F, ph)
                GW = sb([16, 256], F, ph)
                GQ = sb([128, 2, S], F, ph)
                GK = sb([128, 2, S], F, ph)
                Q = sb([128, 4, S], F, ph)
                K = sb([128, 4, S], F, ph)
                QP = [sb([128, S], F, ph) for _ in range(2)]
                R1 = [sb([128, S], F, ph) for _ in range(2)]
                V = sb([128, 2, 512], F, ph)
                GV = sb([128, 2, 512], F, ph)
                GR = sb([128, 2, 512], F, ph)
                O = Y[:, :, :].rearrange("p c s -> p (c s)").rearrange("p (q d) -> p q d", q=2)
                SM = sb([128, 40], F, ph)
                P = att_pool(ph)
                s_g = s_gu
                act.dma(s_g, lambda e: e.dma_start(GW[:, :], gup[layer]))
                gw_ready = (s_g, 16 * (layer + 1))
                kq, gq, gl = [], [], []
                qpf = [None] * 2
                r1f = [None] * 2

                def take(n, o, tok):
                    if n == 12:
                        t = dve.do(lambda e: e.tensor_copy(GL[:, :], o), tok)
                        gl.append(t)
                        return t
                    if n < 2:
                        t = act.do(lambda e: e.activation(GQ[:, n, :], o, ACT.Copy, scale=0.125), tok)
                        gq.append(t)
                        return t
                    if n < 4:
                        t = dve.do(lambda e: e.tensor_copy(GK[:, n - 2, :], o), tok)
                        gq.append(t)
                        return t
                    j = n % 2
                    dst = Q[:, n - 4, :] if n < 8 else K[:, n - 8, :]
                    sc = 0.125 if n < 8 else 1.0
                    t = act.do(lambda e: e.activation(QP[j][:, :], o, ACT.Copy, scale=sc), tok, qpf[j])
                    free_o = t
                    b = 4 + j
                    t2 = mm(banks[b][:, 0:256], rot, QP[j][:, :], toks=[t, free[b], small])
                    t3 = dve.do(lambda e: e.tensor_tensor(R1[j][:, :], banks[b][:, 0:256], sinT, ALU.mult), t2, r1f[j])
                    free[b] = [t3]
                    t4 = dve.do(lambda e: e.tensor_tensor(dst, QP[j][:, :], cosT, ALU.mult), t)
                    t5 = dve.do(lambda e: e.tensor_tensor(dst, dst, R1[j][:, :], ALU.add), t3, t4)
                    qpf[j] = [t4, t2]
                    r1f[j] = t5
                    kq.append(t5)
                    return free_o

                proj_T(HY_T, htoks, take, (0, 1, 2, 3))
                vt, gv, gr = [], [], []

                def take_m(n, qt, o, tok):
                    dst = (V, GV, GR)[n // 2][:, qt, 256 * (n % 2):256 * (n % 2) + 256]
                    lst = (vt, gv, gr)[n // 2]
                    if n < 4:
                        t = dve.do(lambda e: e.tensor_copy(dst, o), tok)
                    else:
                        t = act.do(lambda e: e.activation(dst, o, ACT.Silu), tok)
                    lst.append(t)
                    return t

                proj_M(HY_M, take_m, (0, 1, 2, 3))
                o_toks = [[None, None], [None, None]]
                lst = []
                sq = R1
                nw = V_ONORM + 8 * layer
                for qt in range(2):
                    stoks = []
                    sums = SM[:, 8 * qt:8 * qt + 8]

                    def norm(t, qt=qt):
                        ss = SM[:, 16 + qt:17 + qt]
                        t1 = act.do(lambda e: e.activation(SQ512, O[:, qt, 0:512], ACT.Square, accum_out=ss), t,
                                    sq512_free[0])
                        t2 = act.do(lambda e: e.activation(ss, ss, ACT.Ln, scale=1.0 / 512, bias=eps), t1)
                        t3 = act.do(lambda e: e.activation(ss, ss, ACT.Exp, scale=-0.5), t2)
                        sq512_free[0] = t1
                        o_toks[qt][0] = dve.do(lambda e: e.tensor_scalar(
                            O[:, qt, 0:512], O[:, qt, 0:512], ss, None, ALU.mult), t3)

                    lst += heads_list(P, qt, Q, K, V, lambda h: dil, qt, sums, stoks, kq, vt,
                                      plain_after(O, qt, 0, qt, sums, stoks, o_toks, norm), grouped=False)
                SQ512 = SIDER[0][:, 512:1024]
                sq512_free = [None]
                softmax_heads(lst, P)
                release(P)

                with ExitStack() as p2:
                    ONE, B, T1, T2, E1, E2 = (BIAS[:, k, :] for k in range(6))
                    X1, X2, QD_, KD_ = ([BIAS[:, 6 + 2 * k + n, :] for n in range(2)] for k in range(4))
                    AT = [sb([128, 384], F, p2) for _ in range(2)]
                    SG = SIDER[0][:, 0:512]
                    one_t = dve.do(lambda e: e.memset(ONE[:, :], 1.0), sq512_free[0])
                    atz = [dve.do(lambda e, j=j: e.memset(AT[j][:, :], 0.0)) for j in range(2)]
                    atf = [atz[0], atz[1]]
                    ready = []
                    chain = one_t
                    for p in range(2):
                        z = mm(banks[4][:, 0:256], GW[:, 128 * p:128 * p + 128], GL[:, :],
                               toks=[gl, gw_ready, free[4]])
                        gb = VEC[:, V_GB + 2 * layer + p:V_GB + 2 * layer + p + 1]
                        t = dve.do(lambda e, gb=gb: e.tensor_scalar(B[:, :], banks[4][:, 0:256], gb, None, ALU.add),
                                   z, chain)
                        free[4] = [t]
                        t = dve.do(lambda e: e.scalar_tensor_tensor(
                            out=T1[:, :], in0=B[:, :], scalar=-1.0, in1=B[:, :], op0=ALU.mult, op1=ALU.min), t)
                        t = act.do(lambda e: e.activation(T1[:, :], T1[:, :], ACT.Exp), t)
                        t = act.do(lambda e: e.activation(T1[:, :], T1[:, :], ACT.Ln, bias=1.0), t)
                        t = dve.do(lambda e: e.scalar_tensor_tensor(
                            out=T1[:, :], in0=B[:, :], scalar=0.0, in1=T1[:, :], op0=ALU.min, op1=ALU.subtract), t)
                        tb = dve.do(lambda e: e.tensor_tensor_scan(
                            B[:, :], ONE[:, :], T1[:, :], 0.0, ALU.mult, ALU.add), t)
                        t = dve.do(lambda e: e.tensor_scalar(
                            T1[:, :], B[:, :], B[:, 127:128], None, ALU.subtract), tb)
                        t = dve.do(lambda e: e.scalar_tensor_tensor(
                            out=T1[:, :], in0=T1[:, :], scalar=-1.0, in1=T1[:, :], op0=ALU.mult, op1=ALU.min), t)
                        t = act.do(lambda e: e.activation(E1[:, :], T1[:, :], ACT.Exp, scale=1.0 / 16), t)
                        t1 = dve.do(lambda e, p=p: e.tensor_tensor(
                            X1[p][:, 0:128], E1[:, 0:128], GK[:, p, 0:128], ALU.mult), t, gq)
                        t2 = dve.do(lambda e, p=p: e.tensor_tensor(
                            X1[p][:, 128:256], E1[:, 128:256], GQ[:, p, 128:256], ALU.mult), t)
                        v4 = lambda a: a.rearrange("p (c t) -> p c t", c=2)
                        t = dve.do(lambda e: e.tensor_tensor(
                            v4(T2[:, :]), v4(B[:, :]), B[:, 63:192:128].unsqueeze(2).to_broadcast([128, 2, 128]),
                            ALU.subtract), tb)
                        t = dve.do(lambda e: e.scalar_tensor_tensor(
                            out=T2[:, :], in0=T2[:, :], scalar=-1.0, in1=T2[:, :], op0=ALU.mult, op1=ALU.min), t)
                        t = act.do(lambda e: e.activation(E2[:, :], T2[:, :], ACT.Exp, scale=1.0 / 16), t)
                        t3 = dve.do(lambda e, p=p: e.tensor_tensor(
                            v4(X2[p][:, :])[:, :, 0:64], v4(E2[:, :])[:, :, 0:64], v4(GK[:, p, :])[:, :, 0:64],
                            ALU.mult), t)
                        t4 = dve.do(lambda e, p=p: e.tensor_tensor(
                            v4(X2[p][:, :])[:, :, 64:128], v4(E2[:, :])[:, :, 64:128], v4(GQ[:, p, :])[:, :, 64:128],
                            ALU.mult), t)
                        t = dve.do(lambda e: e.tensor_tensor(
                            T1[:, :].rearrange("p (c t) -> p c t", c=4), B[:, :].rearrange("p (c t) -> p c t", c=4),
                            B[:, 31:256:64].unsqueeze(2).to_broadcast([128, 4, 64]), ALU.subtract), t1, t2)
                        t = dve.do(lambda e: e.tensor_scalar(T1[:, :], T1[:, :], 1280.0, -1280.0, ALU.min, ALU.max), t)
                        ta = act.do(lambda e: e.activation(E1[:, :], T1[:, :], ACT.Exp, scale=1.0 / 16), t)
                        tc = act.do(lambda e: e.activation(E2[:, :], T1[:, :], ACT.Exp, scale=-1.0 / 16), t3, t4)
                        t5 = dve.do(lambda e, p=p: e.tensor_tensor(QD_[p][:, :], E1[:, :], GQ[:, p, :], ALU.mult), ta)
                        t6 = dve.do(lambda e, p=p: e.tensor_tensor(KD_[p][:, :], E2[:, :], GK[:, p, :], ALU.mult), tc)
                        chain = [t5, t6]
                        ready.append([t1, t2, t3, t4, t5, t6])
                    causal = hmask
                    for h in range(4):
                        p, r, j = h // 2, 64 * (h % 2), h % 2
                        b = 4 + j
                        x1, x2, qd, kd = (a[p][r:r + 64, :] for a in (X1, X2, QD_, KD_))
                        pe.wait(free[b], ready[p])

                        def m(o, l, rr, b=b):
                            return pe.do(lambda e: e.matmul(o, l, rr, start=True, stop=True, skip_group_check=True))
                        m(banks[b][:, 128:256], x1[:, 0:128], x1[:, 128:256])
                        for hh in range(2):
                            c0 = 0 if hh == 0 else 256
                            t0 = 128 * hh
                            m(banks[b][0:64, c0:c0 + 64], kd[:, t0:t0 + 64], qd[:, t0:t0 + 64])
                            m(banks[b][0:64, c0 + 64:c0 + 128], x2[:, t0:t0 + 64], x2[:, t0 + 64:t0 + 128])
                            tok = m(banks[b][64:128, c0:c0 + 128], kd[:, t0 + 64:t0 + 128], qd[:, t0:t0 + 128])
                        A = AT[j]
                        ta = act.do(lambda e, A=A, b=b: e.activation(A[:, 128:256], banks[b][:, 128:256], ACT.Copy),
                                    tok, atf[j])
                        tc = [dve.do(lambda e, A=A, b=b, c0=c0: e.copy_predicated(
                            A[:, c0:c0 + 128], causal, banks[b][:, c0:c0 + 128]), tok, ta, atf[j], mask_ready)
                            for c0 in (0, 256)]
                        free[b] = [ta] + tc
                        pe.wait(ta, tc, gv)
                        if h == 0:
                            pe.wait(free[6], free[3])
                        v = [GV[:, kt, 128 * h:128 * h + 128] for kt in range(2)]
                        oc = slice(128 * h, 128 * h + 128)
                        mm(banks[6][:, oc], A[:, 0:128], v[0], sig=False)
                        mm(banks[3][:, oc], A[:, 128:256], v[0], stop=False, sig=False)
                        tok = mm(banks[3][:, oc], A[:, 256:384], v[1], start=False)
                        atf[j] = tok
                    gfree = None
                    for qt in range(2):
                        bn = (6, 3)[qt]
                        bb = banks[bn]
                        ss = SM[:, 20 + 4 * qt:24 + 4 * qt]
                        g = O[:, qt, 512:1024]
                        t = dve.do(lambda e, bb=bb, g=g: e.tensor_copy(g, bb[:, :]), tok)
                        free[bn] = [t]
                        t1 = act.do(lambda e, g=g: e.activation(SQ512, g, ACT.Square), t, sq512_free[0], gfree)
                        t2 = dve.do(lambda e, ss=ss: e.tensor_reduce(
                            ss, SQ512.rearrange("p (h e) -> p h e", h=4), AX.X, ALU.add), t1)
                        sq512_free[0] = t2
                        t3 = act.do(lambda e, ss=ss: e.activation(ss, ss, ACT.Ln, scale=1.0 / 128, bias=eps), t2)
                        t3 = act.do(lambda e, ss=ss: e.activation(ss, ss, ACT.Exp, scale=-0.5), t3)
                        t5 = dve.do(lambda e, qt=qt, g=g: e.tensor_tensor(SG, GR[:, qt, :], g, ALU.mult), gr, t)
                        t6 = dve.do(lambda e, g=g, ss=ss: e.tensor_tensor(
                            g.rearrange("p (h e) -> p h e", h=4), SG.rearrange("p (h e) -> p h e", h=4),
                            bc(ss, 128), ALU.mult), t5, t3)
                        gfree = t6
                        o_toks[qt][1] = t6
                    transposed(O, o_toks, lambda c: VEC[:, nw + c:nw + c + 1])
                    return out_proj()

        t = pool.do(lambda e: e.memset(HM[:, :], 1.0))
        mask_ready = pool.do(lambda e: e.affine_select(
            out=HM[:, :], in_=HM[:, :], compare_op=ALU.is_ge, fill=0.0, base=0, pattern=[[1, 128]],
            channel_multiplier=-1), t)
        hmask = HM[:, :].bitcast(U32)

        xt = [x_in] * KC
        for j in range(8):
            i = next_tile("T")
            mod_tile(raw[i % RAW], raw_ready(i), j)
            done_tile(i, [(dve.sem, dve.count)])
        for layer in range(2):
            for sub in range(2):
                st = 2 * layer + sub
                mt = modulation(st)
                h = make_h(x_stats(xt), lambda c: A4[:, c:c + 1], lambda c: MOD[:, c:c + 1], mt)
                if sub == 0:
                    y, stat = (mixer_ab if layer == 0 else mixer_cd)(h)
                else:
                    y, stat = ffn(h)
                xt = residual(stat, lambda c: G4[:, c:c + 1], gating(st), y)
                mod_tok[0] = xt[-1]
        for layer in range(2):
            for sub in range(2):
                o = V_NORM2 + 32 * layer + 16 * sub
                h = make_h(x_stats(xt), lambda c, o=o: VEC[:, o + c:o + c + 1], None, small)
                y, st = hybrid(layer, h) if sub == 0 else ffn(h)
                xt = residual(st, lambda c, o=o: VEC[:, o + 8 + c:o + 9 + c], small, y)
        sp.dma(s_out, lambda e: e.dma_start(out, X[:, :, :]), xt[-1])
        sp.wait((s_out, 16))
        assert state["use"] == len(TILES) and side["use"] == len(SIDE)

        block = ctx.enter_context(nc.Block())
        block.sync(sp.emit)
        block.gpsimd(pool.emit)
        block.scalar(act.emit)
        block.vector(dve.emit)
        block.tensor(pe.emit)


def shape_constants():
    c = np.zeros((128, NCONST), np.float32)
    i = np.arange(128)
    c[:, C_ID:C_ID + 128] = i[:, None] == i[None, :]
    c[:, C_TRI:C_TRI + 128] = i[:, None] >= i[None, :]
    c[:, C_ONE:C_ONE + 128] = 1.0
    d = i % 64
    for p in range(128):
        if d[p] < 8:
            c[p + 8, C_ROT + p] = 1.0
        elif d[p] < 16:
            c[p - 8, C_ROT + p] = 1.0
    q = np.arange(256)
    st = np.concatenate([np.where(i[:, None] < q[None, :], 0.0, NEG),
                         np.where(128 + i[:, None] < q[None, 128:], 0.0, NEG)], axis=1)
    c[:, C_STRICT:C_STRICT + 384] = st
    dist = 128 + i[:, None] - q[None, :]
    m = ((dist >= 0) & (dist <= 128)).astype(np.int64) + ((dist >= 0) & (dist % 4 == 0)) + \
        ((dist >= 0) & (dist % 16 == 0))
    c[:, C_DIL:C_DIL + 256] = np.where(m > 0, np.log(np.maximum(m, 1)), NEG)
    inv = (np.float32(500000.0) ** (-(np.arange(8, dtype=np.float32) * np.float32(2.0)) / np.float32(16))).astype(
        np.float32)
    ang = (q.astype(np.float32)[None, :] * inv[:, None]).astype(np.float32).astype(np.float64)
    for p in range(128):
        if d[p] < 16:
            c[p, C_COS:C_COS + 256] = np.cos(ang[d[p] % 8])
            c[p, C_SIN:C_SIN + 256] = np.sin(ang[d[p] % 8]) * (-1.0 if d[p] < 8 else 1.0)
        else:
            c[p, C_COS:C_COS + 256] = 1.0
    c[:, C_HSEL:C_HSEL + 8] = (i[:, None] // 16) == np.arange(8)[None, :]
    c[:, C_REV:C_REV + 128] = (i[:, None] + i[None, :]) == 127
    c[0:16, C_REP:C_REP + 128] = i[:16, None] == (i[None, :] % 16)
    u = np.zeros((33, 1024), np.float32)
    for j in range(2):
        for t in range(512):
            dd = 255 - t
            lim = 256 if j == 0 else 128
            if dd < 0 or dd >= lim:
                u[32, 512 * j + t] = 1.0
            else:
                b = dd if dd < 16 else min(31, 16 + int(math.log(dd / 16) / math.log(8) * 16 + 1e-9))
                u[b, 512 * j + t] = 1.0
    return c, u


def pack_weights(a):
    tiles, side = plan()
    tiles = tiles + side
    wall = np.zeros((len(tiles), 128, TW), np.float32)

    def src(name):
        n = name[0]
        if n == "mod":
            return a["mod_w"][name[1], name[2]]
        if n in ("ab", "ab_out", "cd", "cd_out"):
            return a[{"ab": "w_in_ab", "ab_out": "w_out_ab", "cd": "w_in_cd", "cd_out": "w_out_cd"}[n]][0]
        if n in ("wk", "wv"):
            return a["nsa_cmp_" + n][0]
        return a[{"hy": "w_in_2", "hy_out": "w_out_2", "gate": "w_gate_2", "up": "w_up_2", "down": "w_down_2",
                  "ffn_in": "ffn_w_in", "ffn_out": "ffn_w_out"}[n]][name[1]]

    for i, (name, what, arg, _) in enumerate(tiles):
        if what == "T":
            w = src(name).reshape(KC, 128, -1)
            off = 0
            for c in arg:
                m = len(c)
                wall[i, :, off:off + KC * m] = w[:, :, c].transpose(1, 0, 2).reshape(128, KC * m)
                off += KC * m
        elif what == "M":
            w = src(name).reshape(KC, 128, -1)
            wall[i, :, :KC * len(arg)] = w[:, :, arg].transpose(1, 0, 2).reshape(128, -1)
        elif what == "GU":
            j, off = arg
            for c in range(2):
                w = src(name[c]).reshape(KC, 128, -1)
                o = 128 * j + (off if c else 0)
                wall[i, :, 1024 * c:1024 * c + 1024] = w[:, :, o:o + 128].transpose(1, 0, 2).reshape(128, 1024)
        elif what == "DN":
            m, half = arg
            w = src(name).reshape(FC, 128, D)[11 * half:11 * half + 11, :, 128 * m:128 * m + 128]
            wall[i, :, :11 * 128] = w.transpose(1, 0, 2).reshape(128, -1)
        else:
            w = src(name)[16 * arg:16 * arg + 16].transpose(1, 0, 2)
            t = wall[i].reshape(128, 16, 128)
            t[0:64, :, 0:64] = w
            t[64:128, :, 64:128] = w
    return wall


def pack_vectors(a):
    v = np.zeros((128, NV), np.float32)
    col = lambda x: x.reshape(-1, 128).T
    v[:, V_C:V_C + 8] = col(a["c"])
    for l in range(2):
        for s in range(2):
            o = V_MODB + 24 * (2 * l + s)
            v[:, o:o + 24] = col(a["mod_b"][l, s])
            o = V_NORM + 16 * (2 * l + s)
            v[:, o:o + 16] = col(a["norm_w"][l, s])
            o = V_NORM2 + 32 * l + 16 * s
            pre, post = (("mix_pre_norm_2", "mix_post_norm_2"), ("ffn_pre_norm_2", "ffn_post_norm_2"))[s]
            v[:, o:o + 8] = col(a[pre][l])
            v[:, o + 8:o + 16] = col(a[post][l])
        o = V_ONORM + 8 * l
        v[:, o:o + 4] = col(a["attn_out_norm_2"][l])
        v[:, o + 4:o + 8] = col(a["gla_out_norm_2"][l])
        v[:, V_GB + 2 * l:V_GB + 2 * l + 2] = col(a["gla_b_gate_2"][l])
    pe = a["nsa_cmp_pe"][0].T
    v[0:64, V_PE:V_PE + 32] = pe
    v[64:128, V_PE:V_PE + 32] = pe
    v[:, V_EPS] = 1e-6
    v[31:, V_ROW] = 1.0
    return v


def kernel(**inputs):
    import numpy as _np
    import concourse.bacc as _bacc
    from concourse import mybir as _mybir
    from concourse.bass_utils import run_bass_kernel_spmd as _run

    a = {k: _np.asarray(v) for k, v in inputs.items()}
    con, onehot = shape_constants()
    arrays = {
        "wall": pack_weights(a),
        "xin": _np.ascontiguousarray(a["x"][0].T.reshape(KC, 128, S).transpose(1, 0, 2)),
        "vecs": pack_vectors(a),
        "consts": con,
        "onehot": onehot,
        "sinks": _np.ascontiguousarray(a["swa_sinks"][0]),
        "table": _np.ascontiguousarray(a["rel_table"]),
        "gup": _np.ascontiguousarray(a["gla_w_gate_up_2"]),
    }
    nc = _bacc.Bacc("TRN2", target_bir_lowering=False, num_devices=1)
    f = _mybir.dt.float32
    args = [nc.dram_tensor(n, v.shape, f, kind="ExternalInput").ap() for n, v in arrays.items()]
    out = nc.dram_tensor("out_0", (128, KC, S), f, kind="ExternalOutput").ap()
    scratch = nc.dram_tensor("scratch", (16, 512), f).ap()
    build(nc, *args, out, scratch)
    r = _run(nc, [arrays], core_ids=[0])
    got = r.results[0]["out_0"]
    return _np.ascontiguousarray(got.transpose(1, 0, 2).reshape(D, S).T)[None]
```

```python
import math
from contextlib import ExitStack

import numpy as np
import concourse.bass as bass
from concourse import mybir

F = mybir.dt.float32
R = mybir.dt.float32r
U32 = mybir.dt.uint32
ACT = mybir.ActivationFunctionType
ALU = mybir.AluOpType
AX = mybir.AxisListType

S = 256
D = 1024
KC = 8
DFF = 2816
FC = 22
NEG = -1e30
TW = 2048
RAW = 4
SPL = 3
MRING = 2
AHEAD = 3
BIG = 3.0e38

V_C = 0
V_MODB = 8
V_NORM = V_MODB + 96
V_NORM2 = V_NORM + 64
V_ONORM = V_NORM2 + 64
V_GB = V_ONORM + 16
V_PE = V_GB + 4
V_EPS = V_PE + 16
V_ROW = V_EPS + 1
NV = V_ROW + 1

C_ID = 0
C_TRI = 128
C_ONE = 256
C_ROT = 384
C_STRICT = 512
C_DIL = 896
C_COS = 1152
C_SIN = 1408
C_HSEL = 1664
C_REP = 1672
C_REV = 1800
C_HALF = 1928
NCONST = 1930

HQ, KVW = 512, 128


def split_heads(base):
    return [np.concatenate([base + 64 * c + np.arange(64), base + 64 * (4 + c) + np.arange(64)])
            for c in range(4)]


def chunks(base, n):
    return [base + 128 * c + np.arange(128) for c in range(n)]


AB = np.cumsum([0, 512, 128, 128, 128, 128, 128, 128, 24, 512, 128, 128]).tolist()
AB_T = (chunks(AB[1], 1) + chunks(AB[2], 1) + chunks(AB[3], 1) + chunks(AB[5], 1)
        + split_heads(AB[0]) + chunks(AB[9], 1) + split_heads(AB[8]))
AB_PRE, AB_Q, AB_K = 6, 8, 10
AB_M = [np.concatenate([AB[4] + np.arange(128), AB[6] + np.arange(128)]),
        np.concatenate([AB[10] + np.arange(128), AB[7] + np.arange(24)])]
CD = np.cumsum([0, 512, 128, 128, 512, 512, 512]).tolist()
CD_T = chunks(CD[1], 1) + split_heads(CD[0]) + [CD[s] + 128 * c + np.arange(128) for c in range(4) for s in (3, 4)]
CD_PRE, CD_Q = 2, 8
CD_M = [CD[2] + np.arange(128), CD[5] + np.arange(256), CD[5] + 256 + np.arange(256)]
HY = np.cumsum([0, 512, 512, 512, 256, 256, 512, 512, 16]).tolist()
HY_T = chunks(HY[3], 2) + chunks(HY[4], 2) + [HY[7] + np.arange(16)] + [
    HY[s] + 128 * c + np.arange(128) for c in range(4) for s in (0, 1)]
HY_PRE = 6
HY_M = [HY[s] + 256 * i + np.arange(256) for s, i in ((5, 0), (5, 1), (2, 0), (6, 0), (6, 1), (2, 1))]


def plan():
    out = []

    def t_tiles(name, cols):
        for i in range(0, len(cols), 2):
            out.append((name, "T", cols[i:i + 2], True))

    def m_tiles(name, cols):
        for c in cols:
            out.append((name, "M", c, True))

    def mods(layer, sub, a, b):
        return [(("mod", layer, sub), "T", chunks(256 * i, 2), False) for i in range(a, b)]

    def ffn(gate, up, down, off):
        for j in range(FC):
            out.append(((gate, up), "GU", (j, off), True))
        for m in range(KC):
            for half in range(2):
                out.append((down, "DN", (m, half), True))

    out += mods(0, 0, 0, 8)
    for layer in range(2):
        if layer == 0:
            t_tiles(("ab",), AB_T[:AB_PRE])
            m_tiles(("ab",), AB_M[:1])
            t_tiles(("ab",), AB_T[AB_PRE:AB_Q])
            m_tiles(("ab",), AB_M[1:])
            for name in ("wk", "wv"):
                out.append(((name,), "CMP", name, False))
            t_tiles(("ab",), AB_T[AB_Q:])
            t_tiles(("ab_out",), chunks(0, 8))
        else:
            t_tiles(("cd",), CD_T[:CD_PRE])
            m_tiles(("cd",), CD_M[:1])
            t_tiles(("cd",), CD_T[CD_PRE:CD_Q + 2])
            m_tiles(("cd",), CD_M[1:2])
            t_tiles(("cd",), CD_T[CD_Q + 2:])
            m_tiles(("cd",), CD_M[2:])
            t_tiles(("cd_out",), chunks(0, 8))
        ffn(("ffn_in", layer), ("ffn_in", layer), ("ffn_out", layer), DFF)
    for layer in range(2):
        t_tiles(("hy", layer), HY_T[:HY_PRE])
        m_tiles(("hy", layer), HY_M[:2])
        t_tiles(("hy", layer), HY_T[HY_PRE:HY_PRE + 2])
        m_tiles(("hy", layer), HY_M[2:5])
        t_tiles(("hy", layer), HY_T[HY_PRE + 2:])
        m_tiles(("hy", layer), HY_M[5:])
        t_tiles(("hy_out", layer), chunks(0, 8))
        ffn(("gate", layer), ("up", layer), ("down", layer), 0)
    side = mods(0, 0, 8, 12) + mods(0, 1, 0, 12) + mods(1, 0, 0, 12) + mods(1, 1, 0, 12)
    return out, side


def width(tile):
    _, what, arg, _ = tile
    if what == "T":
        return KC * sum(len(c) for c in arg)
    if what == "M":
        return KC * len(arg)
    if what == "CMP":
        return 2048 if arg == "wk" else 1024
    if what == "DN":
        return 11 * 128
    return TW


class Queue:

    def __init__(self, sem):
        self.sem = sem
        self.count = 0
        self.ops = []
        self.seen = {}

    def wait(self, *toks):
        for t in toks:
            if t is None:
                continue
            if isinstance(t, list):
                self.wait(*t)
                continue
            sem, val = t
            if self.seen.get(sem.name, 0) < val:
                self.seen[sem.name] = val
                self.ops.append(lambda e, sem=sem, val=val: e.wait_ge(sem, val))

    def run(self, f, *toks):
        self.wait(*toks)
        self.ops.append(f)

    def do(self, f, *toks):
        self.wait(*toks)
        self.count += 1
        self.ops.append(lambda e: f(e).then_inc(self.sem, 1))
        return (self.sem, self.count)

    def dma(self, sem, f, *toks):
        self.wait(*toks)
        self.ops.append(lambda e: f(e).then_inc(sem, 16))

    def emit(self, e):
        for f in self.ops:
            f(e)


def build(nc, wall, xin, vecs, consts, onehot, sinks, table, gup, out, scratch):
    TILES, SIDE = plan()
    ctx = ExitStack()
    with ctx:
        names = [0]

        def sb(shape, dt=F, where=ctx):
            names[0] += 1
            return where.enter_context(nc.sbuf_tensor(f"t{names[0]}", shape, dt))

        def sem(name):
            return ctx.enter_context(nc.semaphore(name))

        banks = [ctx.enter_context(nc.psum_tensor(f"bank{i}", [128, 512], F)) for i in range(8)]
        free = [None] * 8

        pe, act, dve, pool, sp = (Queue(sem(f"s_{n}")) for n in ("pe", "act", "dve", "pool", "sp"))

        raw = [sb([128, TW]) for _ in range(RAW)]
        wh = [sb([128, TW], R) for _ in range(SPL)]
        wl = [sb([128, TW], R) for _ in range(SPL)]
        s_raw = [sem(f"s_raw{i}") for i in range(RAW)]
        X = sb([128, KC, S])
        HH = sb([128, KC, S], R)
        HL = sb([128, KC, S], R)
        Y = sb([128, KC, S])
        RS = sb([128, S])
        LN = sb([128, S])
        SQ = [sb([128, S]) for _ in range(2)]
        VEC = sb([128, NV])
        CON = sb([128, NCONST])
        BIAS = sb([128, 16, S])
        A4 = sb([128, 8])
        MOD = sb([128, 24])
        SIDER = [sb([128, TW]) for _ in range(MRING)]
        ACC = [[sb([128, 256]) for _ in range(2)] for _ in range(2)]
        s_side = [sem(f"s_side{i}") for i in range(MRING)]
        G4 = sb([128, 8])
        COL = sb([128, 1])
        col_ready = dve.do(lambda e: e.memset(COL[:, :], 1.0))
        MB = sb([128, 16])
        HM = sb([128, 128])

        s_in = sem("s_in")
        s_con = sem("s_con")
        s_x = sem("s_x")
        s_tab = sem("s_tab")
        s_u = sem("s_u")
        s_b = sem("s_b")
        s_sk = sem("s_sk")
        s_gu = sem("s_gu")
        s_out = sem("s_out")
        s_sw = sem("s_sw")

        ident = CON[:, C_ID:C_ID + 128]
        tri = CON[:, C_TRI:C_TRI + 128]
        ones = CON[:, C_ONE:C_ONE + 128]
        rot = CON[:, C_ROT:C_ROT + 128]
        strict = CON[:, C_STRICT:C_STRICT + 384]
        dil = CON[:, C_DIL:C_DIL + 256]
        cosT = CON[:, C_COS:C_COS + 256]
        sinT = CON[:, C_SIN:C_SIN + 256]
        rep33 = CON[0:33, C_REP:C_REP + 128]
        hsel = CON[:, C_HSEL:C_HSEL + 8]
        halves = CON[:, C_HALF:C_HALF + 2]
        eps = VEC[:, V_EPS:V_EPS + 1]

        raw_free = {}
        spl_free = {}
        state = {"dma": 0, "split": 0, "use": 0}
        split_tok = {}
        split_no = {}
        k = 0
        for i, t in enumerate(TILES):
            if t[3]:
                split_no[i] = k
                k += 1

        def raw_ready(i):
            return (s_raw[i % RAW], 16 * (i // RAW + 1))

        def pump():
            while state["dma"] < len(TILES):
                i = state["dma"]
                if i >= RAW and i - RAW not in raw_free:
                    return
                n = width(TILES[i])
                toks = raw_free[i - RAW] if i >= RAW else None
                sp.dma(s_raw[i % RAW], lambda e, i=i, n=n: e.dma_start(raw[i % RAW][:, 0:n], wall[i, :, 0:n]), toks)
                state["dma"] += 1

        def splits(upto):
            while state["split"] <= min(upto, len(TILES) - 1):
                i = state["split"]
                state["split"] += 1
                if i not in split_no:
                    continue
                n = width(TILES[i])
                sl = split_no[i] % SPL
                r, h, l = raw[i % RAW], wh[sl], wl[sl]
                fr = spl_free.get(split_no[i] - SPL)
                th = act.do(lambda e, r=r, h=h, n=n: e.activation(h[:, 0:n], r[:, 0:n], ACT.Copy),
                            raw_ready(i), fr)
                tl = dve.do(lambda e, r=r, h=h, l=l, n=n: e.tensor_tensor(
                    l[:, 0:n], r[:, 0:n], h[:, 0:n].bitcast(F), ALU.subtract), raw_ready(i), th, fr)
                split_tok[i] = [th, tl]
                raw_free[i] = [tl]
                pump()

        def next_tile(kind):
            i = state["use"]
            state["use"] += 1
            assert TILES[i][1] == kind, (i, TILES[i], kind)
            j = i
            while j < len(TILES) and j < i + AHEAD:
                if i < 8 and j in split_no:
                    break
                if j in split_no and split_no[j] - SPL >= 0 and split_no[j] - SPL not in spl_free:
                    break
                if j > i and state["dma"] <= j:
                    break
                splits(j)
                j += 1
            return i

        def done_tile(i, tok):
            if i in split_no:
                spl_free[split_no[i]] = tok
            else:
                raw_free[i] = tok
            pump()

        def wt(i):
            sl = split_no[i] % SPL
            return wh[sl], wl[sl]

        def mm3(out, lh, ll, rh, rl, first, last, sig=False):
            pe.run(lambda e: e.matmul(out, lh, rh, start=first, stop=False, skip_group_check=True))
            pe.run(lambda e: e.matmul(out, lh, rl, start=False, stop=False, skip_group_check=True))
            f = lambda e: e.matmul(out, ll, rh, start=False, stop=last, skip_group_check=True)
            if last or sig:
                return pe.do(f)
            pe.run(f)

        def mm(out, l, r, start=True, stop=True, toks=(), sig=True):
            f = lambda e: e.matmul(out, l, r, start=start, stop=stop, skip_group_check=True)
            pe.wait(*toks)
            return pe.do(f) if sig else pe.run(f)

        pump()

        act.dma(s_in, lambda e: e.dma_start(VEC[:, :], vecs))
        act.dma(s_x, lambda e: e.dma_start(X[:, :, :], xin), raw_ready(0))
        act.dma(s_con, lambda e: e.dma_start(CON[:, :], consts), raw_ready(2))
        vec_in = (s_in, 16)
        small = [vec_in, (s_con, 16)]
        x_in = (s_x, 16)

        TB = MB[0:33, :]
        OH = BIAS[0:33, 0:4, :].rearrange("p c s -> p (c s)")
        UT = BIAS[0:8, 4:8, :].rearrange("p c s -> p (c s)")
        t0 = dve.do(lambda e: e.memset(TB, NEG))
        act.dma(s_tab, lambda e: e.dma_start(TB[0:32, :], table), t0)
        act.dma(s_tab, lambda e: e.dma_start(OH, onehot))
        bias_ready = []

        def looked_up():
            for j in range(2):
                tp = mm(banks[j][0:8, 0:512], TB[:, 8 * j:8 * j + 8], OH[:, 512 * j:512 * j + 512],
                        toks=[(s_tab, 32), t0])
            return tp

        def expand(tp):
            tu = [dve.do(lambda e, j=j: e.tensor_copy(UT[:, 512 * j:512 * j + 512], banks[j][0:8, 0:512]), tp)
                  for j in range(2)]
            free[0], free[1] = [tu[0]], [tu[1]]
            for j in range(2):
                act.dma(s_u, lambda e, j=j: e.dma_start(scratch[8 * j:8 * j + 8, :],
                                                         UT[:, 512 * j:512 * j + 512]), tu[j])
            toep = bass.AP(tensor=scratch.tensor, offset=0, ap=[[1, 128], [512, 16], [1, 256]])
            sp.dma(s_b, lambda e: e.dma_start(BIAS[:, :, :], toep), (s_u, 32))

        def reverse():
            rev = CON[:, C_REV:C_REV + 128]
            for j in range(8):
                b = j % 4
                dst = BIAS[:, 2 * j:2 * j + 2, :]
                pe.wait(free[b], small, (s_b, 16))
                t = pe.do(lambda e, b=b, dst=dst: e.matmul(banks[b][:, :], rev, dst, start=True, stop=True))
                t = dve.do(lambda e, b=b, dst=dst: e.tensor_copy(dst.rearrange("p a b -> p (a b)"), banks[b][:, :]), t)
                free[b] = [t]
            bias_ready.append(t)

        acc_free = [None, None]
        accn = [0]
        mod_done = {}
        pending = []
        side = {"dma": 0, "use": 0}
        side_free = {}

        def side_pump():
            while side["dma"] < len(SIDE):
                i = side["dma"]
                if i >= MRING and i - MRING not in side_free:
                    return
                toks = side_free[i - MRING] if i >= MRING else None
                sp.dma(s_side[i % MRING], lambda e, i=i: e.dma_start(SIDER[i % MRING][:, :], wall[len(TILES) + i]),
                       toks)
                side["dma"] += 1

        def mod_tile(buf, ready, block):
            w = buf[:, :].rearrange("p (c k m) -> p c k m", c=2, k=KC)
            j = accn[0] % 2
            accn[0] += 1
            t = [None, None]
            for kc in range(KC):
                a = ACC[j][kc % 2]
                av = a[:, :].rearrange("p (c m) -> p c m", c=2)
                cc = VEC[:, V_C + kc:V_C + kc + 1]
                if kc < 2:
                    t[kc] = dve.do(lambda e, av=av, kc=kc, cc=cc: e.tensor_scalar(
                        av, w[:, :, kc, :], cc, None, ALU.mult), ready, vec_in, acc_free[j])
                else:
                    t[kc % 2] = dve.do(lambda e, av=av, kc=kc, cc=cc: e.scalar_tensor_tensor(
                        out=av, in0=w[:, :, kc, :], scalar=cc, in1=av, op0=ALU.mult, op1=ALU.add), t[kc % 2])
            col = 24 * (block // 12 % 2) + 2 * (block % 12)

            def over_partitions():
                pe.wait(free[7], t[0], t[1], col_ready)
                for c in range(2):
                    pe.run(lambda e, c=c: e.matmul(
                        banks[7][:, col + c:col + c + 1], ACC[j][0][:, 128 * c:128 * c + 128], COL[:, :],
                        start=True, stop=False, skip_group_check=True))
                    tok = pe.do(lambda e, c=c: e.matmul(
                        banks[7][:, col + c:col + c + 1], ACC[j][1][:, 128 * c:128 * c + 128], COL[:, :],
                        start=False, stop=True, skip_group_check=True))
                acc_free[j] = tok
                mod_done[block] = mod_done["last"] = tok

            pending.append(over_partitions)
            if len(pending) > 1:
                pending.pop(0)()
            return [t[0], t[1]]

        def mod_tile_pe(buf, ready, block):
            w = buf[:, :].rearrange("p (c k m) -> p c k m", c=2, k=KC)
            col = 2 * block
            pe.wait(free[7], ready, vec_in)
            for c in range(2):
                for kc in range(KC):
                    f = lambda e, c=c, kc=kc: e.matmul(
                        banks[7][:, col + c:col + c + 1], w[:, c, kc, :], VEC[:, V_C + kc:V_C + kc + 1],
                        start=(kc == 0), stop=(kc == KC - 1), skip_group_check=True)
                    tok = pe.do(f) if kc == KC - 1 else pe.run(f)
            mod_done[block] = mod_done["last"] = tok
            return [tok]

        hold = [False]

        def background(n=1):
            if hold[0]:
                return
            for _ in range(n):
                i = side["use"]
                if i >= len(SIDE):
                    return
                side["use"] += 1
                side_pump()
                side_free[i] = mod_tile(SIDER[i % MRING], (s_side[i % MRING], 16 * (i // MRING + 1)), 8 + i)
                side_pump()

        def need(block):
            while 8 + side["use"] <= block:
                print("forced", block, side["use"])
                background()
            while pending:
                pending.pop(0)()
            return mod_done["last"]

        def modulation(st):
            tok = need(12 * st + 7)
            o = V_MODB + 24 * st
            n = V_NORM + 16 * st
            b = 24 * (st % 2)
            t1 = dve.do(lambda e: e.tensor_tensor(MOD[:, 0:16], banks[7][:, b:b + 16], VEC[:, o:o + 16], ALU.add),
                        tok, small, mod_tok[0])
            free[7] = [t1]
            return [dve.do(lambda e: e.scalar_tensor_tensor(
                out=A4[:, :], in0=MOD[:, 8:16], scalar=1.0, in1=VEC[:, n:n + 8], op0=ALU.add, op1=ALU.mult), t1)]

        def gating(st):
            tok = need(12 * st + 11)
            o = V_MODB + 24 * st + 16
            n = V_NORM + 16 * st + 8
            b = 24 * (st % 2) + 16
            t1 = dve.do(lambda e: e.tensor_tensor(MOD[:, 16:24], banks[7][:, b:b + 8], VEC[:, o:o + 8], ALU.add), tok)
            free[7] = [t1]
            return [dve.do(lambda e: e.tensor_tensor(G4[:, :], MOD[:, 16:24], VEC[:, n:n + 8], ALU.mult), t1)]

        mod_tok = [None]

        sq_free = [None, None]
        sqn = [0]

        def stat_start(src, tok):
            j = sqn[0] % 2
            sqn[0] += 1
            t = act.do(lambda e: e.activation(SQ[j][:, :], src, ACT.Square), tok, sq_free[j])
            return j, t

        def stat_add(c, jt):
            j, t = jt
            if c == 0:
                pe.wait(free[6])
            tok = mm(banks[6][:, 0:S], ones, SQ[j][:, :], start=(c == 0), stop=(c == KC - 1), toks=[t, small])
            sq_free[j] = tok
            return tok

        rs_free = [None]

        def rstd(tok):
            t = act.do(lambda e: e.activation(LN[:, :], banks[6][:, 0:S], ACT.Ln, scale=1.0 / D, bias=eps),
                       tok, small)
            free[6] = t
            return act.do(lambda e: e.activation(RS[:, :], LN[:, :], ACT.Exp, scale=-0.5), t, rs_free[0])

        h_free = [None]

        def make_h(stat, a_of, shift_of, mtok):
            r = rstd(stat)
            toks = []
            for c in range(KC):
                t = dve.do(lambda e, c=c: e.scalar_tensor_tensor(
                    out=Y[:, c, :], in0=X[:, c, :], scalar=a_of(c), in1=RS[:, :], op0=ALU.mult, op1=ALU.mult),
                    r, mtok)
                if shift_of is None:
                    th = act.do(lambda e, c=c: e.activation(HH[:, c, :], Y[:, c, :], ACT.Copy), t, h_free[0])
                    f = lambda e, c=c: e.tensor_tensor(HL[:, c, :], Y[:, c, :], HH[:, c, :].bitcast(F), ALU.subtract)
                else:
                    th = act.do(lambda e, c=c: e.activation(
                        HH[:, c, :], Y[:, c, :], ACT.Identity, bias=shift_of(c)), t, h_free[0])
                    f = lambda e, c=c: e.scalar_tensor_tensor(
                        out=HL[:, c, :], in0=Y[:, c, :], scalar=shift_of(c), in1=HH[:, c, :].bitcast(F),
                        op0=ALU.add, op1=ALU.subtract)
                toks.append([th])
                if c:
                    toks[c - 1].append(dve.do(fl, toks[c - 1]))
                fl = f
            toks[-1].append(dve.do(fl, th))
            rs_free[0] = t
            return toks

        def x_stats(toks):
            for c in range(KC):
                st = stat_add(c, stat_start(X[:, c, :], toks[c]))
            return st

        def residual(stat, g_of, mtok, ytoks):
            r = rstd(stat)
            toks = []
            for c in range(KC + 1):
                if c < KC:
                    t = dve.do(lambda e, c=c: e.scalar_tensor_tensor(
                        out=Y[:, c, :], in0=Y[:, c, :], scalar=g_of(c), in1=RS[:, :], op0=ALU.mult, op1=ALU.mult),
                        r, mtok, ytoks[c])
                    rs_free[0] = t
                if c:
                    toks.append(dve.do(lambda e, c=c - 1: e.tensor_tensor(
                        X[:, c, :], X[:, c, :], Y[:, c, :], ALU.add), tp))
                tp = t
            return toks

        def blocks2(parts, h, l, htoks):
            order = [(p, kc) for p in range(len(parts)) for kc in range(KC)]
            if htoks is not None:
                order = [(p, kc) for kc in range(KC) for p in range(len(parts))]
            for p, kc in order:
                m, off, o = parts[p]
                if htoks is not None:
                    pe.wait(htoks[kc])
                q = slice(off + kc * m, off + kc * m + m)
                first = kc == 0 and (htoks is None or p == 0)
                tok = mm3(o, h[:, q], l[:, q], HH[:, kc, :], HL[:, kc, :], first, kc == KC - 1)
            return tok

        later = []

        def take_turns(handle, toks):
            t = toks[-1][-1]
            for x in toks:
                t = handle(*x[:-1], [t, toks[-1][-1]])
            return [t]

        def proj_T(cols, n0, htoks, handle, ring):
            for t in range(0, len(cols), 2):
                i = next_tile("T")
                h, l = wt(i)
                b = ring[(t // 2) % len(ring)]
                pe.wait(free[b], split_tok[i])
                parts, off = [], 0
                for k, c in enumerate(cols[t:t + 2]):
                    parts.append((len(c), off, banks[b][0:len(c), 256 * k:256 * k + 256]))
                    off += KC * len(c)
                if t == 0 and htoks is not None:
                    tok = blocks2(parts, h, l, htoks)
                else:
                    for k in range(len(parts)):
                        if k:
                            yield
                        tok = blocks2(parts[k:k + 1], h, l, None)
                done_tile(i, tok)
                free[b] = take_turns(handle, [(n0 + t + k, p[2], tok) for k, p in enumerate(parts)])
                h_free[0] = tok
                background()
                yield
                if later:
                    tok = [f(free[b]) for f, _ in later][-1]
                    free[b] = [[g(tok) for _, g in later][-1]]
                    later.clear()

        def proj_M(cols, n0, handle, ring):
            for n, c in enumerate(cols):
                i = next_tile("M")
                h, l = wt(i)
                m = len(c)
                b = ring[n % len(ring)]
                pe.wait(free[b], split_tok[i])
                toks = []
                for qt in range(2):
                    if qt:
                        yield
                    o = banks[b][:, 256 * qt:256 * qt + m]
                    for kc in range(KC):
                        q = slice(kc * m, kc * m + m)
                        s = slice(128 * qt, 128 * qt + 128)
                        tok = mm3(o, HH[:, kc, s], HL[:, kc, s], h[:, q], l[:, q], kc == 0, kc == KC - 1)
                    toks.append((n0 + n, qt, o, tok))
                done_tile(i, tok)
                free[b] = take_turns(handle, toks)
                h_free[0] = tok
                background()
                yield

        def drain(*gens):
            for g in gens:
                for _ in g:
                    pass

        def turns(*gens):
            live = list(gens)
            while live:
                for g in list(live):
                    try:
                        next(g)
                    except StopIteration:
                        live.remove(g)
                        continue
                    yield

        def by_pairs(a, b):
            return [x for ab in zip(a, b) for x in ab]

        def weave(main, fill, per=1):
            for _ in main:
                for _ in range(per):
                    next(fill, None)

        def weave_before(main, *fills):
            going = True
            while going:
                for f in fills:
                    next(f, None)
                going = next(main, 0) is None

        def out_proj():
            ytoks, pend = [], None
            for t in range(4):
                i = next_tile("T")
                h, l = wt(i)
                b = t % 4
                fr = []
                pe.wait(free[b], split_tok[i])
                outs = [(2 * t + c, banks[b][:, 256 * c:256 * c + 256]) for c in range(2)]
                tok = blocks2([(128, 1024 * c, outs[c][1]) for c in range(2)], h, l, ot_tok if t == 0 else None)
                done_tile(i, tok)
                if pend is not None:
                    for m, jt in pend:
                        stat_add(m, jt)
                pend = []
                for m, o in outs:
                    ty = dve.do(lambda e, m=m, o=o: e.tensor_copy(Y[:, m, :], o), tok)
                    ytoks.append(ty)
                    pend.append((m, stat_start(Y[:, m, :], ty)))
                    fr.append(ty)
                free[b] = fr
            for m, jt in pend:
                st = stat_add(m, jt)
            h_free[0] = tok
            return ytoks, st

        def ffn(htoks):
            with ExitStack() as ph:
                AH = sb([128, FC, S], R, ph)
                AL = sb([128, FC, S], R, ph)
                SG = [Y[:, 4 + k, :] for k in range(2)]
                PV = [Y[:, 6 + k, :] for k in range(2)]
                sg_free, pv_free = [None] * 2, [None] * 2
                atoks = []
                for j in range(FC):
                    i = next_tile("GU")
                    h, l = wt(i)
                    b = j % 3
                    pe.wait(free[b], split_tok[i])
                    tok = blocks2([(128, 1024 * c, banks[b][:, 256 * c:256 * c + 256]) for c in range(2)], h, l,
                                  htoks if j == 0 else None)
                    done_tile(i, tok)
                    if j % 3 == 1:
                        background()
                    s, v, bb = SG[j % 2], PV[j % 2], banks[b]
                    t1 = act.do(lambda e, s=s, bb=bb: e.activation(s, bb[:, 0:256], ACT.Silu),
                                tok, sg_free[j % 2])
                    t2 = dve.do(lambda e, s=s, v=v, bb=bb: e.tensor_tensor(
                        v, s, bb[:, 256:512], ALU.mult), t1, pv_free[j % 2])
                    th = act.do(lambda e, v=v, j=j: e.activation(AH[:, j, :], v, ACT.Copy), t2)
                    tl = dve.do(lambda e, v=v, j=j: e.tensor_tensor(
                        AL[:, j, :], v, AH[:, j, :].bitcast(F), ALU.subtract), th)
                    sg_free[j % 2], pv_free[j % 2] = t2, tl
                    free[b] = [t2]
                    atoks.append([th, tl])
                h_free[0] = tok
                ytoks, pend = [], None
                for m in range(KC):
                    b = 3 + m % 3
                    o = banks[b][:, 0:256]
                    pe.wait(free[b])
                    for half in range(2):
                        i = next_tile("DN")
                        h, l = wt(i)
                        pe.wait(split_tok[i])
                        for kk in range(11):
                            kc = 11 * half + kk
                            if m == 0:
                                pe.wait(atoks[kc])
                            q = slice(kk * 128, kk * 128 + 128)
                            last = kk == 10 and half == 1
                            tok = mm3(o, h[:, q], l[:, q], AH[:, kc, :], AL[:, kc, :], kc == 0, last,
                                      sig=kk == 10)
                        done_tile(i, tok)
                    ty = dve.do(lambda e, m=m, o=o: e.tensor_copy(Y[:, m, :], o), tok)
                    ytoks.append(ty)
                    jt = stat_start(Y[:, m, :], ty)
                    free[b] = [ty]
                    if m % 2 or m == 4:
                        background()
                    if pend is not None:
                        stat_add(m - 1, pend)
                    pend = jt
                return ytoks, stat_add(KC - 1, pend)

        ot_tok = [None] * KC

        def transposed(o_sb, o_toks, scale_of, ring=(0, 1)):
            for c in range(KC):
                b = ring[c % len(ring)]
                pe.wait(free[b])
                for qt in range(2):
                    tok = pe.do(lambda e, qt=qt, b=b, c=c: e.transpose(
                        banks[b][:, 128 * qt:128 * qt + 128], o_sb[:, qt, 128 * c:128 * c + 128], ident),
                        o_toks[qt][c // 4], small)
                src = banks[b][:, 0:S]
                if scale_of is None:
                    th = act.do(lambda e, c=c, src=src: e.activation(HH[:, c, :], src, ACT.Copy), tok, h_free[0])
                    tl = dve.do(lambda e, c=c, src=src: e.tensor_tensor(
                        HL[:, c, :], src, HH[:, c, :].bitcast(F), ALU.subtract), th)
                else:
                    w = scale_of(c)
                    th = act.do(lambda e, c=c, src=src, w=w: e.activation(
                        HH[:, c, :], src, ACT.Copy, scale=w), tok, h_free[0])
                    tl = dve.do(lambda e, c=c, src=src, w=w: e.scalar_tensor_tensor(
                        out=HL[:, c, :], in0=src, scalar=w, in1=HH[:, c, :].bitcast(F),
                        op0=ALU.mult, op1=ALU.subtract), th)
                free[b] = [th, tl]
                ot_tok[c] = [th, tl]

        def softmax_pairs(steps, P):
            n = len(steps)

            def score(i):
                a = steps[i]
                g = P["n"] + i
                qt = a["qt"]
                K = 128 * (qt + 1)
                b = 4 + g % 2
                pe.wait(P["fr_s"][g % 2], free[b], a["toks"])
                t = pe.do(lambda e: e.matmul(
                    banks[b][:, 0:2 * K].rearrange("p (h k) -> p h k", h=2), a["q"][:, 128 * qt:128 * qt + 128],
                    a["kz"][:, :, 0:K], start=True, stop=True, skip_group_check=True))
                s, p = P["s"][g % 2], P["p"][g % 3]
                nms = []
                for h in range(2):
                    nm = P["nm"][:, (2 * g + h) % 8:(2 * g + h) % 8 + 1]
                    t2 = dve.do(lambda e, h=h, nm=nm: e.tensor_tensor_reduce(
                        out=s[:, h * K:h * K + K], in0=banks[b][:, h * K:h * K + K], in1=a["bias"][h], scale=-1.0,
                        scalar=a["start"][h], op0=ALU.add, op1=ALU.min, accum_out=nm),
                        t, P["fr_n"][g % 2], bias_ready, a.get("nmwait"))
                    nms.append((nm, t2))
                P["fr_s"][g % 2] = t2
                ex = []
                for h, (nm, t2) in enumerate(nms):
                    if a.get("keep"):
                        t3 = dve.do(lambda e, h=h, nm=nm: e.tensor_copy(a["keep"][h], nm), t2)
                        a["kept"].append(t3)
                    ex.append(act.do(lambda e, h=h, nm=nm: e.activation(
                        p[:, h * K:h * K + K], s[:, h * K:h * K + K], ACT.Exp, scale=-1.0, bias=nm,
                        accum_out=a["sum"][h]), t2, P["fr_p"][g % 3]))
                P["fr_n"][g % 2] = ex[-1] if not a.get("keep") else [ex[-1], t3]
                a["exp"] = ex
                a["sums"] += ex

            def turn(i):
                a = steps[i]
                g = P["n"] + i
                nt = 2 * (a["qt"] + 1)
                p, pT = P["p"][g % 3], P["pT"][g % 2]
                pe.wait(P["fr_t"], free[6], a["exp"])
                for k in range(nt):
                    t = pe.do(lambda e, k=k: e.transpose(
                        banks[6][:, 128 * k:128 * k + 128], p[:, 128 * k:128 * k + 128], ident))
                P["fr_p"][g % 3] = t
                src = banks[6][:, 0:128 * nt]
                if g % 2:
                    t = dve.do(lambda e: e.tensor_copy(pT[:, 0:128 * nt], src), t, P["fr_pt"][g % 2])
                else:
                    t = act.do(lambda e: e.activation(pT[:, 0:128 * nt], src, ACT.Copy), t, P["fr_pt"][g % 2])
                P["fr_t"] = t
                a["turned"] = t

            def value(i):
                a = steps[i]
                g = P["n"] + i
                qt = a["qt"]
                pT = P["pT"][g % 2]
                pe.wait(a["turned"], free[a["ob"]], a["vtoks"])
                for h in range(2):
                    for kt in range(qt + 1):
                        k = h * (qt + 1) + kt
                        t = pe.do(lambda e, k=k, h=h, kt=kt: e.matmul(
                            a["out"][h], pT[:, 128 * k:128 * k + 128], a["v"][h][kt], start=(kt == 0),
                            stop=(kt == qt), skip_group_check=True))
                P["fr_pt"][g % 2] = t
                if a.get("after"):
                    a["after"](t)

            for i in range(n + 3):
                if i < n:
                    score(i)
                if 2 <= i < n + 2:
                    turn(i - 2)
                if i >= 3:
                    value(i - 3)
                if i == n + 2:
                    P["n"] += n
                yield

        def att_pool(ph):
            return {"s": [sb([128, 512], F, ph) for _ in range(2)], "p": [sb([128, 512], F, ph) for _ in range(3)],
                    "pT": [sb([128, 512], F, ph) for _ in range(2)], "nm": sb([128, 8], F, ph),
                    "fr_s": [None] * 2, "fr_p": [None] * 3, "fr_n": [None] * 2, "fr_t": None,
                    "fr_pt": [None] * 2, "n": 0}

        def head_pairs(qt, Q, KZ, V, bias, ob, sums, sumtoks, qtoks, vtoks, after, grouped=True, sink=None):
            out = []
            for c in range(4):
                hs = (c, 4 + c) if grouped else (2 * c, 2 * c + 1)
                vc = [g if grouped else h for g, h in enumerate(hs)]
                a = dict(q=Q[:, c, :], kz=KZ if grouped else KZ[:, c, :, :], qt=qt,
                         v=[[V[:, kt, 64 * x:64 * x + 64] for kt in range(2)] for x in vc],
                         bias=[bias(h)[:, 0:256] if qt else bias(h)[:, 128:256] for h in hs],
                         start=[BIG, BIG], ob=ob, out=[banks[ob][:, 64 * h:64 * h + 64] for h in hs],
                         sum=[sums[:, h:h + 1] for h in hs], sums=sumtoks, toks=qtoks, vtoks=vtoks)
                if sink is not None:
                    a["start"] = [sink["neg"][:, h:h + 1] for h in hs]
                    a["keep"] = [sink["nm"][:, h:h + 1] for h in hs]
                    a["kept"] = sink["toks"]
                    a["nmwait"] = sink["ready"]
                if c == 3:
                    a["after"] = after
                out.append(a)
            return out

        def apart(dst, src, *toks):
            return dve.do(lambda e: e.tensor_tensor(
                dst, src.unsqueeze(1).to_broadcast([128, 2, S]), halves.unsqueeze(2).to_broadcast([128, 2, S]),
                ALU.mult), *toks, small)

        def bc(ap, n):
            return ap.unsqueeze(2).to_broadcast([ap.shape[0], ap.shape[1], n])

        def mixer_ab(htoks):
            hold[0] = True
            with ExitStack() as ph:
                KV = sb([128, 2, S], F, ph)
                KZ = sb([128, 3, 2, S], F, ph)
                QA = sb([128, 4, S], F, ph)
                QB = sb([128, 4, S], F, ph)
                VM = sb([128, 2, 408], F, ph)
                KCZ = sb([128, 2, 16], F, ph)
                VBD = sb([128, 512], F, ph)
                BC = sb([128, 2, 8, 16], F, ph)
                SC = sb([128, 8, 16], F, ph)
                PC = sb([128, 8, 16], F, ph)
                PCT = sb([128, 128], F, ph)
                O = Y[:, :, :].rearrange("p c s -> p (c s)").rearrange("p (q d) -> p q d", q=2)
                CA = sb([128, 2, 2, 2, 136], F, ph)
                OT = sb([128, 512], F, ph)
                KVS = OT[:, :].rearrange("p (x s) -> p x s", x=2)
                GT = sb([128, 2, 24], F, ph)
                NS = sb([128, 8], F, ph)
                SM = sb([128, 96], F, ph)
                P = att_pool(ph)
                act.dma(s_sk, lambda e: e.dma_start(SM[:, 0:8], sinks.partition_broadcast(128)))
                kv, ka, qa, qb, va, vb = [], [], [], [], [], []

                def take(n, o, tok):
                    if n < 2:
                        t = act.do(lambda e: e.activation(KV[:, n, :], o, ACT.Copy), tok)
                        kv.append(t)
                    elif n < 4:
                        t = apart(KZ[:, n - 2, :, :], o, tok)
                        ka.append(t)
                    elif n < 8:
                        t = act.do(lambda e: e.activation(QA[:, n - 4, :], o, ACT.Copy, scale=0.125), tok)
                        qa.append(t)
                    elif n == 8:
                        t = apart(KZ[:, 2, :, :], o, tok)
                        qb.append(t)
                    else:
                        t = act.do(lambda e: e.activation(QB[:, n - 9, :], o, ACT.Copy, scale=0.125), tok)
                        qb.append(t)
                    return t

                def take_m(n, qt, o, tok):
                    m = 256 if n == 0 else 152
                    t = act.do(lambda e: e.activation(VM[:, qt, 256 * n:256 * n + m], o, ACT.Copy), tok)
                    (vb if n else va).append(t)
                    return t

                drain(proj_T(AB_T[:AB_PRE], 0, htoks, take, (0, 1, 2, 3)), proj_M(AB_M[:1], 0, take_m, (2, 3)))
                reverse()
                tg, ns, got = [], [], {}

                def gates():
                    for qt in range(2):
                        t = act.do(lambda e, qt=qt: e.activation(GT[:, qt, :], VM[:, qt, 384:408], ACT.Exp,
                                                                 scale=-1.0), vb)
                        t = dve.do(lambda e, qt=qt: e.tensor_scalar(GT[:, qt, :], GT[:, qt, :], 1.0, None, ALU.add), t)
                        tg.append(dve.do(lambda e, qt=qt: e.reciprocal(GT[:, qt, :], GT[:, qt, :]), t))
                    ns.append(dve.do(lambda e: e.tensor_scalar(NS[:, :], SM[:, 0:8], -1.0, None, ALU.mult),
                                     (s_sk, 16)))

                def compress():
                    for r, o in ((0, 64), (64, 0)):
                        pool.dma(s_sw, lambda e, r=r, o=o: e.dma_start(KVS[r:r + 64, :, :], KV[o:o + 64, :, :]), kv)
                    tz = dve.do(lambda e: e.memset(CA[:, :, :, :, 128:136], 0.0))
                    yield
                    for g in range(2):
                        for par in range(2):
                            rows = slice(64 * par, 64 * par + 64)
                            src = (KV if g == par else KVS)[rows, :, par:256:2].rearrange(
                                "p x (m l) -> p x m l", l=8)
                            for v in range(2):
                                cat = dve.do(lambda e, rows=rows, src=src, v=v, g=g: e.tensor_tensor(
                                    CA[rows, :, v, g, 0:128].rearrange("p x (m l) -> p x m l", l=8), src,
                                    VEC[rows, V_PE + 8 * v:V_PE + 8 * v + 8].unsqueeze(1).unsqueeze(1).to_broadcast(
                                        [64, 2, 16, 8]), ALU.add), kv, small, (s_sw, 32))
                    yield
                    for x in range(2):
                        i = next_tile("CMP")
                        m = 64 if x else 128
                        w = raw[i % RAW][:, 0:16 * m].rearrange("p (l m) -> p l m", l=16)
                        pe.wait(raw_ready(i), free[2 + x], cat, tz)
                        for l in range(16):
                            src = CA[:, x, l // 8, :, :].rearrange("p g j -> p (g j)")[:, l:l + 257:8]
                            if x == 0:
                                f = lambda e, w=w, l=l, src=src: e.matmul(
                                    banks[2][:, 0:33], w[:, l, :], src, start=(l == 0), stop=(l == 15),
                                    skip_group_check=True)
                            else:
                                f = lambda e, w=w, l=l, src=src: e.matmul(
                                    banks[3][0:33, 0:64], src, w[:, l, :], start=(l == 0), stop=(l == 15),
                                    skip_group_check=True)
                            tok = pe.do(f) if l == 15 else pe.run(f)
                            if l == 7:
                                yield
                        done_tile(i, tok)
                        if x == 0:
                            t = dve.do(lambda e: e.tensor_tensor(
                                KCZ[:, :, :], banks[2][:, 0:34].rearrange("p (g n) -> p g n", g=2)[:, :, 0:16],
                                halves.unsqueeze(2).to_broadcast([128, 2, 16]), ALU.mult), tok, small)
                            got["k"] = t
                            free[2] = [t]
                        yield
                    t = dve.do(lambda e: e.tensor_copy(PCT[0:33, 0:64], banks[3][0:33, 0:64]), tok)
                    tok = mm(banks[3][:, 0:64], rep33, PCT[0:33, 0:64], toks=[t, small])
                    yield
                    t = dve.do(lambda e: e.tensor_tensor(
                        VBD[:, :].rearrange("p (g r e) -> p g r e", g=2, r=4),
                        banks[3][:, 0:64].unsqueeze(1).unsqueeze(1).to_broadcast([128, 2, 4, 64]),
                        hsel.rearrange("p (g r) -> p g r", g=2).unsqueeze(3).to_broadcast([128, 2, 4, 64]),
                        ALU.mult), tok, small)
                    free[3] = [t]
                    got["v"] = t
                    t = dve.do(lambda e: e.memset(BC[:, :, :, :], NEG))
                    t1 = dve.do(lambda e: e.tensor_copy(BC[:, 0, :, 0:7], BIAS[:, 0:8, 159:256:16]), t, bias_ready)
                    got["b"] = dve.do(lambda e: e.tensor_copy(BC[:, 1, :, 0:15], BIAS[:, 0:8, 31:256:16]), t)
                    yield

                def fill():
                    yield from proj_T(AB_T[AB_PRE:AB_Q], AB_PRE, None, take, (2, 3))
                    yield from proj_M(AB_M[1:], 1, take_m, (3,))
                    gates()
                    yield
                    yield from compress()
                    yield from proj_T(AB_T[AB_Q:], AB_Q, None, take, (2, 3))
                    yield from compressed()

                o_toks = [[None, None], [None, None]]
                last = [None, None]
                hv = lambda a: a.rearrange("p (h e) -> p h e", h=8)
                otf = [None]

                def add_in(qt, ps, w, toks, first=False):
                    acc = hv(O[:, qt, 0:512])
                    if first:
                        t = dve.do(lambda e: e.tensor_tensor(acc, hv(ps), bc(w, 64), ALU.mult), toks)
                        last[qt] = t
                        return t
                    t = dve.do(lambda e: e.tensor_tensor(hv(OT[:, :]), hv(ps), bc(w, 64), ALU.mult), toks, otf[0])
                    t2 = dve.do(lambda e: e.tensor_tensor(acc, acc, hv(OT[:, :]), ALU.add), t, last[qt])
                    otf[0] = t2
                    last[qt] = t2
                    return t

                lst = []
                for w in range(2):
                    both = []
                    for qt in range(2):
                        n = 2 * w + qt
                        sums = SM[:, 32 + 8 * n:40 + 8 * n]
                        stoks = []

                        def after(tok, w=w, sums=sums, stoks=stoks, qt=qt):
                            t = dve.do(lambda e: e.reciprocal(sums, sums), stoks)
                            t = dve.do(lambda e: e.tensor_tensor(sums, sums, GT[:, qt, 1 + w:24:3], ALU.mult), t, tg)
                            free[qt] = [add_in(qt, banks[qt][:, :], sums, [t, tok], first=(w == 0))]

                        both.append(head_pairs(qt, QA, KZ[:, w, :, :], VM[:, :, 128 * w:128 * w + 128],
                                               lambda h: BIAS[:, h, :], qt, sums, stoks, [qa, ka], va, after))
                    lst += by_pairs(*both)

                def compressed():
                    mx, sm, rc = SM[:, 8:16], SM[:, 16:24], SM[:, 24:32]
                    pc = [got["v"]]
                    for qt in range(2):
                        pe.wait(free[2], qa, got["k"])
                        for c in range(4):
                            tok = pe.do(lambda e, c=c, qt=qt: e.matmul(
                                banks[2][:, 32 * c:32 * c + 32].rearrange("p (g n) -> p g n", g=2),
                                QA[:, c, 128 * qt:128 * qt + 128], KCZ[:, :, :],
                                start=True, stop=True, skip_group_check=True))
                        yield
                        t = dve.do(lambda e, qt=qt: e.tensor_tensor(
                            SC[:, :, :].rearrange("p (g r) n -> p g r n", g=2),
                            banks[2][:, 0:128].rearrange("p (r g n) -> p g r n", r=4, g=2),
                            BC[:, qt, :, :].rearrange("p (g r) n -> p g r n", g=2), ALU.add), tok, got["b"], pc)
                        free[2] = [t]
                        t = dve.do(lambda e: e.tensor_reduce(mx, SC[:, :, :], AX.X, ALU.max), t)
                        background()
                        t = dve.do(lambda e: e.tensor_tensor(SC[:, :, :], SC[:, :, :], bc(mx, 16), ALU.subtract), t)
                        te = act.do(lambda e: e.activation(PC[:, :, :], SC[:, :, :], ACT.Exp), t, pc)
                        yield
                        t = dve.do(lambda e: e.tensor_reduce(sm, PC[:, :, :], AX.X, ALU.add), te)
                        t = dve.do(lambda e: e.reciprocal(rc, sm), t)
                        t = dve.do(lambda e, qt=qt: e.tensor_tensor(rc, rc, GT[:, qt, 0:24:3], ALU.mult), t, tg)
                        if qt == 0:
                            t = dve.do(lambda e: e.tensor_scalar(rc, rc, VEC[:, V_ROW:V_ROW + 1], None, ALU.mult), t)
                        trc = t
                        pe.wait(free[2])
                        tok = pe.do(lambda e: e.transpose(
                            banks[2][:, 0:128], PC[:, :, :].rearrange("p h n -> p (h n)"), ident), te)
                        t = dve.do(lambda e: e.tensor_copy(PCT[:, :], banks[2][:, 0:128]), tok, pc)
                        free[2] = [t]
                        yield
                        pe.wait(free[3])
                        tok = mm(banks[3][:, 0:512], PCT[:, :], VBD[:, :], toks=[t, got["v"]])
                        pc = [tok, trc]
                        yield
                        t = add_in(qt, banks[3][:, :], rc, [tok, trc])
                        free[3] = [t]
                        pc.append(t)
                        o_toks[qt][0] = last[qt]
                        yield

                both = []
                for qt in range(2):
                    sums, es, nms = SM[:, 64 + 16 * qt:72 + 16 * qt], SM[:, 72 + 16 * qt:80 + 16 * qt], MB[:, 8 * qt:8 * qt + 8]
                    stoks, keeps = [], []

                    def after_b(tok, sums=sums, es=es, nms=nms, stoks=stoks, keeps=keeps, qt=qt):
                        t = dve.do(lambda e: e.tensor_tensor(es, nms, NS[:, :], ALU.subtract), keeps)
                        t = act.do(lambda e: e.activation(es, es, ACT.Exp), t)
                        t = dve.do(lambda e: e.tensor_tensor(sums, sums, es, ALU.add), t, stoks)
                        t = dve.do(lambda e: e.reciprocal(sums, sums), t)
                        t = dve.do(lambda e: e.tensor_tensor(
                            hv(O[:, qt, 512:1024]), hv(banks[qt][:, :]), bc(sums, 64), ALU.mult), t, tok)
                        free[qt] = [t]
                        o_toks[qt][1] = t

                    both.append(head_pairs(qt, QB, KZ[:, 2, :, :], VM[:, :, 256:384], lambda h: BIAS[:, 8 + h, :], qt,
                                           sums, stoks, qb, vb, after_b,
                                           sink={"neg": NS, "nm": nms, "toks": keeps, "ready": ns}))
                lst += by_pairs(*both)
                f = fill()
                for n, _ in enumerate(softmax_pairs(lst, P)):
                    next(f, None)
                    if n % 2 == 0:
                        hold[0] = False
                        background()
                        hold[0] = True
                hold[0] = False
                drain(f)
                release(P)
                transposed(O, o_toks, None)
                return out_proj()

        def release(P):
            free[4] = free[5] = [t for t in P["fr_s"] if t]
            free[6] = [P["fr_t"]]

        def plain_after(O, qt, half, bank, sums, stoks, o_toks, done=None):
            def after(tok):
                t = dve.do(lambda e: e.reciprocal(sums, sums), stoks)
                t = dve.do(lambda e: e.tensor_tensor(
                    O[:, qt, 512 * half:512 * half + 512].rearrange("p (h e) -> p h e", h=8),
                    banks[bank][:, :].rearrange("p (h e) -> p h e", h=8), bc(sums, 64), ALU.mult), t, tok)
                free[bank] = [t]
                o_toks[qt][half] = t
                if done:
                    done(t)
            return after

        def mixer_cd(htoks):
            with ExitStack() as ph:
                KCZ = sb([128, 2, S], F, ph)
                QC = sb([128, 4, S], F, ph)
                QD = sb([128, 4, S], F, ph)
                KD = sb([128, 4, 2, S], F, ph)
                VC = sb([128, 2, 128], F, ph)
                VD = sb([128, 2, 512], F, ph)
                O = Y[:, :, :].rearrange("p c s -> p (c s)").rearrange("p (q d) -> p q d", q=2)
                SM = sb([128, 16], F, ph)
                P = att_pool(ph)
                kq, dq, vt, vd = [], [], [], []

                def take(n, o, tok):
                    if n == 0:
                        t = apart(KCZ[:, :, :], o, tok)
                        kq.append(t)
                    elif n < 5:
                        t = act.do(lambda e: e.activation(QC[:, n - 1, :], o, ACT.Copy, scale=0.125), tok)
                        kq.append(t)
                    elif n % 2:
                        t = act.do(lambda e: e.activation(QD[:, (n - 5) // 2, :], o, ACT.Copy, scale=0.125), tok)
                        dq.append(t)
                    else:
                        t = apart(KD[:, (n - 5) // 2, :, :], o, tok)
                        dq.append(t)
                    return t

                def take_m(n, qt, o, tok):
                    if n == 0:
                        t = act.do(lambda e: e.activation(VC[:, qt, :], o, ACT.Copy), tok)
                        vt.append(t)
                    else:
                        t = act.do(lambda e: e.activation(VD[:, qt, 256 * (n - 1):256 * n], o, ACT.Copy), tok)
                        vd.append(t)
                    return t

                drain(proj_T(CD_T[:CD_PRE], 0, htoks, take, (0, 1, 2, 3)), proj_M(CD_M[:1], 0, take_m, (2, 3)))
                o_toks = [[None, None], [None, None]]
                both = []
                for qt in range(2):
                    stoks = []
                    sums = SM[:, 8 * qt:8 * qt + 8]
                    both.append(head_pairs(qt, QC, KCZ[:, :, :], VC[:, :, :], lambda h: BIAS[:, h, :], qt, sums,
                                           stoks, kq, vt, plain_after(O, qt, 0, qt, sums, stoks, o_toks)))
                f = proj_T(CD_T[CD_PRE:CD_Q], CD_PRE, None, take, (2, 3))
                weave(softmax_pairs(by_pairs(*both), P), f)
                drain(f)
                release(P)

                Z = [P["s"][0], P["s"][1], P["p"][0]]
                AZ = [P["p"][1], P["p"][2]]
                WT = [P["pT"][0], P["pT"][1]]
                zf, wf, af = [None] * 3, [None] * 2, [None] * 2
                begun = [P["fr_pt"], P["fr_t"]]

                def first(h):
                    j = h % 2
                    z, az = Z[h % 3], AZ[j]
                    q, kk = QD[:, h // 2, :], KD[:, h // 2, j, :]
                    b = 4 + j
                    pe.wait(free[b], dq)
                    pe.run(lambda e: e.matmul(banks[b][:, 0:256], kk[:, 0:128], q, start=True, stop=True,
                                              skip_group_check=True))
                    t = pe.do(lambda e: e.matmul(banks[b][:, 256:384], kk[:, 128:256], q[:, 128:256], start=True,
                                                 stop=True, skip_group_check=True))
                    tz = dve.do(lambda e: e.tensor_tensor(z[:, 0:384], banks[b][:, 0:384], strict, ALU.add), t,
                                zf[h % 3], begun)
                    free[b] = [tz]
                    t = dve.do(lambda e: e.scalar_tensor_tensor(
                        out=az[:, 0:384], in0=z[:, 0:384], scalar=-1.0, in1=z[:, 0:384], op0=ALU.mult, op1=ALU.min),
                        tz, af[j])
                    t = act.do(lambda e: e.activation(az[:, 0:384], az[:, 0:384], ACT.Exp), t)
                    t = act.do(lambda e: e.activation(az[:, 0:384], az[:, 0:384], ACT.Ln, bias=1.0), t)
                    return t

                def second(h, t):
                    j = h % 2
                    z, az = Z[h % 3], AZ[j]
                    tsp = dve.do(lambda e: e.scalar_tensor_tensor(
                        out=az[:, 0:384], in0=z[:, 0:384], scalar=0.0, in1=az[:, 0:384], op0=ALU.max, op1=ALU.add), t)
                    b = (6, 0)[j]
                    pe.wait(free[b], tsp, small)
                    pe.run(lambda e: e.matmul(banks[b][:, 0:256], tri, az[:, 0:256], start=True, stop=False,
                                              skip_group_check=True))
                    pe.run(lambda e: e.matmul(banks[b][:, 128:256], ones, az[:, 256:384], start=False, stop=True,
                                              skip_group_check=True))
                    t = pe.do(lambda e: e.matmul(banks[b][:, 256:384], tri, az[:, 256:384], start=False, stop=True,
                                                 skip_group_check=True))
                    af[j] = t
                    return t

                def third(h, t):
                    j = h % 2
                    z = Z[h % 3]
                    b = (6, 0)[j]
                    t = dve.do(lambda e: e.tensor_tensor(z[:, 0:384], z[:, 0:384], banks[b][:, 0:384], ALU.subtract), t)
                    free[b] = [t]
                    t = act.do(lambda e: e.activation(WT[j][:, 0:384], z[:, 0:384], ACT.Exp), t, wf[j])
                    zf[h % 3] = t
                    return t

                def fourth(h, tw):
                    w = WT[h % 2]
                    v = [VD[:, kt, 64 * h:64 * h + 64] for kt in range(2)]
                    pe.wait(tw, vd, free[1], free[3] if h == 0 else None)
                    pe.run(lambda e: e.matmul(banks[1][:, 64 * h:64 * h + 64], w[:, 0:128], v[0], start=True,
                                              stop=True, skip_group_check=True))
                    pe.run(lambda e: e.matmul(banks[3][:, 64 * h:64 * h + 64], w[:, 128:256], v[0], start=True,
                                              stop=False, skip_group_check=True))
                    t = pe.do(lambda e: e.matmul(banks[3][:, 64 * h:64 * h + 64], w[:, 256:384], v[1],
                                                 start=False, stop=True, skip_group_check=True))
                    wf[h % 2] = t
                    return t

                out_tok = [None]

                def stick():
                    a = {}
                    for i in range(11):
                        if i < 8:
                            a[i] = first(i)
                        if 1 <= i < 9:
                            a[i - 1] = second(i - 1, a[i - 1])
                        if 2 <= i < 10:
                            a[i - 2] = third(i - 2, a[i - 2])
                        if i in (4, 6):
                            background()
                        if i >= 3:
                            out_tok[0] = fourth(i - 3, a[i - 3])
                        yield

                def fill():
                    yield from proj_T(CD_T[CD_Q:CD_Q + 2], CD_Q, None, take, (2,))
                    yield from proj_M(CD_M[1:2], 1, take_m, (2,))
                    yield from proj_T(CD_T[CD_Q + 2:], CD_Q + 2, None, take, (2,))
                    yield from proj_M(CD_M[2:], 2, take_m, (2,))

                f = fill()
                weave(stick(), f, per=2)
                drain(f)
                for qt in range(2):
                    t = dve.do(lambda e, qt=qt: e.tensor_copy(O[:, qt, 512:1024], banks[1 + 2 * qt][:, :]), out_tok[0])
                    free[1 + 2 * qt] = [t]
                    o_toks[qt][1] = t
                transposed(O, o_toks, None)
                return out_proj()

        def hybrid(layer, htoks):
            with ExitStack() as ph:
                GL = sb([16, S], F, ph)
                GW = sb([16, 256], F, ph)
                GQ = sb([128, 2, S], F, ph)
                GK = sb([128, 2, S], F, ph)
                Q = sb([128, 4, S], F, ph)
                KZ = sb([128, 4, 2, S], F, ph)
                QP = [SIDER[1][:, 256 * k:256 * k + 256] for k in range(2)]
                R1 = [SIDER[1][:, 512 + 256 * k:768 + 256 * k] for k in range(2)]
                V = sb([128, 2, 512], F, ph)
                GV = sb([128, 2, 512], F, ph)
                GR = SIDER[0][:, 1024:2048].rearrange("p (q d) -> p q d", q=2)
                O = Y[:, :, :].rearrange("p c s -> p (c s)").rearrange("p (q d) -> p q d", q=2)
                SM = sb([128, 40], F, ph)
                P = att_pool(ph)
                s_g = s_gu
                act.dma(s_g, lambda e: e.dma_start(GW[:, :], gup[layer]))
                gw_ready = (s_g, 16 * (layer + 1))
                kq, gq, gl = [], [], []
                qpf = [None] * 2
                r1f = [None] * 2

                def take(n, o, tok):
                    if n == 4:
                        t = act.do(lambda e: e.activation(GL[:, :], o, ACT.Copy), tok)
                        gl.append(t)
                        return t
                    if n < 2:
                        t = act.do(lambda e: e.activation(GQ[:, n, :], o, ACT.Copy, scale=0.125), tok)
                        gq.append(t)
                        return t
                    if n < 4:
                        t = act.do(lambda e: e.activation(GK[:, n - 2, :], o, ACT.Copy), tok)
                        gq.append(t)
                        return t
                    j, c = n % 2, (n - 5) // 2
                    query = n % 2 == 1
                    t = act.do(lambda e: e.activation(QP[j], o, ACT.Copy, scale=0.125 if query else 1.0), tok, qpf[j])

                    def turned(toks):
                        return mm(o, rot, QP[j], toks=[*toks, small])

                    def rotated(t2):
                        t3 = dve.do(lambda e: e.tensor_tensor(R1[j], o, sinT, ALU.mult), t2, r1f[j])
                        if query:
                            dst = Q[:, c, :]
                            t4 = dve.do(lambda e: e.tensor_tensor(dst, QP[j], cosT, ALU.mult), t)
                            t5 = dve.do(lambda e: e.tensor_tensor(dst, dst, R1[j], ALU.add), t3, t4)
                            r1f[j] = t5
                        else:
                            t4 = dve.do(lambda e: e.tensor_tensor(QP[j], QP[j], cosT, ALU.mult), t, t2)
                            r1f[j] = dve.do(lambda e: e.tensor_tensor(QP[j], QP[j], R1[j], ALU.add), t3, t4)
                            t4 = t5 = apart(KZ[:, c, :, :], QP[j], r1f[j])
                        qpf[j] = [t4, t2]
                        kq.append(t5)
                        return t3

                    later.append((turned, rotated))
                    return t

                vt, gv, gr = [], [], []

                def take_m(n, qt, o, tok):
                    buf, lst, i = ((GV, gv, 0), (GV, gv, 1), (V, vt, 0), (GR, gr, 0), (GR, gr, 1), (V, vt, 1))[n]
                    dst = buf[:, qt, 256 * i:256 * i + 256]
                    t = act.do(lambda e: e.activation(dst, o, ACT.Silu if buf is GR else ACT.Copy), tok)
                    lst.append(t)
                    return t

                drain(proj_T(HY_T[:HY_PRE], 0, htoks, take, (0, 1, 2, 3)))
                o_toks = [[None, None], [None, None]]
                nw = V_ONORM + 8 * layer
                SG, SQ512 = SIDER[0][:, 0:512], SIDER[0][:, 512:1024]
                AT = [SIDER[1][:, 1024 + 384 * k:1408 + 384 * k] for k in range(2)]
                sq512_free = [None]

                ONE, B, T1, T2, E1, E2 = (BIAS[:, k, :] for k in range(6))
                X1, X2, QD_, KD_ = ([BIAS[:, 6 + 2 * k + n, :] for n in range(2)] for k in range(4))
                ready = []

                def decays():
                    chain = dve.do(lambda e: e.memset(ONE, 1.0))
                    for p in range(2):
                        z = mm(banks[1][:, 0:256], GW[:, 128 * p:128 * p + 128], GL[:, :],
                               toks=[gl, gw_ready, free[1]])
                        gb = VEC[:, V_GB + 2 * layer + p:V_GB + 2 * layer + p + 1]
                        t = dve.do(lambda e, gb=gb: e.tensor_scalar(B[:, :], banks[1][:, 0:256], gb, None, ALU.add),
                                   z, chain)
                        free[1] = [t]
                        yield
                        t = dve.do(lambda e: e.scalar_tensor_tensor(
                            out=T1[:, :], in0=B[:, :], scalar=-1.0, in1=B[:, :], op0=ALU.mult, op1=ALU.min), t)
                        t = act.do(lambda e: e.activation(T1[:, :], T1[:, :], ACT.Exp), t)
                        t = act.do(lambda e: e.activation(T1[:, :], T1[:, :], ACT.Ln, bias=1.0), t)
                        yield
                        t = dve.do(lambda e: e.scalar_tensor_tensor(
                            out=T1[:, :], in0=B[:, :], scalar=0.0, in1=T1[:, :], op0=ALU.min, op1=ALU.subtract), t)
                        tb = dve.do(lambda e: e.tensor_tensor_scan(
                            B[:, :], ONE[:, :], T1[:, :], 0.0, ALU.mult, ALU.add), t)
                        yield
                        t = dve.do(lambda e: e.tensor_scalar(
                            T1[:, :], B[:, :], B[:, 127:128], None, ALU.subtract), tb)
                        t = dve.do(lambda e: e.scalar_tensor_tensor(
                            out=T1[:, :], in0=T1[:, :], scalar=-1.0, in1=T1[:, :], op0=ALU.mult, op1=ALU.min), t)
                        t = act.do(lambda e: e.activation(E1[:, :], T1[:, :], ACT.Exp, scale=1.0 / 16), t)
                        t1 = dve.do(lambda e, p=p: e.tensor_tensor(
                            X1[p][:, 0:128], E1[:, 0:128], GK[:, p, 0:128], ALU.mult), t, gq)
                        t2 = dve.do(lambda e, p=p: e.tensor_tensor(
                            X1[p][:, 128:256], E1[:, 128:256], GQ[:, p, 128:256], ALU.mult), t)
                        yield
                        v4 = lambda a: a.rearrange("p (c t) -> p c t", c=2)
                        t = dve.do(lambda e: e.tensor_tensor(
                            v4(T2[:, :]), v4(B[:, :]), B[:, 63:192:128].unsqueeze(2).to_broadcast([128, 2, 128]),
                            ALU.subtract), tb)
                        t = dve.do(lambda e: e.scalar_tensor_tensor(
                            out=T2[:, :], in0=T2[:, :], scalar=-1.0, in1=T2[:, :], op0=ALU.mult, op1=ALU.min), t)
                        t = act.do(lambda e: e.activation(E2[:, :], T2[:, :], ACT.Exp, scale=1.0 / 16), t)
                        t3 = dve.do(lambda e, p=p: e.tensor_tensor(
                            v4(X2[p][:, :])[:, :, 0:64], v4(E2[:, :])[:, :, 0:64], v4(GK[:, p, :])[:, :, 0:64],
                            ALU.mult), t)
                        t4 = dve.do(lambda e, p=p: e.tensor_tensor(
                            v4(X2[p][:, :])[:, :, 64:128], v4(E2[:, :])[:, :, 64:128], v4(GQ[:, p, :])[:, :, 64:128],
                            ALU.mult), t)
                        yield
                        t = dve.do(lambda e: e.tensor_tensor(
                            T1[:, :].rearrange("p (c t) -> p c t", c=4), B[:, :].rearrange("p (c t) -> p c t", c=4),
                            B[:, 31:256:64].unsqueeze(2).to_broadcast([128, 4, 64]), ALU.subtract), t1, t2)
                        t = dve.do(lambda e: e.tensor_scalar(T1[:, :], T1[:, :], 1280.0, -1280.0, ALU.min, ALU.max), t)
                        ta = act.do(lambda e: e.activation(E1[:, :], T1[:, :], ACT.Exp, scale=1.0 / 16), t)
                        tc = act.do(lambda e: e.activation(E2[:, :], T1[:, :], ACT.Exp, scale=-1.0 / 16), t3, t4)
                        t5 = dve.do(lambda e, p=p: e.tensor_tensor(QD_[p][:, :], E1[:, :], GQ[:, p, :], ALU.mult), ta)
                        t6 = dve.do(lambda e, p=p: e.tensor_tensor(KD_[p][:, :], E2[:, :], GK[:, p, :], ALU.mult), tc)
                        chain = [t5, t6]
                        ready.append([t1, t2, t3, t4, t5, t6])
                        yield

                def weights(h):
                    p, r, j = h // 2, 64 * (h % 2), h % 2
                    x1, x2, qd, kd = (a[p][r:r + 64, :] for a in (X1, X2, QD_, KD_))
                    bank = banks[1]
                    pe.wait(free[1], ready[p])

                    def m(o, l, rr):
                        return pe.do(lambda e: e.matmul(o, l, rr, start=True, stop=True, skip_group_check=True))
                    m(bank[:, 128:256], x1[:, 0:128], x1[:, 128:256])
                    for hh in range(2):
                        c0 = 0 if hh == 0 else 256
                        t0 = 128 * hh
                        m(bank[0:64, c0:c0 + 64], kd[:, t0:t0 + 64], qd[:, t0:t0 + 64])
                        m(bank[0:64, c0 + 64:c0 + 128], x2[:, t0:t0 + 64], x2[:, t0 + 64:t0 + 128])
                        tok = m(bank[64:128, c0:c0 + 128], kd[:, t0 + 64:t0 + 128], qd[:, t0:t0 + 128])
                    A = AT[j]
                    ta = act.do(lambda e: e.activation(A[:, 128:256], bank[:, 128:256], ACT.Copy), tok, atf[j])
                    tc = [dve.do(lambda e, c0=c0: e.copy_predicated(
                        A[:, c0:c0 + 128], hmask, bank[:, c0:c0 + 128]), tok, ta, atf[j], mask_ready)
                        for c0 in (0, 256)]
                    free[1] = [ta] + tc
                    return [ta] + tc

                def values(h, t):
                    A = AT[h % 2]
                    v = [GV[:, kt, 128 * h:128 * h + 128] for kt in range(2)]
                    oc = slice(128 * h, 128 * h + 128)
                    pe.wait(t, gv)
                    if h == 0:
                        pe.wait(free[0], free[7])
                    mm(banks[0][:, oc], A[:, 0:128], v[0], sig=False)
                    mm(banks[7][:, oc], A[:, 128:256], v[0], stop=False, sig=False)
                    atf[h % 2] = mm(banks[7][:, oc], A[:, 256:384], v[1], start=False)
                    return atf[h % 2]

                atf, lin = [], []

                def linear():
                    for j in range(2):
                        atf.append(dve.do(lambda e, j=j: e.memset(AT[j], 0.0)))
                    t = weights(0)
                    yield
                    for h in range(4):
                        nxt = weights(h + 1) if h < 3 else None
                        yield
                        tok = values(h, t)
                        t = nxt
                    for qt, b in enumerate((0, 7)):
                        g = O[:, qt, 512:1024]
                        free[b] = [dve.do(lambda e, b=b, g=g: e.tensor_copy(g, banks[b][:, :]), tok)]
                        lin.append(free[b])

                def finish():
                    gfree = None
                    for qt in range(2):
                        ss = SM[:, 20 + 4 * qt:24 + 4 * qt]
                        g = O[:, qt, 512:1024]
                        t = lin[qt]
                        t1 = act.do(lambda e, g=g: e.activation(SQ512, g, ACT.Square), t, sq512_free[0], gfree)
                        yield
                        t2 = dve.do(lambda e, ss=ss: e.tensor_reduce(
                            ss, SQ512.rearrange("p (h e) -> p h e", h=4), AX.X, ALU.add), t1)
                        sq512_free[0] = t2
                        t3 = act.do(lambda e, ss=ss: e.activation(ss, ss, ACT.Ln, scale=1.0 / 128, bias=eps), t2)
                        t3 = act.do(lambda e, ss=ss: e.activation(ss, ss, ACT.Exp, scale=-0.5), t3)
                        t5 = dve.do(lambda e, qt=qt, g=g: e.tensor_tensor(SG, GR[:, qt, :], g, ALU.mult), gr, t)
                        yield
                        t6 = dve.do(lambda e, g=g, ss=ss: e.tensor_tensor(
                            g.rearrange("p (h e) -> p h e", h=4), SG.rearrange("p (h e) -> p h e", h=4),
                            bc(ss, 128), ALU.mult), t5, t3)
                        gfree = t6
                        o_toks[qt][1] = t6
                        yield

                def fill1():
                    yield from proj_M(HY_M[:2], 0, take_m, (2, 3))
                    yield from proj_T(HY_T[HY_PRE:HY_PRE + 2], HY_PRE, None, take, (2, 3))
                    yield from proj_M(HY_M[2:5], 2, take_m, (2, 3))

                def fill2():
                    yield from proj_T(HY_T[HY_PRE + 2:], HY_PRE + 2, None, take, (2, 3))
                    yield from proj_M(HY_M[5:], 5, take_m, (2, 3))

                f = fill1()
                weave(decays(), f)
                weave(linear(), f)
                drain(f)
                both = []
                for qt in range(2):
                    stoks = []
                    sums = SM[:, 8 * qt:8 * qt + 8]

                    def norm(t, qt=qt):
                        ss = SM[:, 16 + qt:17 + qt]
                        t1 = act.do(lambda e: e.activation(SQ512, O[:, qt, 0:512], ACT.Square, accum_out=ss), t,
                                    sq512_free[0])
                        t2 = act.do(lambda e: e.activation(ss, ss, ACT.Ln, scale=1.0 / 512, bias=eps), t1)
                        t3 = act.do(lambda e: e.activation(ss, ss, ACT.Exp, scale=-0.5), t2)
                        sq512_free[0] = t1
                        o_toks[qt][0] = dve.do(lambda e: e.tensor_scalar(
                            O[:, qt, 0:512], O[:, qt, 0:512], ss, None, ALU.mult), t3)

                    ob = 7 if qt else 0
                    both.append(head_pairs(qt, Q, KZ, V, lambda h: dil, ob, sums, stoks, kq, vt,
                                           plain_after(O, qt, 0, ob, sums, stoks, o_toks, norm), grouped=False))
                f, g = fill2(), finish()
                weave_before(softmax_pairs(by_pairs(*both), P), f, g)
                drain(f, g)
                release(P)
                transposed(O, o_toks, lambda c: VEC[:, nw + c:nw + c + 1])
                return out_proj()

        t = pool.do(lambda e: e.memset(HM[:, :], 1.0))
        mask_ready = pool.do(lambda e: e.affine_select(
            out=HM[:, :], in_=HM[:, :], compare_op=ALU.is_ge, fill=0.0, base=0, pattern=[[1, 128]],
            channel_multiplier=-1), t)
        hmask = HM[:, :].bitcast(U32)

        xt = [x_in] * KC
        for j in range(8):
            i = next_tile("T")
            done_tile(i, (mod_tile_pe if j in (1, 4) else mod_tile)(raw[i % RAW], raw_ready(i), j))
            if j == 4:
                stat0 = x_stats(xt)
                tp = looked_up()
        expand(tp)
        splits(8)
        for layer in range(2):
            for sub in range(2):
                st = 2 * layer + sub
                mt = modulation(st)
                h = make_h(x_stats(xt) if st else stat0, lambda c: A4[:, c:c + 1], lambda c: MOD[:, c:c + 1], mt)
                if sub == 0:
                    y, stat = (mixer_ab if layer == 0 else mixer_cd)(h)
                else:
                    y, stat = ffn(h)
                xt = residual(stat, lambda c: G4[:, c:c + 1], gating(st), y)
                mod_tok[0] = xt[-1]
        for layer in range(2):
            for sub in range(2):
                o = V_NORM2 + 32 * layer + 16 * sub
                h = make_h(x_stats(xt), lambda c, o=o: VEC[:, o + c:o + c + 1], None, small)
                y, st = hybrid(layer, h) if sub == 0 else ffn(h)
                xt = residual(st, lambda c, o=o: VEC[:, o + 8 + c:o + 9 + c], small, y)
        sp.dma(s_out, lambda e: e.dma_start(out, X[:, :, :]), xt[-1])
        sp.wait((s_out, 16))
        assert state["use"] == len(TILES) and side["use"] == len(SIDE)

        block = ctx.enter_context(nc.Block())
        block.sync(sp.emit)
        block.gpsimd(pool.emit)
        block.scalar(act.emit)
        block.vector(dve.emit)
        block.tensor(pe.emit)


def shape_constants():
    c = np.zeros((128, NCONST), np.float32)
    i = np.arange(128)
    c[:, C_ID:C_ID + 128] = i[:, None] == i[None, :]
    c[:, C_TRI:C_TRI + 128] = i[:, None] >= i[None, :]
    c[:, C_ONE:C_ONE + 128] = 1.0
    d = i % 64
    for p in range(128):
        if d[p] < 8:
            c[p + 8, C_ROT + p] = 1.0
        elif d[p] < 16:
            c[p - 8, C_ROT + p] = 1.0
    q = np.arange(256)
    st = np.concatenate([np.where(i[:, None] < q[None, :], 0.0, NEG),
                         np.where(128 + i[:, None] < q[None, 128:], 0.0, NEG)], axis=1)
    c[:, C_STRICT:C_STRICT + 384] = st
    dist = 128 + i[:, None] - q[None, :]
    m = ((dist >= 0) & (dist <= 128)).astype(np.int64) + ((dist >= 0) & (dist % 4 == 0)) + \
        ((dist >= 0) & (dist % 16 == 0))
    c[:, C_DIL:C_DIL + 256] = np.where(m > 0, np.log(np.maximum(m, 1)), NEG)
    inv = (np.float32(500000.0) ** (-(np.arange(8, dtype=np.float32) * np.float32(2.0)) / np.float32(16))).astype(
        np.float32)
    ang = (q.astype(np.float32)[None, :] * inv[:, None]).astype(np.float32).astype(np.float64)
    for p in range(128):
        if d[p] < 16:
            c[p, C_COS:C_COS + 256] = np.cos(ang[d[p] % 8])
            c[p, C_SIN:C_SIN + 256] = np.sin(ang[d[p] % 8]) * (-1.0 if d[p] < 8 else 1.0)
        else:
            c[p, C_COS:C_COS + 256] = 1.0
    c[:, C_HSEL:C_HSEL + 8] = (i[:, None] // 16) == np.arange(8)[None, :]
    c[:, C_HALF:C_HALF + 2] = (i[:, None] // 64) == np.arange(2)[None, :]
    c[:, C_REV:C_REV + 128] = (i[:, None] + i[None, :]) == 127
    c[0:33, C_REP:C_REP + 128] = i[:33, None] == (17 * (i[None, :] // 64) + i[None, :] % 16)
    u = np.zeros((33, 1024), np.float32)
    for j in range(2):
        for t in range(512):
            dd = 255 - t
            lim = 256 if j == 0 else 128
            if dd < 0 or dd >= lim:
                u[32, 512 * j + t] = 1.0
            else:
                b = dd if dd < 16 else min(31, 16 + int(math.log(dd / 16) / math.log(8) * 16 + 1e-9))
                u[b, 512 * j + t] = 1.0
    return c, u


def pack_weights(a):
    tiles, side = plan()
    tiles = tiles + side
    wall = np.zeros((len(tiles), 128, TW), np.float32)

    def src(name):
        n = name[0]
        if n == "mod":
            return a["mod_w"][name[1], name[2]]
        if n in ("ab", "ab_out", "cd", "cd_out"):
            return a[{"ab": "w_in_ab", "ab_out": "w_out_ab", "cd": "w_in_cd", "cd_out": "w_out_cd"}[n]][0]
        if n in ("wk", "wv"):
            return a["nsa_cmp_" + n][0]
        return a[{"hy": "w_in_2", "hy_out": "w_out_2", "gate": "w_gate_2", "up": "w_up_2", "down": "w_down_2",
                  "ffn_in": "ffn_w_in", "ffn_out": "ffn_w_out"}[n]][name[1]]

    for i, (name, what, arg, _) in enumerate(tiles):
        if what == "T":
            w = src(name).reshape(KC, 128, -1)
            off = 0
            for c in arg:
                m = len(c)
                wall[i, :, off:off + KC * m] = w[:, :, c].transpose(1, 0, 2).reshape(128, KC * m)
                off += KC * m
        elif what == "M":
            w = src(name).reshape(KC, 128, -1)
            wall[i, :, :KC * len(arg)] = w[:, :, arg].transpose(1, 0, 2).reshape(128, -1)
        elif what == "GU":
            j, off = arg
            for c in range(2):
                w = src(name[c]).reshape(KC, 128, -1)
                o = 128 * j + (off if c else 0)
                wall[i, :, 1024 * c:1024 * c + 1024] = w[:, :, o:o + 128].transpose(1, 0, 2).reshape(128, 1024)
        elif what == "DN":
            m, half = arg
            w = src(name).reshape(FC, 128, D)[11 * half:11 * half + 11, :, 128 * m:128 * m + 128]
            wall[i, :, :11 * 128] = w.transpose(1, 0, 2).reshape(128, -1)
        else:
            w = src(name).reshape(16, 128, 64).transpose(1, 0, 2)
            if arg == "wk":
                w = np.concatenate([w, w], axis=2)
            wall[i, :, :w.shape[1] * w.shape[2]] = w.reshape(128, -1)
    return wall


def pack_vectors(a):
    v = np.zeros((128, NV), np.float32)
    col = lambda x: x.reshape(-1, 128).T
    v[:, V_C:V_C + 8] = col(a["c"])
    for l in range(2):
        for s in range(2):
            o = V_MODB + 24 * (2 * l + s)
            v[:, o:o + 24] = col(a["mod_b"][l, s])
            o = V_NORM + 16 * (2 * l + s)
            v[:, o:o + 16] = col(a["norm_w"][l, s])
            o = V_NORM2 + 32 * l + 16 * s
            pre, post = (("mix_pre_norm_2", "mix_post_norm_2"), ("ffn_pre_norm_2", "ffn_post_norm_2"))[s]
            v[:, o:o + 8] = col(a[pre][l])
            v[:, o + 8:o + 16] = col(a[post][l])
        o = V_ONORM + 8 * l
        v[:, o:o + 4] = col(a["attn_out_norm_2"][l])
        v[:, o + 4:o + 8] = col(a["gla_out_norm_2"][l])
        v[:, V_GB + 2 * l:V_GB + 2 * l + 2] = col(a["gla_b_gate_2"][l])
    v[:, V_PE:V_PE + 16] = a["nsa_cmp_pe"][0].reshape(16, 128).T
    v[:, V_EPS] = 1e-6
    v[31:, V_ROW] = 1.0
    return v


def kernel(**inputs):
    import numpy as _np
    import concourse.bacc as _bacc
    from concourse import mybir as _mybir
    from concourse.bass_utils import run_bass_kernel_spmd as _run

    a = {k: _np.asarray(v) for k, v in inputs.items()}
    con, onehot = shape_constants()
    arrays = {
        "wall": pack_weights(a),
        "xin": _np.ascontiguousarray(a["x"][0].T.reshape(KC, 128, S).transpose(1, 0, 2)),
        "vecs": pack_vectors(a),
        "consts": con,
        "onehot": onehot,
        "sinks": _np.ascontiguousarray(a["swa_sinks"][0]),
        "table": _np.ascontiguousarray(a["rel_table"]),
        "gup": _np.ascontiguousarray(a["gla_w_gate_up_2"]),
    }
    nc = _bacc.Bacc("TRN2", target_bir_lowering=False, num_devices=1)
    f = _mybir.dt.float32
    args = [nc.dram_tensor(n, v.shape, f, kind="ExternalInput").ap() for n, v in arrays.items()]
    out = nc.dram_tensor("out_0", (128, KC, S), f, kind="ExternalOutput").ap()
    scratch = nc.dram_tensor("scratch", (16, 512), f).ap()
    build(nc, *args, out, scratch)
    r = _run(nc, [arrays], core_ids=[0])
    got = r.results[0]["out_0"]
    return _np.ascontiguousarray(got.transpose(1, 0, 2).reshape(D, S).T)[None]
```
